# Optimizing a Trainium2 kernel written in Bass

```python
import jax, jax.numpy as jnp
from jax import lax
import numpy as np

D_MODEL = 1024
BATCH = 1
SEQ = 256
DEPTH = 2

EPS = 1e-5
HEAD_DIM = 64
SSD_HEADS = 8
SSD_WIDTH = SSD_HEADS * HEAD_DIM
SSD_GROUPS = 2
SSD_STATE = 128
SSD_CHUNK = 128
CONV_K = 4
XBC_WIDTH = SSD_WIDTH + 2 * SSD_GROUPS * SSD_STATE
MOBA_HEADS = 4
MOBA_WIDTH = MOBA_HEADS * HEAD_DIM
MOBA_BLOCK = 256
MOBA_TOPK = 3
MOBA_QBLOCK = 64
SWA_HEADS = 4
SWA_KV_HEADS = 2
SWA_WIDTH = SWA_HEADS * HEAD_DIM
SWA_KV_WIDTH = SWA_KV_HEADS * HEAD_DIM
SWA_WINDOW = 128
SWA_BLOCK = 128
MIX_WIDTH = SSD_WIDTH + MOBA_WIDTH + SWA_WIDTH
N_IN = SSD_WIDTH + XBC_WIDTH + SSD_HEADS + 3 * MOBA_WIDTH + SWA_WIDTH + 2 * SWA_KV_WIDTH
PEER_HEADS = 8
PEER_TOPK = 16
PEER_NKEYS = 128
PEER_EXPERTS = PEER_NKEYS * PEER_NKEYS
PEER_DKEY = 256
PEER_HALF = PEER_DKEY // 2
PEER_CHUNK = 128


def rms_norm(x, g):
    x32 = x.astype(jnp.float32)
    y = x32 * lax.rsqrt(jnp.mean(x32 * x32, axis=-1, keepdims=True) + EPS)
    return y.astype(x.dtype) * g.astype(x.dtype)

def causal_depthwise_conv(x, w, b):
    y = lax.conv_general_dilated(
        x, w.astype(x.dtype)[:, None, :], window_strides=(1,), padding=[(CONV_K - 1, 0)],
        dimension_numbers=("NWC", "WIO", "NWC"), feature_group_count=x.shape[-1])
    return y + b.astype(x.dtype)

def segsum(a):
    t = a.shape[-1]
    xr = jnp.broadcast_to(a[..., None], a.shape + (t,))
    xr = jnp.where(jnp.tril(jnp.ones((t, t), bool), -1), xr, 0.0)
    cs = jnp.cumsum(xr, axis=-2)
    return jnp.where(jnp.tril(jnp.ones((t, t), bool)), cs, -jnp.inf)

def ssd_mixer(z, xbc, dt_raw, conv_w, conv_b, dt_bias, a_log, d_skip, norm_g):
    f32 = jnp.float32
    b, s, _ = z.shape
    G, R, L, P, N = SSD_GROUPS, SSD_HEADS // SSD_GROUPS, SSD_CHUNK, HEAD_DIM, SSD_STATE
    nc = s // L
    xbc = jax.nn.silu(causal_depthwise_conv(xbc, conv_w, conv_b))
    xs, bm, cm = jnp.split(xbc, [SSD_WIDTH, SSD_WIDTH + G * N], axis=-1)
    dt = jax.nn.softplus(dt_raw.astype(f32) + dt_bias.astype(f32))
    a_head = -jnp.exp(a_log.astype(f32))
    xh = xs.reshape(b, nc, L, G, R, P)
    xdt = xh.astype(f32) * dt.reshape(b, nc, L, G, R)[..., None]
    bc = bm.reshape(b, nc, L, G, N)
    cc = cm.reshape(b, nc, L, G, N)
    a = (dt * a_head).reshape(b, nc, L, G, R).transpose(0, 3, 4, 1, 2)
    a_cs = jnp.cumsum(a, axis=-1)
    decay = jnp.exp(segsum(a))
    cb = jnp.einsum("bclgn,bcsgn->bgcls", cc, bc)
    y_diag = jnp.einsum("bgcls,bgrcls,bcsgrp->bclgrp", cb, decay, xdt)
    decay_states = jnp.exp(a_cs[..., -1:] - a_cs)
    states = jnp.einsum("bclgn,bgrcl,bclgrp->bcgrpn", bc, decay_states, xdt)
    states = jnp.concatenate([jnp.zeros_like(states[:, :1]), states], axis=1)
    last = jnp.pad(a_cs[..., -1], ((0, 0), (0, 0), (0, 0), (1, 0)))
    chunk_decay = jnp.exp(segsum(last))
    states = jnp.einsum("bgrzc,bcgrpn->bzgrpn", chunk_decay, states)[:, :-1]
    y_off = jnp.einsum("bclgn,bcgrpn,bgrcl->bclgrp", cc, states, jnp.exp(a_cs))
    y = (y_diag + y_off).reshape(b, s, SSD_HEADS, P) \
        + d_skip.astype(f32)[:, None] * xs.reshape(b, s, SSD_HEADS, P).astype(f32)
    y = y.reshape(b, s, SSD_WIDTH).astype(z.dtype)
    return rms_norm(y * jax.nn.silu(z), norm_g)

def moba_attention(q, k, v, norm_g):
    f32 = jnp.float32
    b, s, _ = q.shape
    H, Dh, BL, QB = MOBA_HEADS, HEAD_DIM, MOBA_BLOCK, MOBA_QBLOCK
    nb = -(-s // BL)
    pad = nb * BL - s
    q, k, v = (t.reshape(b, s, H, Dh).transpose(0, 2, 1, 3) for t in (q, k, v))
    k = jnp.pad(k, ((0, 0), (0, 0), (0, pad), (0, 0)))
    v = jnp.pad(v, ((0, 0), (0, 0), (0, pad), (0, 0)))
    kb = k.reshape(b, H, nb, BL, Dh)
    vb = v.reshape(b, H, nb, BL, Dh)
    k_mean = jnp.mean(kb.astype(f32), axis=3)
    gate = jnp.einsum("bhsd,bhnd->bhsn", q.astype(f32), k_mean)
    past = jnp.arange(nb)[None, :] < (jnp.arange(s) // BL)[:, None]
    gate = jnp.where(past, gate, -jnp.inf)
    topk = min(MOBA_TOPK, nb)
    _, sel = lax.top_k(gate, topk)
    nq = s // QB
    q_chunks = q.reshape(b, H, nq, QB, Dh).transpose(2, 0, 1, 3, 4)
    sel_chunks = sel.reshape(b, H, nq, QB, topk).transpose(2, 0, 1, 3, 4)
    bi = jnp.arange(b)[:, None, None, None]
    hi = jnp.arange(H)[None, :, None, None]
    scale = Dh ** -0.5

    def one_chunk(args):
        qc, selc, ci = args
        q0 = ci * QB
        blk = q0 // BL
        q_pos = q0 + jnp.arange(QB)
        k_sel = kb[bi, hi, selc]
        v_sel = vb[bi, hi, selc]
        s_sel = jnp.einsum("bhqd,bhqjkd->bhqjk", qc, k_sel).astype(f32) * scale
        valid = jnp.arange(topk) < blk
        s_sel = jnp.where(valid[:, None], s_sel, -jnp.inf).reshape(b, H, QB, topk * BL)
        start = blk * BL
        k_own = lax.dynamic_slice_in_dim(k, start, BL, axis=2)
        v_own = lax.dynamic_slice_in_dim(v, start, BL, axis=2)
        s_own = jnp.einsum("bhqd,bhkd->bhqk", qc, k_own).astype(f32) * scale
        k_pos = start + jnp.arange(BL)
        s_own = jnp.where(k_pos[None, :] <= q_pos[:, None], s_own, -jnp.inf)
        p = jax.nn.softmax(jnp.concatenate([s_sel, s_own], axis=-1), axis=-1).astype(v.dtype)
        p_sel = p[..., :topk * BL].reshape(b, H, QB, topk, BL)
        p_own = p[..., topk * BL:]
        return jnp.einsum("bhqjk,bhqjkd->bhqd", p_sel, v_sel) + jnp.einsum("bhqk,bhkd->bhqd", p_own, v_own)

    out = lax.map(one_chunk, (q_chunks, sel_chunks, jnp.arange(nq)))
    out = out.transpose(1, 0, 3, 2, 4).reshape(b, s, H * Dh)
    return rms_norm(out, norm_g)

def swa_attention(q, k, v, sinks, norm_g):
    f32 = jnp.float32
    b, s, _ = q.shape
    W, G, R, Dh = SWA_BLOCK, SWA_KV_HEADS, SWA_HEADS // SWA_KV_HEADS, HEAD_DIM
    nb = s // W
    qb = q.reshape(b, nb, W, G, R, Dh)
    kb = k.reshape(b, nb, W, G, Dh)
    vb = v.reshape(b, nb, W, G, Dh)
    shift = lambda t: jnp.concatenate([jnp.zeros_like(t[:, :1]), t[:, :-1]], axis=1)
    k_band = jnp.concatenate([shift(kb), kb], axis=2)
    v_band = jnp.concatenate([shift(vb), vb], axis=2)
    scores = jnp.einsum("bnqgrd,bnkgd->bngrqk", qb, k_band).astype(f32) * (Dh ** -0.5)
    i = jnp.arange(W)[:, None]
    j = jnp.arange(2 * W)[None, :]
    rel = i + W - j
    in_win = (rel >= 0) & (rel < SWA_WINDOW)
    has_prev = (jnp.arange(nb) > 0)[:, None, None] | (j >= W)[None]
    mask = in_win[None] & has_prev
    scores = jnp.where(mask[None, :, None, None], scores, -jnp.inf)
    sink = jnp.broadcast_to(sinks.astype(f32).reshape(G, R)[None, None, :, :, None, None],
                            scores.shape[:-1] + (1,))
    p = jax.nn.softmax(jnp.concatenate([scores, sink], axis=-1), axis=-1)[..., :-1].astype(v.dtype)
    out = jnp.einsum("bngrqk,bnkgd->bnqgrd", p, v_band).reshape(b, s, SWA_WIDTH)
    return rms_norm(out, norm_g)

def peer_ffn(h, wq, k1, k2, u, v):
    f32 = jnp.float32
    b, s, d = h.shape
    nch = (b * s) // PEER_CHUNK
    hc = h.reshape(nch, PEER_CHUNK, d)

    def one_chunk(xc):
        q = (xc @ wq).reshape(PEER_CHUNK, PEER_HEADS, 2, PEER_HALF).astype(f32)
        s1 = jnp.einsum("thd,nd->thn", q[:, :, 0], k1.astype(f32))
        s2 = jnp.einsum("thd,nd->thn", q[:, :, 1], k2.astype(f32))
        v1, i1 = lax.top_k(s1, PEER_TOPK)
        v2, i2 = lax.top_k(s2, PEER_TOPK)
        cand = (v1[..., :, None] + v2[..., None, :]).reshape(PEER_CHUNK, PEER_HEADS, PEER_TOPK * PEER_TOPK)
        sc, ci = lax.top_k(cand, PEER_TOPK)
        e = jnp.take_along_axis(i1, ci // PEER_TOPK, axis=-1) * PEER_NKEYS \
            + jnp.take_along_axis(i2, ci % PEER_TOPK, axis=-1)
        g = jax.nn.softmax(sc, axis=-1)
        u_sel = u[e]
        v_sel = v[e]
        pre = jnp.einsum("td,thkd->thk", xc, u_sel).astype(f32)
        act = (jax.nn.gelu(pre, approximate=False) * g).astype(v.dtype)
        return jnp.einsum("thk,thkd->td", act, v_sel)

    return lax.map(one_chunk, hc).reshape(b, s, d)

def first_inputs(seed: int = 0) -> dict:
    key = jax.random.key(seed)
    ks = jax.random.split(key, 24)
    f32 = jnp.float32
    nrm = lambda k, shape, scale: jax.random.normal(k, shape, f32) * scale
    L, D = DEPTH, D_MODEL
    dt0 = jnp.exp(jax.random.uniform(ks[8], (L, SSD_HEADS), f32) * (np.log(0.1) - np.log(0.001)) + np.log(0.001))
    return {
        "x": nrm(ks[0], (BATCH, SEQ, D), 1.0),
        "c": nrm(ks[1], (BATCH, D), 1.0),
        "ada_w": nrm(ks[2], (L, D, 6 * D), 0.5 * D ** -0.5),
        "ada_b": nrm(ks[3], (L, 6 * D), 0.01),
        "norm1_g": 1.0 + nrm(ks[4], (L, D), 0.02),
        "norm2_g": 1.0 + nrm(ks[5], (L, D), 0.02),
        "w_in": nrm(ks[6], (L, D, N_IN), D ** -0.5),
        "conv_w": nrm(ks[7], (L, CONV_K, XBC_WIDTH), CONV_K ** -0.5),
        "conv_b": nrm(ks[9], (L, XBC_WIDTH), 0.01),
        "dt_bias": dt0 + jnp.log(-jnp.expm1(-dt0)),
        "a_log": jnp.log(jax.random.uniform(ks[10], (L, SSD_HEADS), f32, 1.0, 16.0)),
        "d_skip": 1.0 + nrm(ks[11], (L, SSD_HEADS), 0.1),
        "ssd_norm_g": 1.0 + nrm(ks[12], (L, SSD_WIDTH), 0.02),
        "moba_norm_g": 1.0 + nrm(ks[13], (L, MOBA_WIDTH), 0.02),
        "swa_sinks": nrm(ks[14], (L, SWA_HEADS), 0.5),
        "swa_norm_g": 1.0 + nrm(ks[15], (L, SWA_WIDTH), 0.02),
        "w_out": nrm(ks[16], (L, MIX_WIDTH, D), MIX_WIDTH ** -0.5),
        "peer_wq": nrm(ks[17], (L, D, PEER_HEADS * PEER_DKEY), D ** -0.5),
        "peer_k1": nrm(ks[18], (L, PEER_NKEYS, PEER_HALF), PEER_HALF ** -0.5),
        "peer_k2": nrm(ks[19], (L, PEER_NKEYS, PEER_HALF), PEER_HALF ** -0.5),
        "peer_u": nrm(ks[20], (L, PEER_EXPERTS, D), D ** -0.5),
        "peer_v": nrm(ks[21], (L, PEER_EXPERTS, D), PEER_HEADS ** -0.5),
        "final_g": 1.0 + nrm(ks[22], (D,), 0.02),
    }

def first_block(x, c, ada_w, ada_b, norm1_g, norm2_g, w_in, conv_w, conv_b, dt_bias, a_log, d_skip,
              ssd_norm_g, moba_norm_g, swa_sinks, swa_norm_g, w_out, peer_wq, peer_k1, peer_k2,
              peer_u, peer_v, final_g):
    in_widths = [SSD_WIDTH, XBC_WIDTH, SSD_HEADS, MOBA_WIDTH, MOBA_WIDTH, MOBA_WIDTH,
                 SWA_WIDTH, SWA_KV_WIDTH, SWA_KV_WIDTH]
    offsets = np.cumsum(in_widths)[:-1].tolist()
    cond = jax.nn.silu(c)
    for l in range(DEPTH):
        mod = cond @ ada_w[l] + ada_b[l]
        sh1, sc1, g1, sh2, sc2, g2 = [m[:, None, :] for m in jnp.split(mod, 6, axis=-1)]
        h = rms_norm(x, norm1_g[l]) * (1.0 + sc1) + sh1
        proj = h @ w_in[l]
        z, xbc, dt_raw, mq, mk, mv, sq, sk, sv = jnp.split(proj, offsets, axis=-1)
        y_ssd = ssd_mixer(z, xbc, dt_raw, conv_w[l], conv_b[l], dt_bias[l], a_log[l], d_skip[l], ssd_norm_g[l])
        y_moba = moba_attention(mq, mk, mv, moba_norm_g[l])
        y_swa = swa_attention(sq, sk, sv, swa_sinks[l], swa_norm_g[l])
        y = jnp.concatenate([y_ssd, y_moba, y_swa], axis=-1) @ w_out[l]
        x = x + g1 * y
        h = rms_norm(x, norm2_g[l]) * (1.0 + sc2) + sh2
        x = x + g2 * peer_ffn(h, peer_wq[l], peer_k1[l], peer_k2[l], peer_u[l], peer_v[l])
    return rms_norm(x, final_g)


NSA_HEADS = 8
NSA_HEAD_DIM = 64
NSA_KV_HEADS = 2
NSA_GROUP = NSA_HEADS // NSA_KV_HEADS
NSA_WIDTH = NSA_HEADS * NSA_HEAD_DIM
KV_WIDTH = NSA_KV_HEADS * NSA_HEAD_DIM
CMP_LEN = 32
CMP_STRIDE = 16
CMP_HIDDEN = 256
SLC_LEN = 64
SLC_TOPN = 16
WINDOW = 512
Q_BLOCK = 128
RET_HEADS = 4
RET_HEAD_DIM = 128
RET_WIDTH = RET_HEADS * RET_HEAD_DIM
RET_CHUNK = 128
MEM_LEN = 256
MEM_HEADS = 4
MEM_HEAD_DIM = D_MODEL // MEM_HEADS
D_FF = 2816
EPS_2 = 1e-6
NEG = -1e30

IN_SIZES = (NSA_WIDTH,
            KV_WIDTH, KV_WIDTH,
            KV_WIDTH, KV_WIDTH,
            KV_WIDTH, KV_WIDTH,
            NSA_HEADS * 3,
            RET_WIDTH, RET_WIDTH, RET_WIDTH, RET_WIDTH)
IN_WIDTH = sum(IN_SIZES)
IN_OFFSETS = tuple(int(o) for o in np.cumsum(IN_SIZES)[:-1])


def rms_norm_2(x, g):
    xf = x.astype(jnp.float32)
    y = xf * lax.rsqrt(jnp.mean(xf * xf, axis=-1, keepdims=True) + EPS_2)
    return (y * g.astype(jnp.float32)).astype(x.dtype)

def swiglu(x, w_gate, w_up, w_down):
    return (jax.nn.silu(x @ w_gate) * (x @ w_up)) @ w_down

def masked_softmax(s, mask):
    s = jnp.where(mask, s, NEG)
    m = jnp.max(s, axis=-1, keepdims=True)
    p = jnp.where(mask, jnp.exp(s - m), 0.0)
    return p / jnp.maximum(jnp.sum(p, axis=-1, keepdims=True), 1e-30)

def alibi_slopes(n):
    return jnp.asarray(2.0 ** (-8.0 * np.arange(1, n + 1) / n), dtype=jnp.float32)

def compress(kv, pe, w1, w2):
    B, T, G, dh = kv.shape
    nc = (T - CMP_LEN) // CMP_STRIDE + 1
    idx = np.arange(nc)[:, None] * CMP_STRIDE + np.arange(CMP_LEN)[None, :]
    blocks = kv[:, idx] + pe[None, None, :, None, :]
    flat = blocks.transpose(0, 1, 3, 2, 4).reshape(B, nc, G, CMP_LEN * dh)
    return jax.nn.silu(flat @ w1) @ w2

def nsa_mixer(q, k_cmp, v_cmp, k_slc, v_slc, k_win, v_win, gates, cmp_pe, cmp_w1, cmp_w2):
    B, T = q.shape[:2]
    G, R, dh = NSA_KV_HEADS, NSA_GROUP, NSA_HEAD_DIM
    scale = dh ** -0.5
    slopes = alibi_slopes(NSA_HEADS).reshape(G, R)

    kc = compress(k_cmp, cmp_pe[0], cmp_w1[0], cmp_w2[0])
    vc = compress(v_cmp, cmp_pe[1], cmp_w1[1], cmp_w2[1])
    nc = kc.shape[1]
    nsel = T // SLC_LEN
    n_top = min(SLC_TOPN, nsel)

    c_start_np = np.arange(nc) * CMP_STRIDE
    c_end_np = c_start_np + CMP_LEN - 1
    s_start_np = np.arange(nsel) * SLC_LEN
    s_end_np = s_start_np + SLC_LEN - 1
    overlap = jnp.asarray(np.clip(np.minimum(c_end_np[:, None], s_end_np[None, :])
                                  - np.maximum(c_start_np[:, None], s_start_np[None, :]) + 1,
                                  0, None) / CMP_LEN, dtype=jnp.float32)
    c_end = jnp.asarray(c_end_np, dtype=jnp.int32)
    c_mid = jnp.asarray(c_start_np + (CMP_LEN - 1) / 2.0, dtype=jnp.float32)

    k_blocks = k_slc.reshape(B, nsel, SLC_LEN, G, dh).transpose(0, 3, 1, 2, 4)
    v_blocks = v_slc.reshape(B, nsel, SLC_LEN, G, dh).transpose(0, 3, 1, 2, 4)
    k_win_p = jnp.pad(k_win, ((0, 0), (WINDOW, 0), (0, 0), (0, 0)))
    v_win_p = jnp.pad(v_win, ((0, 0), (WINDOW, 0), (0, 0), (0, 0)))

    nb = T // Q_BLOCK
    qb = q.reshape(B, nb, Q_BLOCK, G, R, dh).transpose(1, 0, 2, 3, 4, 5)
    gb = gates.reshape(B, nb, Q_BLOCK, G, R, 3).transpose(1, 0, 2, 3, 4, 5)
    b_ix = jnp.arange(B)[:, None, None, None]
    g_ix = jnp.arange(G)[None, None, :, None]
    jb = jnp.arange(nsel)

    def block_fn(args):
        i, qi, gi = args
        t = i * Q_BLOCK + jnp.arange(Q_BLOCK)
        tf = t.astype(jnp.float32)

        s_c = jnp.einsum('bqgrd,bngd->bgrqn', qi, kc).astype(jnp.float32) * scale
        s_c = s_c - slopes[None, :, :, None, None] * (tf[:, None] - c_mid[None, :])
        p_c = masked_softmax(s_c, (c_end[None, :] <= t[:, None])[None, None, None])
        o_c = jnp.einsum('bgrqn,bngd->bqgrd', p_c.astype(vc.dtype), vc)

        imp = jnp.einsum('bgrqn,nj->bqgj', p_c, overlap)
        cur = t // SLC_LEN
        forced = (jb[None, :] == 0) | (jb[None, :] == cur[:, None]) | (jb[None, :] == cur[:, None] - 1)
        valid = jb[None, :] <= cur[:, None]
        imp = jnp.where(forced[None, :, None, :], 1e4,
                        jnp.where(valid[None, :, None, :], imp, -1.0))
        _, idx = lax.top_k(imp, n_top)

        ks = k_blocks[b_ix, g_ix, idx].reshape(B, Q_BLOCK, G, n_top * SLC_LEN, dh)
        vs = v_blocks[b_ix, g_ix, idx].reshape(B, Q_BLOCK, G, n_top * SLC_LEN, dh)
        spos = (idx[..., None] * SLC_LEN + jnp.arange(SLC_LEN)).reshape(B, Q_BLOCK, G, 1, n_top * SLC_LEN)
        dist_s = t[None, :, None, None, None] - spos
        s_s = jnp.einsum('bqgrd,bqgmd->bqgrm', qi, ks).astype(jnp.float32) * scale
        s_s = s_s - slopes[None, None, :, :, None] * dist_s.astype(jnp.float32)
        p_s = masked_softmax(s_s, dist_s >= 0)
        o_s = jnp.einsum('bqgrm,bqgmd->bqgrd', p_s.astype(vs.dtype), vs)

        kw = lax.dynamic_slice_in_dim(k_win_p, i * Q_BLOCK, WINDOW + Q_BLOCK, axis=1)
        vw = lax.dynamic_slice_in_dim(v_win_p, i * Q_BLOCK, WINDOW + Q_BLOCK, axis=1)
        kpos = i * Q_BLOCK - WINDOW + jnp.arange(WINDOW + Q_BLOCK)
        dist_w = t[:, None] - kpos[None, :]
        mask_w = (dist_w >= 0) & (dist_w < WINDOW) & (kpos[None, :] >= 0)
        s_w = jnp.einsum('bqgrd,bkgd->bqgrk', qi, kw).astype(jnp.float32) * scale
        s_w = s_w - slopes[None, None, :, :, None] * dist_w[None, :, None, None, :].astype(jnp.float32)
        p_w = masked_softmax(s_w, mask_w[None, :, None, None, :])
        o_w = jnp.einsum('bqgrk,bkgd->bqgrd', p_w.astype(vw.dtype), vw)

        gs = jax.nn.sigmoid(gi.astype(jnp.float32))
        o = (gs[..., 0:1] * o_c.astype(jnp.float32) + gs[..., 1:2] * o_s.astype(jnp.float32)
             + gs[..., 2:3] * o_w.astype(jnp.float32))
        return o.reshape(B, Q_BLOCK, NSA_WIDTH).astype(q.dtype)

    out = lax.map(block_fn, (jnp.arange(nb), qb, gb))
    return out.transpose(1, 0, 2, 3).reshape(B, T, NSA_WIDTH)

def retention(q, k, v, g, gn_gain):
    B, T, Hr, d = q.shape
    C = RET_CHUNK
    nch = T // C
    log_g = jnp.log(1.0 - jnp.exp2(-5.0 - jnp.arange(Hr, dtype=jnp.float32)))
    pos = jnp.arange(C, dtype=jnp.float32)
    diff = pos[:, None] - pos[None, :]
    decay_mask = jnp.where(diff >= 0, jnp.exp(jnp.maximum(diff, 0.0) * log_g[:, None, None]), 0.0)
    q_dec = jnp.exp((pos + 1.0) * log_g[:, None])
    k_dec = jnp.exp((C - 1.0 - pos) * log_g[:, None])
    chunk_dec = jnp.exp(C * log_g)

    def to_chunks(a):
        return a.astype(jnp.float32).reshape(B, nch, C, Hr, d).transpose(1, 0, 3, 2, 4)
    qc, kc, vc = to_chunks(q), to_chunks(k * (d ** -0.5)), to_chunks(v)

    def step(state, xs):
        qi, ki, vi = xs
        s = jnp.einsum('bhnd,bhmd->bhnm', qi, ki) * decay_mask[None]
        inner = jnp.einsum('bhnm,bhmd->bhnd', s, vi)
        cross = jnp.einsum('bhnd,bhde->bhne', qi, state) * q_dec[None, :, :, None]
        new_state = (state * chunk_dec[None, :, None, None]
                     + jnp.einsum('bhmd,bhme->bhde', ki * k_dec[None, :, :, None], vi))
        return new_state, inner + cross

    state0 = jnp.zeros((B, Hr, d, d), jnp.float32)
    _, o = lax.scan(step, state0, (qc, kc, vc))
    o = o.transpose(1, 0, 3, 2, 4).reshape(B, T, Hr, d)
    mu = jnp.mean(o, axis=-1, keepdims=True)
    var = jnp.mean(jnp.square(o - mu), axis=-1, keepdims=True)
    o = (o - mu) * lax.rsqrt(var + EPS_2) * gn_gain.astype(jnp.float32).reshape(Hr, d)
    o = o.reshape(B, T, RET_WIDTH) * jax.nn.silu(g.astype(jnp.float32))
    return o.astype(q.dtype)

def hybrid_mixer(h, w_in, cmp_pe, cmp_w1, cmp_w2, nsa_out_g, ret_gn_g, w_out):
    B, T, _ = h.shape
    parts = jnp.split(h @ w_in, IN_OFFSETS, axis=-1)
    q_n, kc, vc, ks, vs, kw, vw, gates, q_r, k_r, v_r, g_r = parts
    kvs = lambda a: a.reshape(B, T, NSA_KV_HEADS, NSA_HEAD_DIM)
    o_nsa = nsa_mixer(q_n.reshape(B, T, NSA_HEADS, NSA_HEAD_DIM), kvs(kc), kvs(vc), kvs(ks), kvs(vs),
                      kvs(kw), kvs(vw), gates.reshape(B, T, NSA_HEADS, 3), cmp_pe, cmp_w1, cmp_w2)
    o_nsa = rms_norm_2(o_nsa, nsa_out_g)
    rs = lambda a: a.reshape(B, T, RET_HEADS, RET_HEAD_DIM)
    o_ret = retention(rs(q_r), rs(k_r), rs(v_r), g_r, ret_gn_g)
    return jnp.concatenate([o_nsa, o_ret], axis=-1) @ w_out

def memory_xattn(h, m, wq, wk, wv, wo):
    B, T, _ = h.shape
    M = m.shape[1]
    q = (h @ wq).reshape(B, T, MEM_HEADS, MEM_HEAD_DIM)
    k = (m @ wk).reshape(B, M, MEM_HEADS, MEM_HEAD_DIM)
    v = (m @ wv).reshape(B, M, MEM_HEADS, MEM_HEAD_DIM)
    s = jnp.einsum('bthd,bmhd->bhtm', q, k).astype(jnp.float32) * (MEM_HEAD_DIM ** -0.5)
    p = jax.nn.softmax(s, axis=-1)
    o = jnp.einsum('bhtm,bmhd->bthd', p.astype(v.dtype), v).reshape(B, T, D_MODEL)
    return o @ wo

def second_inputs(seed: int = 0) -> dict:
    key = jax.random.key(seed)
    ks = jax.random.split(key, 28)
    f32 = jnp.float32

    def dense(k, shape, fan_in):
        return jax.random.normal(k, shape, f32) * (fan_in ** -0.5)

    def gain(k, n):
        return 1.0 + 0.02 * jax.random.normal(k, (DEPTH, n), f32)

    L, dh = CMP_LEN, NSA_HEAD_DIM
    return {
        "x": jax.random.normal(ks[0], (BATCH, SEQ, D_MODEL), f32),
        "mem": jax.random.normal(ks[1], (BATCH, MEM_LEN, D_MODEL), f32),
        "ffn1_pre_g": gain(ks[2], D_MODEL),
        "ffn1_w_gate": dense(ks[3], (DEPTH, D_MODEL, D_FF), D_MODEL),
        "ffn1_w_up": dense(ks[4], (DEPTH, D_MODEL, D_FF), D_MODEL),
        "ffn1_w_down": dense(ks[5], (DEPTH, D_FF, D_MODEL), D_FF),
        "ffn1_post_g": gain(ks[6], D_MODEL),
        "mix_pre_g": gain(ks[7], D_MODEL),
        "w_in": dense(ks[8], (DEPTH, D_MODEL, IN_WIDTH), D_MODEL),
        "cmp_pe": 0.5 * jax.random.normal(ks[9], (DEPTH, 2, L, dh), f32),
        "cmp_w1": dense(ks[10], (DEPTH, 2, L * dh, CMP_HIDDEN), L * dh),
        "cmp_w2": dense(ks[11], (DEPTH, 2, CMP_HIDDEN, dh), CMP_HIDDEN),
        "nsa_out_g": gain(ks[12], NSA_WIDTH),
        "ret_gn_g": gain(ks[13], RET_WIDTH),
        "w_out": dense(ks[14], (DEPTH, NSA_WIDTH + RET_WIDTH, D_MODEL), NSA_WIDTH + RET_WIDTH),
        "mix_post_g": gain(ks[15], D_MODEL),
        "xa_pre_g": gain(ks[16], D_MODEL),
        "xa_mem_g": gain(ks[17], D_MODEL),
        "xa_wq": dense(ks[18], (DEPTH, D_MODEL, D_MODEL), D_MODEL),
        "xa_wk": dense(ks[19], (DEPTH, D_MODEL, D_MODEL), D_MODEL),
        "xa_wv": dense(ks[20], (DEPTH, D_MODEL, D_MODEL), D_MODEL),
        "xa_wo": dense(ks[21], (DEPTH, D_MODEL, D_MODEL), D_MODEL),
        "xa_post_g": gain(ks[22], D_MODEL),
        "ffn2_pre_g": gain(ks[23], D_MODEL),
        "ffn2_w_gate": dense(ks[24], (DEPTH, D_MODEL, D_FF), D_MODEL),
        "ffn2_w_up": dense(ks[25], (DEPTH, D_MODEL, D_FF), D_MODEL),
        "ffn2_w_down": dense(ks[26], (DEPTH, D_FF, D_MODEL), D_FF),
        "ffn2_post_g": gain(ks[27], D_MODEL),
    }

def second_block(x, mem, ffn1_pre_g, ffn1_w_gate, ffn1_w_up, ffn1_w_down, ffn1_post_g,
              mix_pre_g, w_in, cmp_pe, cmp_w1, cmp_w2, nsa_out_g, ret_gn_g, w_out, mix_post_g,
              xa_pre_g, xa_mem_g, xa_wq, xa_wk, xa_wv, xa_wo, xa_post_g,
              ffn2_pre_g, ffn2_w_gate, ffn2_w_up, ffn2_w_down, ffn2_post_g):
    for l in range(DEPTH):
        y = swiglu(rms_norm_2(x, ffn1_pre_g[l]), ffn1_w_gate[l], ffn1_w_up[l], ffn1_w_down[l])
        x = x + 0.5 * rms_norm_2(y, ffn1_post_g[l])
        y = hybrid_mixer(rms_norm_2(x, mix_pre_g[l]), w_in[l], cmp_pe[l], cmp_w1[l], cmp_w2[l],
                         nsa_out_g[l], ret_gn_g[l], w_out[l])
        x = x + rms_norm_2(y, mix_post_g[l])
        y = memory_xattn(rms_norm_2(x, xa_pre_g[l]), rms_norm_2(mem, xa_mem_g[l]),
                         xa_wq[l], xa_wk[l], xa_wv[l], xa_wo[l])
        x = x + rms_norm_2(y, xa_post_g[l])
        y = swiglu(rms_norm_2(x, ffn2_pre_g[l]), ffn2_w_gate[l], ffn2_w_up[l], ffn2_w_down[l])
        x = x + 0.5 * rms_norm_2(y, ffn2_post_g[l])
    return x


def setup_inputs(seed=0):
    out = dict(first_inputs(seed))
    for name, value in second_inputs(seed + 1).items():
        if name != "x":
            out[name + "_2"] = value
    return out


def reference(
    x, c, ada_w, ada_b, norm1_g, norm2_g, w_in, conv_w, conv_b, dt_bias, a_log, d_skip,
    ssd_norm_g, moba_norm_g, swa_sinks, swa_norm_g, w_out, peer_wq, peer_k1, peer_k2, peer_u,
    peer_v, final_g, mem_2, ffn1_pre_g_2, ffn1_w_gate_2, ffn1_w_up_2, ffn1_w_down_2,
    ffn1_post_g_2, mix_pre_g_2, w_in_2, cmp_pe_2, cmp_w1_2, cmp_w2_2, nsa_out_g_2, ret_gn_g_2,
    w_out_2, mix_post_g_2, xa_pre_g_2, xa_mem_g_2, xa_wq_2, xa_wk_2, xa_wv_2, xa_wo_2,
    xa_post_g_2, ffn2_pre_g_2, ffn2_w_gate_2, ffn2_w_up_2, ffn2_w_down_2, ffn2_post_g_2,
):
    x = first_block(
        x, c, ada_w, ada_b, norm1_g, norm2_g, w_in, conv_w, conv_b, dt_bias, a_log, d_skip,
        ssd_norm_g, moba_norm_g, swa_sinks, swa_norm_g, w_out, peer_wq, peer_k1, peer_k2,
        peer_u, peer_v, final_g,
    )
    return second_block(
        x, mem_2, ffn1_pre_g_2, ffn1_w_gate_2, ffn1_w_up_2, ffn1_w_down_2, ffn1_post_g_2,
        mix_pre_g_2, w_in_2, cmp_pe_2, cmp_w1_2, cmp_w2_2, nsa_out_g_2, ret_gn_g_2, w_out_2,
        mix_post_g_2, xa_pre_g_2, xa_mem_g_2, xa_wq_2, xa_wk_2, xa_wv_2, xa_wo_2, xa_post_g_2,
        ffn2_pre_g_2, ffn2_w_gate_2, ffn2_w_up_2, ffn2_w_down_2, ffn2_post_g_2,
    )


_drawn_inputs = setup_inputs


def setup_inputs(seed=0):
    import zlib

    import numpy as np

    out = dict(_drawn_inputs(seed))
    spreads = {}
    factors = {'norm2_g': 2.884,
     'conv_b': 4.935,
     'ssd_norm_g': 3.953,
     'moba_norm_g': 4.514,
     'swa_sinks': 3.444,
     'swa_norm_g': 4.372,
     'ffn1_pre_g_2': 2.911,
     'ffn1_post_g_2': 3.714,
     'nsa_out_g_2': 3.427,
     'ret_gn_g_2': 6.096,
     'mix_post_g_2': 3.098,
     'xa_pre_g_2': 3.483,
     'xa_post_g_2': 3.343,
     'ffn2_pre_g_2': 5.3,
     'ffn2_post_g_2': 7.359}
    for name, (base, spread) in spreads.items():
        noise = np.random.default_rng([zlib.crc32(name.encode()), seed]).standard_normal(out[name].shape)
        drawn = base * np.exp(spread * noise) if base else spread * noise
        out[name] = __import__('jax').numpy.asarray(drawn.astype(out[name].dtype))
    for name, factor in factors.items():
        out[name] = (out[name] * factor).astype(out[name].dtype)
    return out
```

```python
from contextlib import ExitStack

import concourse.bass as bass
import numpy as np
from concourse import mybir

F32 = mybir.dt.float32
F32R = mybir.dt.float32r
U32 = mybir.dt.uint32
ALU = mybir.AluOpType
ACT = mybir.ActivationFunctionType
AX = mybir.AxisListType

P = 128
DEPTH = 2
D = 1024
T = 256
TT = T // P
KC = D // P
NBLK = 512
TILE = KC * NBLK
RING = 4
EXPERTS = 2048
NEG = -1e30
LOWEST = -3.0e38

HD = 64
SSD_H = 8
SSD_W = SSD_H * HD
ATT_H = 4
PH, PK, NKEYS = 8, 16, 128
HALF = NKEYS // 2
TURNS = HALF // 4
GROUPS = T // 8
EPS1, EPS2 = 1e-5, 1e-6

D_FF = 2816
FC = D_FF // P
NSA_H, NSA_G = 8, 2
NCMP = (T - 32) // 16 + 1
JP = 16
RH = 4
XH = 4

C_ID, C_STRICT, C_KEEP, C_CAUS, C_BAND, C_IOTA, C_END = np.cumsum([0, 128, 128, 384, 256, 384, 128]).tolist()
R1 = dict(zip(["n1", "n2", "ssd", "moba", "swa", "dtb", "alog", "dsk", "sink", "end"],
              np.cumsum([0, D, D, SSD_W, 256, 256, 8, 8, 8, 4]).tolist()))
K1 = dict(zip(["cw", "cb", "k1", "k2", "end"], np.cumsum([0, 32, 8, 128, 128]).tolist()))
R2 = dict(zip(["f1", "mix", "xa", "f2", "nsa", "ret", "end"], np.cumsum([0, D, D, D, D, 512, 512]).tolist()))
K2 = dict(zip(["f1", "mix", "xa", "mem", "f2", "pe", "w2", "end"], np.cumsum([0, 8, 8, 8, 8, 8, 32, 256]).tolist()))
C2 = dict(zip(["alibi", "cbias", "cmask", "bmask", "ret", "end"],
              np.cumsum([0, NSA_H * 384, 240, 240, 4, RH * 384]).tolist()))


class Plan:

    def __init__(self, banks_before, tiles_before):
        self.bank_base = banks_before
        self.tile_base = tiles_before
        self.count = [0] * 8
        self.next = 0
        self.fills = {}
        self.tiles = {}

    def fill(self, name, n, bank=None, times=1):
        for i in range(n):
            b = self.next if bank is None else bank + i
            if bank is None:
                self.next = (b + 1) % 8
            self.fills[name, i] = (b, self.count[b])
            self.count[b] += times

    def tile(self, name, n):
        for i in range(n):
            self.tiles[name, i] = len(self.tiles)


def plan_first():
    p = Plan([0] * 8, 0)
    p.tile("ada", 12)
    p.tile("win", 6)
    p.tile("wout", 2)
    p.tile("wq", 4)
    p.fill("ada", 12)
    p.fill("hT", 4)
    p.fill("win", 12)
    p.fill("mS", ATT_H)
    p.fill("sS", ATT_H)
    p.fill("xs", 2)
    p.fill("cb", 2)
    p.fill("mPT", ATT_H)
    p.fill("mO", 1)
    p.fill("sPT", ATT_H)
    p.fill("sO", 1)
    p.fill("seg01", 2)
    p.fill("y", 2)
    p.fill("seg", 6)
    p.fill("yT", 4)
    p.fill("wout", 4)
    p.fill("h2T", 4)
    p.fill("wq", 8)
    p.fill("s", 8)
    p.fill("eT", 2)
    for hf in range(2):
        p.fill(f"G{hf}", 4, bank=0, times=8)
        if hf == 0:
            p.fill("acc", 4, bank=4)
        p.fill(f"U{hf}", 2, bank=0, times=TURNS)
    p.per_slot = len(p.tiles) // RING
    assert len(p.tiles) % RING == 0
    return p


def plan_second(first):
    p = Plan([DEPTH * c for c in first.count], DEPTH * first.per_slot)
    for f in ("f1", "f2"):
        if f == "f2":
            p.tile("nin", 8)
            p.tile("cw1", 2)
            p.tile("nout", 2)
            p.tile("xk", 2)
            p.tile("xv", 2)
            p.tile("xq", 2)
            p.tile("xo", 2)
            p.fill("nT", 4)
            p.fill("nin", 16)
            p.fill("hid", 1)
            p.fill("hidT", 1)
            p.fill("kc", 1)
            p.fill("cS", 1)
            p.fill("wS", NSA_H)
            p.fill("cPT", 1)
            p.fill("cO", 2)
            p.fill("wPT", NSA_H)
            p.fill("wO", 2)
            p.fill("lS", NSA_H)
            p.fill("rS", RH)
            p.fill("lPT", NSA_H)
            p.fill("lO", 2)
            p.fill("rO", 2)
            p.fill("oT", 4)
            p.fill("nout", 4)
            p.fill("xT", 4)
            p.fill("xk", 4)
            p.fill("xv", 4)
            p.fill("xq", 4)
            p.fill("xS", XH)
            p.fill("xPT", XH)
            p.fill("xO", XH)
            p.fill("xo", 4)
        p.tile(f + "gu", 12)
        p.tile(f + "d", 6)
        p.fill(f + "T", 4)
        p.fill(f + "gu", 22)
        p.fill(f + "d", 4)
    p.per_slot = len(p.tiles) // RING
    assert len(p.tiles) % RING == 0
    return p


class At:

    def __init__(self, plan, l, banks_filled, banks_emptied, tiles_landed, tiles_used, ps, ring):
        self.plan, self.l = plan, l
        self.bf, self.be, self.tl, self.tu = banks_filled, banks_emptied, tiles_landed, tiles_used
        self.ps, self.ring = ps, ring

    def bank(self, name, i=0):
        return self.ps[:, self.plan.fills[name, i][0], :]

    def _use(self, name, i, it):
        b, n = self.plan.fills[name, i]
        return b, self.l * self.plan.count[b] + it + (self.plan.bank_base[b] + n)

    def free(self, name, i=0, it=0):
        b, n = self._use(name, i, it)
        return self.be[b], n + 1

    def filled(self, name, i=0, it=0):
        b, n = self._use(name, i, it)
        return self.bf[b], n + 1

    def emptied(self, name, i=0, it=0):
        b, n = self._use(name, i, it)
        return self.be[b], n + 2

    def fill_sem(self, name, i=0):
        return self.bf[self.plan.fills[name, i][0]]

    def empty_sem(self, name, i=0):
        return self.be[self.plan.fills[name, i][0]]

    def _tile(self, name, i, it):
        n = self.plan.tiles[name, i]
        return n % RING, self.l * self.plan.per_slot + it + (self.plan.tile_base + n // RING)

    def tile(self, name, i):
        return self.ring[:, self.plan.tiles[name, i] % RING, :]

    def landed(self, name, i):
        s, n = self._tile(name, i, 0)
        return self.tl[s], 16 * n + 16

    def slot_free(self, name, i):
        s, n = self._tile(name, i, 0)
        return self.tu[s], n + 1

    def used_sem(self, name, i):
        return self.tu[self.plan.tiles[name, i] % RING]

    def land_sem(self, name, i):
        return self.tl[self.plan.tiles[name, i] % RING]

    def slot_over(self, slot):
        return self.tu[slot], self.l * self.plan.per_slot + (self.plan.tile_base + self.plan.per_slot + 1)


class Experts:

    def __init__(self, l, hf, it, landed, parted, used, upper_ready):
        self.turn = l * (2 * TURNS) + it + TURNS * hf
        self._landed, self._parted, self._used, self._upper = landed, parted, used, upper_ready

    def landed(self, r):
        return self._landed[r], 16 * self.turn + 16

    def raw_free(self, r):
        return self._parted[r], 2 * self.turn + 1

    def parted(self, r):
        return self._parted[r], 2 * self.turn + 3

    def split_free(self, r):
        return self._used[r % 2], 2 * self.turn + (r // 2 + 1)

    def used_sem(self, r):
        return self._used[r % 2]

    def upper(self, r):
        return self._upper, 4 * self.turn + (r + 1)


def column(ap, n):
    a = ap.shape[1]
    return ap.rearrange("p (a o) -> p a o", o=1).broadcast_to([ap.shape[0], a, n])


def row(ap, n):
    a = ap.shape[1]
    return ap.rearrange("p (o a) -> p o a", o=1).broadcast_to([ap.shape[0], n, a])


def two_mixers_and_peer_then_nsa_retention_memory(nc, a, out):
    first = plan_first()
    mid = Plan([DEPTH * c for c in first.count], 0)
    mid.fill("mT", 4)
    second = plan_second(first)
    second.bank_base = [b + c for b, c in zip(second.bank_base, mid.count)]

    ctx = ExitStack()
    with ctx:
        def sb(name, n, dt=F32):
            return ctx.enter_context(nc.sbuf_tensor(name, [P, n], dt))

        def sem(name):
            return ctx.enter_context(nc.semaphore(name))

        ring_at = -(-nc.sbuf_base // 32) * 32
        ring = ctx.enter_context(nc.sbuf_tensor("weights", [P, RING, TILE], F32))
        work = sb("work", 16384)
        scr = sb("scr", 6144)
        mod_at = -(-nc.sbuf_base // 32) * 32
        mod = sb("mod", 6 * D)
        x = ctx.enter_context(nc.sbuf_tensor("x_res", [P, TT, D], F32))
        h_at = -(-nc.sbuf_base // 32) * 32
        h = ctx.enter_context(nc.sbuf_tensor("h", [P, TT, D], F32))
        hT = ctx.enter_context(nc.sbuf_tensor("hT", [P, KC, T], F32))
        cst = sb("cst", C_END)
        rowp = sb("rowp", R1["end"])
        colp = sb("colp", K2["end"])
        st = sb("stats", 384)
        ps = ctx.enter_context(nc.psum_tensor("ps", [P, 8, NBLK], F32))

        banks_filled = [sem(f"bank{b}_filled") for b in range(8)]
        banks_emptied = [sem(f"bank{b}_emptied") for b in range(8)]
        tiles_landed = [sem(f"slot{s}_landed") for s in range(RING)]
        tiles_used = [sem(f"slot{s}_used") for s in range(RING)]
        experts_landed = [sem(f"experts{r}_landed") for r in range(4)]
        experts_parted = [sem(f"experts{r}_parted") for r in range(4)]
        experts_used = [sem(f"parts{s}_used") for s in range(2)]
        upper_ready = sem("upper_ready")
        signals = {}

        def S(name):
            if name not in signals:
                signals[name] = sem(name)
            return signals[name]

        def at(plan, l):
            return At(plan, l, banks_filled, banks_emptied, tiles_landed, tiles_used, ps, ring)

        def experts(l, hf, it):
            return Experts(l, hf, it, experts_landed, experts_parted, experts_used, upper_ready)

        ident = cst[:, C_ID:C_ID + P]
        strict = cst[:, C_STRICT:C_STRICT + P]
        keep = cst[:, C_KEEP:C_KEEP + 384]
        tri, tri_ones, ones = keep[:, 0:P], keep[:, 0:2 * P], keep[:, P:2 * P]
        caus = cst[:, C_CAUS:C_CAUS + 384]
        band = cst[:, C_BAND:C_BAND + 384]
        zeros = caus[:, P:2 * P]
        iota = cst[:, C_IOTA:C_IOTA + P]

        def view(buf, at_, n, pat=None, **kw):
            v = buf[:, at_:at_ + n]
            return v.rearrange(pat, **kw) if pat else v

        xpad = view(work, 0, 8 * 259, "p (c t) -> p c t", c=8)
        conv = view(work, 2072, 2048, "p (c t) -> p c t", c=8)
        zs = view(work, 4120, 1024, "p (a n) -> p a n", a=TT)
        mqk = view(work, 5144, 1024, "p (c t) -> p c t", c=4)
        sqk = view(work, 6168, 1024, "p (c t) -> p c t", c=4)
        vt = view(work, 7192, 784, "p (a n) -> p a n", a=TT)
        cbm = view(work, 7976, 768, "p (g n) -> p g n", g=2)
        mP = view(work, 8744, 1536, "p (h n) -> p h n", h=ATT_H)
        sP = view(work, 10280, 1536, "p (h n) -> p h n", h=ATT_H)
        mPT = view(work, 11816, 1536, "p (h n) -> p h n", h=ATT_H)
        sPT = view(work, 13352, 1536, "p (h n) -> p h n", h=ATT_H)
        xs = view(scr, 0, 1024, "p (a n) -> p a n", a=TT)
        xdt = view(scr, 1024, 1024, "p (a n) -> p a n", a=TT)
        Aseg = view(scr, 2048, 768, "p (b n) -> p b n", b=2)
        Ldec = view(scr, 2816, 768, "p (b n) -> p b n", b=2)
        Mssd = view(scr, 3584, 1536, "p (b n) -> p b n", b=4)
        tmpA = view(scr, 5120, 1024, "p (b n) -> p b n", b=2)
        qT = view(work, 0, 4096, "p (c t) -> p c t", c=16)
        sc = view(work, 4096, 4096, "p (g n) -> p g n", g=32)
        sc2 = view(work, 8192, 4096, "p (g n) -> p g n", g=32)
        cand = view(work, 12288, 4096, "p (g n) -> p g n", g=16)
        sc_c = view(work, 4096, 4096, "p (g n) -> p g n", g=16)
        onehot = view(work, 0, 4096, "p (g j) -> p g j", j=16)
        V16 = view(scr, 0, 512, "p (g k) -> p g k", g=32)
        I16u = view(scr, 512, 512).bitcast(U32).rearrange("p (g k) -> p g k", g=32)
        I16 = view(scr, 1024, 512, "p (g k) -> p g k", g=32)
        Vc = view(scr, 1536, 256, "p (g k) -> p g k", g=16)
        Cu = view(scr, 1792, 256).bitcast(U32).rearrange("p (g k) -> p g k", g=16)
        Cd = view(scr, 2048, 512).bitcast(U32).rearrange("p (g k) -> p g k", g=2)
        Cf = view(scr, 2560, 512, "p (g k) -> p g k", g=2)
        E3 = view(scr, 3072, 768, "p (a t) -> p a t", a=3)
        gate = E3[:, 2, :].rearrange("p (g k) -> p g k", k=PK)
        ET = view(scr, 3840, 768, "p (a t) -> p a t", a=3)
        G = view(work, 0, 16384, "p (t i) -> p t i", i=HALF)
        hotA = view(h[:, :, :].rearrange("p a n -> p (a n)"), 0, 2048, "p (b t i) -> p b t i", b=2, t=8)
        hotB = view(scr, 4608, 1024, "p (b t i) -> p b t i", b=2, t=8)
        gact = view(scr, 5120, 1024, "p (u c t) -> p u c t", u=2, c=2)

        def parts_at(name, shape, at_):
            return nc.alloc_sbuf_tensor_at(name, shape, F32R, offset=at_)

        raw = ring[:, 0:2, :].rearrange("p s (r n) -> p (s r) n", r=2)
        upper = parts_at("experts_upper", [P, 2, EXPERTS], ring_at + 4 * 2 * TILE)
        lower = parts_at("experts_lower", [P, 2, EXPERTS], ring_at + 4 * 3 * TILE)
        hT_up = parts_at("hT_upper", [P, KC, T], mod_at)
        hT_lo = parts_at("hT_lower", [P, KC, T], mod_at + 4 * KC * T)
        hid_up = parts_at("hidden_upper", [P, 2, 2, T], h_at)
        hid_lo = parts_at("hidden_lower", [P, 2, 2, T], h_at + 4 * 4 * T)

        hidT = view(work, 0, FC * T, "p (c t) -> p c t", c=FC)
        sgate = view(scr, 2048, 1024, "p (b n) -> p b n", b=2)
        qn = view(work, 0, 1024, "p (c t) -> p c t", c=4)
        Z = view(work, 1024, 1024, "p (c t) -> p c t", c=4)
        kk = view(work, 2048, 1024, "p (c t) -> p c t", c=4)
        qr = view(work, 3072, 1024, "p (c t) -> p c t", c=4)
        kr = view(work, 4096, 1024, "p (c t) -> p c t", c=4)
        vr = view(work, 5120, 1024, "p (a n) -> p a n", a=TT)
        gr = view(work, 6144, 1024, "p (a n) -> p a n", a=TT)
        vt2 = view(work, 7168, 560, "p (a n) -> p a n", a=TT)
        Zp = view(work, 7728, 960, "p (s j n) -> p s j n", s=2, j=JP)
        sA = view(work, 8688, 3072, "p (h n) -> p h n", h=NSA_H)
        PT = view(work, 11760, 3072, "p (h n) -> p h n", h=NSA_H)
        retm = view(work, 14832, RH * 384, "p (h n) -> p h n", h=RH)
        memnT = view(scr, 0, 2048, "p (c t) -> p c t", c=KC)
        tmpB = view(scr, 2048, 1024, "p (b n) -> p b n", b=2)
        onsa = view(scr, 3072, 1024, "p (a n) -> p a n", a=TT)
        hidc = view(scr, 4096, 512)
        hidcT = view(scr, 4608, 128)
        hidrep = view(scr, 4736, 512, "p (k g n) -> p k g n", k=2, g=2)
        kcT = view(scr, 5248, 32)
        vcbd = view(scr, 5280, 512, "p (g r d) -> p g r d", g=2, r=4)
        cS = view(scr, 5792, 240)
        cPad = view(mod, R2["end"] + 484, 512)
        cPT = view(scr, 3072, 512)
        memT = view(work, 0, 2048, "p (c t) -> p c t", c=KC)
        qx = view(work, 2048, 2048, "p (c t) -> p c t", c=KC)
        kx = view(work, 4096, 2048, "p (c t) -> p c t", c=KC)
        vx = view(work, 6144, 2048, "p (a n) -> p a n", a=TT)
        Px = view(work, 8192, 2048, "p (h n) -> p h n", h=XH)
        PTx = view(work, 10240, 2048, "p (h n) -> p h n", h=XH)
        alibi = view(rowp, 0, 3072, "p (h n) -> p h n", h=NSA_H)
        rS = hT[:, 0:6, :].rearrange("p c t -> p (c t)").rearrange("p (h n) -> p h n", h=RH)

        SS, RR, RS = st[:, 0:8], st[:, 8:16], st[:, 16:24]

        def stat(i, n):
            return st[:, i:i + n]

        def halves(i, n):
            return st[:, i:i + TT * n].rearrange("p (a n) -> p a n", a=TT)

        cT = stat(300, 8)
        craw = stat(308, 8)

        block = ctx.enter_context(nc.Block())

        def two_groups_before(k, hf, b, it):
            return k.filled(f"G{hf}", b + 2, it - 1) if b < 2 else k.filled(f"G{hf}", b - 2, it)

        def lower_part(eng, r, c):
            return eng.tensor_tensor(lower[:, r % 2, c], raw[:, r, c], upper[:, r % 2, c].bitcast(F32), ALU.subtract)\
                .then_inc(experts_parted[r], 1)

        @block.sync
        def _(sp):
            def load(k, name, i, src):
                sp.wait_ge(*k.slot_free(name, i))
                sp.dma_start(k.tile(name, i), src).then_inc(k.land_sem(name, i), 16)

            def experts_over(e):
                for r in range(4):
                    sp.wait_ge(*e.raw_free(r))
                for r in range(2):
                    sp.wait_ge(*e.split_free(r))
                sp.sem_inc(S("held"), 1)

            with sp.Fori(0, DEPTH) as l:
                k = at(first, l)
                experts_over(experts(l, 0, 0))
                for (name, i), n in first.tiles.items():
                    load(k, name, i, a["stream1"][bass.ds(l, 1), n].rearrange("o p n -> p (o n)"))
                sp.wait_ge(*k.slot_over(0))
                sp.wait_ge(*k.slot_over(1))
                sp.sem_inc(S("held"), 1)
                for hf in range(2):
                    with sp.Fori(0, TURNS) as it:
                        e = experts(l, hf, it)
                        for r in range(4):
                            sp.wait_ge(*e.raw_free(r))
                            src = a["experts"][bass.ds(l, 1), bass.ds(it * 4 + (4 * TURNS * hf + r), 1)]
                            sp.dma_start(raw[:, r, :], src.rearrange("o q p n -> p (o q n)"))\
                                .then_inc(experts_landed[r], 16)
            experts_over(experts(DEPTH, 0, 0))
            with sp.Fori(0, DEPTH) as l:
                k = at(second, l)
                for (name, i), n in second.tiles.items():
                    load(k, name, i, a["stream2"][bass.ds(l, 1), n].rearrange("o p n -> p (o n)"))
            sp.wait_ge(S("second_done"), DEPTH + 1)
            sp.dma_start(out[0].rearrange("(a p) n -> p a n", a=TT), x[:, :, :]).then_inc(S("stored"), 16)
            sp.wait_ge(S("stored"), 16)

        @block.gpsimd
        def _(g):
            for b in range(8):
                g.sem_inc(banks_emptied[b], 1)
            for s in range(RING):
                g.sem_inc(tiles_used[s], 1)
            g.sem_inc(S("first_done"), 1)
            g.sem_inc(S("second_done"), 1)
            for r in range(4):
                g.sem_inc(experts_parted[r], 1)
            for s in range(2):
                g.sem_inc(experts_used[s], 1)
            with g.Fori(0, DEPTH) as l:
                k = at(first, l)
                g.wait_ge(S("hT_up"), l + 1)
                g.tensor_tensor(hT_lo[:, :, :], hT[:, :, :], hT_up[:, :, :].bitcast(F32), ALU.subtract)\
                    .then_inc(S("hT_lo"), 1)
                for hf in range(2):
                    with g.Fori(0, GROUPS // 4) as it:
                        for b in range(4):
                            g.wait_ge(S("marked"), l * 64 + it * 4 + (32 * hf + b + 1))
                            t8 = bass.ds(it * 32 + 8 * b, 8)
                            g.tensor_tensor(hotB[:, b % 2, :, :], hotB[:, b % 2, :, :], column(ET[:, 2, t8], HALF),
                                            ALU.mult).then_inc(S("hotB"), 1)
                    with g.Fori(0, TURNS) as it:
                        e = experts(l, hf, it)
                        for r in range(4):
                            g.wait_ge(*e.upper(r))
                            lower_part(g, r, slice(EXPERTS // 2, EXPERTS))

        @block.tensor
        def _(pe):
            mm = nc.tensor.matmul

            def transposes(k, name, src):
                for i in range(4):
                    pe.wait_ge(*k.free(name, i))
                    for j in range(4):
                        c, t = 2 * i + j // 2, j % 2
                        m = nc.tensor.transpose(k.bank(name, i)[:, j * P:(j + 1) * P],
                                                src[:, t, c * P:(c + 1) * P], ident)
                    m.then_inc(k.fill_sem(name, i), 1)

            def by_token(k, name, tile, fill, cols=NBLK, w=None, src=hT):
                pe.wait_ge(*k.landed(name, tile))
                w = k.tile(name, tile).rearrange("p (c n) -> p c n", c=KC)
                for t in range(TT):
                    pe.wait_ge(*k.free(name, fill + t))
                    for c in range(KC):
                        m = mm(k.bank(name, fill + t)[:, 0:cols], src[:, c, t * P:(t + 1) * P], w[:, c, 0:cols],
                               start=(c == 0), stop=(c == KC - 1))
                    if t == TT - 1:
                        m.then_inc(k.fill_sem(name, fill + t), 1)
                    else:
                        m.then_inc(k.fill_sem(name, fill + t), 1)
                pe.drain().then_inc(k.used_sem(name, tile), 1)

            def by_feature(k, name, tile, fill, chunks=4, src=hT):
                pe.wait_ge(*k.landed(name, tile))
                w = k.tile(name, tile).rearrange("p (c n) -> p c n", c=KC)
                for j in range(chunks // 2):
                    pe.wait_ge(*k.free(name, fill + j))
                    for e in range(2):
                        for c in range(KC):
                            m = mm(k.bank(name, fill + j)[:, e * T:(e + 1) * T],
                                   w[:, c, (2 * j + e) * P:(2 * j + e + 1) * P], src[:, c, :],
                                   start=(c == 0), stop=(c == KC - 1), skip_group_check=True)
                    m.then_inc(k.fill_sem(name, fill + j), 1)
                pe.drain().then_inc(k.used_sem(name, tile), 1)

            def scores(k, name, i, q, kt):
                pe.wait_ge(*k.free(name, i))
                b = k.bank(name, i)
                mm(b[:, 0:P], q[:, 0:P], kt[:, 0:P], start=True, stop=True, skip_group_check=True)
                mm(b[:, P:3 * P], q[:, P:T], kt, start=True, stop=True, skip_group_check=True)\
                    .then_inc(k.fill_sem(name, i), 1)

            def turn(k, name, i, src):
                pe.wait_ge(*k.free(name, i))
                for j in range(3):
                    m = nc.tensor.transpose(k.bank(name, i)[:, j * P:(j + 1) * P], src[:, j * P:(j + 1) * P], ident)
                m.then_inc(k.fill_sem(name, i), 1)

            def three_blocks(b0, b1, pt, v0, v1, start=True):
                mm(b0, pt[:, 0:P], v0, start=start, stop=True, skip_group_check=True)
                mm(b1, pt[:, P:2 * P], v0, start=start, stop=False, skip_group_check=True)
                return mm(b1, pt[:, 2 * P:3 * P], v1, start=False, stop=True, skip_group_check=True)

            pe.wait_ge(S("const_in"), 16)
            with pe.Fori(0, DEPTH) as l:
                k = at(first, l)
                for i in range(12):
                    pe.wait_ge(S("ada_acc"), l * 12 + (i + 1))
                    pe.wait_ge(*k.free("ada", i))
                    mm(k.bank("ada", i), ones, mod[:, i * NBLK:(i + 1) * NBLK], start=True, stop=True)\
                        .then_inc(k.fill_sem("ada", i), 1)
                pe.wait_ge(S("h1"), l + 1)
                transposes(k, "hT", h)
                for i in range(4):
                    pe.wait_ge(*k.emptied("hT", i))
                by_token(k, "win", 0, 0)
                for i in range(1, 5):
                    by_feature(k, "win", i, 2 * i)
                by_token(k, "win", 5, 10, cols=392)
                pe.wait_ge(*k.emptied("win", 6))
                pe.wait_ge(*k.emptied("win", 7))
                for i in range(ATT_H):
                    q0 = HD * (i % 2)
                    scores(k, "mS", i, mqk[q0:q0 + HD, i // 2, :], mqk[q0:q0 + HD, 2 + i // 2, :])
                pe.wait_ge(*k.emptied("win", 8))
                pe.wait_ge(*k.emptied("win", 9))
                for i in range(ATT_H):
                    q0 = HD * (i % 2)
                    scores(k, "sS", i, sqk[q0:q0 + HD, i // 2, :], sqk[q0:q0 + HD, 2 + i // 2, :])
                pe.wait_ge(S("conv_silu"), l + 1)
                for t in range(TT):
                    pe.wait_ge(*k.free("xs", t))
                    for c in range(4):
                        m = nc.tensor.transpose(k.bank("xs", t)[:, c * P:(c + 1) * P],
                                                conv[:, c, t * P:(t + 1) * P], ident)
                    m.then_inc(k.fill_sem("xs", t), 1)
                for g_ in range(2):
                    pe.wait_ge(*k.free("cb", g_))
                    b = k.bank("cb", g_)
                    mm(b[:, 0:T], conv[:, 4 + g_, 0:P], conv[:, 6 + g_, :], start=True, stop=True,
                       skip_group_check=True)
                    mm(b[:, T:3 * P], conv[:, 4 + g_, P:T], conv[:, 6 + g_, P:T], start=True, stop=True,
                       skip_group_check=True).then_inc(k.fill_sem("cb", g_), 1)
                pe.wait_ge(S("mexp"), l + 1)
                for i in range(ATT_H):
                    turn(k, "mPT", i, mP[:, i, :])
                pe.wait_ge(*k.free("mO"))
                pe.wait_ge(*k.emptied("win", 10))
                pe.wait_ge(*k.emptied("win", 11))
                for i in range(ATT_H):
                    pe.wait_ge(*k.emptied("mPT", i))
                    b = k.bank("mO")
                    m = three_blocks(b[:, i * HD:(i + 1) * HD], b[:, T + i * HD:T + (i + 1) * HD], mPT[:, i, :],
                                     vt[:, 0, i * HD:(i + 1) * HD], vt[:, 1, i * HD:(i + 1) * HD])
                m.then_inc(k.fill_sem("mO"), 1)
                pe.wait_ge(S("sexp"), l + 1)
                for i in range(ATT_H):
                    turn(k, "sPT", i, sP[:, i, :])
                pe.wait_ge(*k.free("sO"))
                for i in range(ATT_H):
                    pe.wait_ge(*k.emptied("sPT", i))
                    b = k.bank("sO")
                    c = 256 + (i // 2) * HD
                    m = three_blocks(b[:, i * HD:(i + 1) * HD], b[:, T + i * HD:T + (i + 1) * HD], sPT[:, i, :],
                                     vt[:, 0, c:c + HD], vt[:, 1, c:c + HD])
                m.then_inc(k.fill_sem("sO"), 1)

                def seg(i):
                    name, j = ("seg01", i) if i < 2 else ("seg", i - 2)
                    pe.wait_ge(S("seg_in"), l * SSD_H + (i + 1))
                    pe.wait_ge(*k.free(name, j))
                    b = k.bank(name, j)
                    mm(b[:, 0:T], Aseg[:, i % 2, 0:P], tri_ones, start=True, stop=False, skip_group_check=True)
                    mm(b[:, P:T], Aseg[:, i % 2, 2 * P:3 * P], tri, start=False, stop=True, skip_group_check=True)
                    mm(b[:, T:3 * P], Aseg[:, i % 2, P:2 * P], tri, start=True, stop=True, skip_group_check=True)\
                        .then_inc(k.fill_sem(name, j), 1)

                def ssd_y(i):
                    pe.wait_ge(S("m_ssd"), l * SSD_H + (i + 1))
                    c = slice(i * HD, (i + 1) * HD)
                    three_blocks(k.bank("y", 0)[:, c], k.bank("y", 1)[:, c], Mssd[:, i % 4, :],
                                 xdt[:, 0, c], xdt[:, 1, c]).then_inc(S("y_head"), 1)

                seg(0)
                seg(1)
                pe.wait_ge(*k.free("y", 0))
                pe.wait_ge(*k.free("y", 1))
                for i in range(SSD_H):
                    ssd_y(i)
                    if i + 2 < SSD_H:
                        seg(i + 2)
                pe.drain().then_inc(k.fill_sem("y", 0), 1)
                pe.drain().then_inc(k.fill_sem("y", 1), 1)
                pe.wait_ge(S("ycat"), l + 1)
                transposes(k, "yT", h)
                for i in range(4):
                    pe.wait_ge(*k.emptied("yT", i))
                by_token(k, "wout", 0, 0)
                by_token(k, "wout", 1, 2)
                pe.wait_ge(S("h2"), l + 1)
                transposes(k, "h2T", h)
                for i in range(4):
                    pe.wait_ge(*k.emptied("h2T", i))
                for i in range(4):
                    by_feature(k, "wq", i, 2 * i)
                for i in range(8):
                    pe.wait_ge(*k.emptied("wq", i))
                for i in range(8):
                    t, hp = i // 4, i % 4
                    pe.wait_ge(*k.free("s", i))
                    for j in range(4):
                        c = 4 * hp + j
                        key = colp[:, K1["k1" if j % 2 == 0 else "k2"]:][:, 0:P]
                        m = mm(k.bank("s", i)[:, j * P:(j + 1) * P], qT[:, c, t * P:(t + 1) * P], key,
                               start=True, stop=True, skip_group_check=True)
                    m.then_inc(k.fill_sem("s", i), 1)
                pe.wait_ge(S("chosen"), l + 1)
                for i in range(2):
                    pe.wait_ge(*k.free("eT", i))
                    for j in range(4 - 2 * i):
                        m = nc.tensor.transpose(k.bank("eT", i)[:, j * P:(j + 1) * P],
                                                E3[:, 2 * i + j // 2, (j % 2) * P:(j % 2 + 1) * P], ident)
                    m.then_inc(k.fill_sem("eT", i), 1)
                for hf in range(2):
                    with pe.Fori(0, 8) as it:
                        for b in range(4):
                            pe.wait_ge(S("hotA"), l * 64 + it * 4 + (32 * hf + b + 1))
                            pe.wait_ge(S("hotB"), l * 64 + it * 4 + (32 * hf + b + 1))
                            pe.wait_ge(*k.free(f"G{hf}", b, it))
                            for t in range(8):
                                m = mm(k.bank(f"G{hf}", b)[:, t * HALF:(t + 1) * HALF], hotA[:, b % 2, t, :],
                                       hotB[:, b % 2, t, :], start=True, stop=True, skip_group_check=True)
                            m.then_inc(k.fill_sem(f"G{hf}", b), 1)
                    if hf == 0:
                        for i in range(4):
                            pe.wait_ge(*k.free("acc", i))
                            mm(k.bank("acc", i), zeros, cst[:, 0:NBLK], start=True, stop=False,
                               skip_group_check=True)
                    if hf == 0:
                        pe.wait_ge(S("hT_lo"), l + 1)
                        pe.sem_inc(S("held"), 1)
                    with pe.Fori(0, TURNS) as it:
                        x_ = experts(l, hf, it)
                        for u in range(2):
                            pe.wait_ge(*x_.parted(u))
                            pe.wait_ge(*k.free(f"U{hf}", u, it))
                            for e in range(2):
                                for p_, (w, src) in enumerate(((upper, hT_up), (upper, hT_lo), (lower, hT_up))):
                                    w = w[:, u, :].rearrange("p (c n) -> p c n", c=KC)
                                    for c in range(KC):
                                        m = mm(k.bank(f"U{hf}", u)[:, e * T:(e + 1) * T],
                                               w[:, c, e * P:(e + 1) * P], src[:, c, :],
                                               start=(p_ == 0 and c == 0), stop=(p_ == 2 and c == KC - 1),
                                               skip_group_check=True)
                            m.then_inc(k.fill_sem(f"U{hf}", u), 1)
                            pe.drain().then_inc(x_.used_sem(u), 1)
                        for u in range(2):
                            pe.wait_ge(*x_.parted(2 + u))
                            pe.wait_ge(S("gated"), l * 64 + it * 2 + (32 * hf + u + 1))
                            for w, src in ((upper, hid_up), (upper, hid_lo), (lower, hid_up)):
                                w = w[:, u, :].rearrange("p (c n) -> p c n", c=2)
                                for c in range(2):
                                    for t in range(TT):
                                        for dh in range(2):
                                            m = mm(k.bank("acc", 2 * t + dh), src[:, u, c, t * P:(t + 1) * P],
                                                   w[:, c, dh * NBLK:(dh + 1) * NBLK], start=False, stop=False,
                                                   skip_group_check=True)
                            m.then_inc(x_.used_sem(2 + u), 1)
                for i in range(4):
                    mm(k.bank("acc", i)[:, 0:2], zeros, cst[:, 0:2], start=False, stop=True,
                       skip_group_check=True).then_inc(k.fill_sem("acc", i), 1)

            pe.wait_ge(S("memn"), 1)
            transposes(at(mid, 0), "mT", h)

            with pe.Fori(0, DEPTH) as l:
                k = at(second, l)

                def ffn(f, n):
                    pe.wait_ge(S("pre2"), l * 4 + (n + 1))
                    transposes(k, f + "T", h)
                    for i in range(4):
                        pe.wait_ge(*k.emptied(f + "T", i))
                    for i in range(6):
                        ch = 4 if i < 5 else 2
                        by_feature(k, f + "gu", 2 * i, 4 * i, ch)
                        by_feature(k, f + "gu", 2 * i + 1, 4 * i + ch // 2, ch)
                    for i in range(14, 22):
                        pe.wait_ge(*k.emptied(f + "gu", i))
                    for nb in range(2):
                        for t in range(TT):
                            pe.wait_ge(*k.free(f + "d", 2 * nb + t))
                        for kg in range(3):
                            pe.wait_ge(*k.landed(f + "d", 3 * nb + kg))
                            w = k.tile(f + "d", 3 * nb + kg).rearrange("p (c n) -> p c n", c=KC)
                            for t in range(TT):
                                for c in range(min(KC, FC - kg * KC)):
                                    cc = kg * KC + c
                                    m = mm(k.bank(f + "d", 2 * nb + t), hidT[:, cc, t * P:(t + 1) * P], w[:, c, :],
                                           start=(cc == 0), stop=(cc == FC - 1))
                                if kg == 2:
                                    m.then_inc(k.fill_sem(f + "d", 2 * nb + t), 1)
                            pe.drain().then_inc(k.used_sem(f + "d", 3 * nb + kg), 1)

                ffn("f1", 0)
                pe.wait_ge(S("pre2"), l * 4 + 2)
                transposes(k, "nT", h)
                for i in range(4):
                    pe.wait_ge(*k.emptied("nT", i))
                for i in range(5):
                    by_feature(k, "nin", i, 2 * i)
                by_token(k, "nin", 5, 10)
                by_token(k, "nin", 6, 12)
                by_token(k, "nin", 7, 14, cols=280)
                pe.wait_ge(S("zp"), l + 1)
                pe.wait_ge(*k.free("hid"))
                for s in range(2):
                    pe.wait_ge(*k.landed("cw1", s))
                    w = k.tile("cw1", s).rearrange("p (j n) -> p j n", j=JP)
                    for j in range(JP):
                        m = mm(k.bank("hid")[0:30, s * T:(s + 1) * T], Zp[:, s, j, :], w[:, j, :],
                               start=(j == 0), stop=(j == JP - 1), skip_group_check=True)
                    if s == 1:
                        m.then_inc(k.fill_sem("hid"), 1)
                    pe.drain().then_inc(k.used_sem("cw1", s), 1)
                pe.wait_ge(*k.free("hidT"))
                pe.wait_ge(*k.emptied("hid"))
                pe.sem_inc(S("held"), 1)
                for j in range(4):
                    m = nc.tensor.transpose(k.bank("hidT")[:, j * 30:(j + 1) * 30], hidc[0:30, j * P:(j + 1) * P],
                                            ident[0:30, 0:30])
                m.then_inc(k.fill_sem("hidT"), 1)
                pe.wait_ge(*k.free("kc"))
                pe.wait_ge(*k.emptied("hidT"))
                w2 = colp[:, K2["w2"]:K2["end"]].rearrange("p (s k d) -> p s k d", s=2, k=2)
                b = k.bank("kc")
                for half in range(2):
                    for c in range(2):
                        mm(b[half * HD:(half + 1) * HD, 0:30], w2[:, 0, c, :], hidcT[:, c * 30:(c + 1) * 30],
                           start=(c == 0), stop=(c == 1), skip_group_check=True)
                for g_ in range(2):
                    for c in range(2):
                        m = mm(b[:, P + g_ * HD:P + (g_ + 1) * HD], hidrep[:, c, g_, :], w2[:, 1, c, :],
                               start=(c == 0), stop=(c == 1), skip_group_check=True)
                m.then_inc(k.fill_sem("kc"), 1)
                pe.wait_ge(*k.free("cS"))
                pe.wait_ge(*k.emptied("kc"))
                for odd in range(2):
                    if odd:
                        pe.drain()
                    for t, i in ((t, i) for t in range(TT) for i in range(odd, NSA_H, 2)):
                        q0 = HD * (i % 2)
                        c = (t * NSA_H + i) * NCMP
                        g_ = i // 4
                        m = mm(k.bank("cS")[:, c:c + NCMP], qn[q0:q0 + HD, i // 2, t * P:(t + 1) * P],
                               kcT[q0:q0 + HD, g_ * NCMP:(g_ + 1) * NCMP], start=True, stop=True,
                               skip_group_check=True)
                m.then_inc(k.fill_sem("cS"), 1)
                for i in range(8, 16):
                    pe.wait_ge(*k.emptied("nin", i))

                def all_scores(name, c0):
                    for i in range(NSA_H):
                        q0 = HD * (i % 2)
                        scores(k, name, i, qn[q0:q0 + HD, i // 2, :], kk[q0:q0 + HD, c0 + i // 4, :])

                def all_values(name, exp_signal, c0):
                    pe.wait_ge(S(exp_signal), l + 1)
                    for i in range(NSA_H):
                        turn(k, name + "PT", i, sA[:, i, :])
                    pe.wait_ge(*k.free(name + "O", 0))
                    pe.wait_ge(*k.free(name + "O", 1))
                    for i in range(NSA_H):
                        pe.wait_ge(*k.emptied(name + "PT", i))
                        c = c0 + (i // 4) * HD
                        m = three_blocks(k.bank(name + "O", 0)[:, i * HD:(i + 1) * HD],
                                         k.bank(name + "O", 1)[:, i * HD:(i + 1) * HD], PT[:, i, :],
                                         vt2[:, 0, c:c + HD], vt2[:, 1, c:c + HD])
                    pe.drain().then_inc(k.fill_sem(name + "O", 0), 1)
                    pe.drain().then_inc(k.fill_sem(name + "O", 1), 1)

                all_scores("wS", 2)
                pe.wait_ge(S("cprob"), l + 1)
                pe.wait_ge(*k.free("cPT"))
                for j in range(4):
                    m = nc.tensor.transpose(k.bank("cPT")[:, j * P:(j + 1) * P], cPad[:, j * P:(j + 1) * P], ident)
                m.then_inc(k.fill_sem("cPT"), 1)
                pe.wait_ge(*k.emptied("cPT"))
                for t in range(TT):
                    pe.wait_ge(*k.free("cO", t))
                    for g_ in range(2):
                        m = mm(k.bank("cO", t)[:, g_ * T:(g_ + 1) * T], cPT[:, (2 * t + g_) * P:(2 * t + g_ + 1) * P],
                               vcbd[:, g_, :, :].rearrange("p r d -> p (r d)"), start=True, stop=True,
                               skip_group_check=True)
                    m.then_inc(k.fill_sem("cO", t), 1)
                all_values("w", "wexp", 2 * HD)
                all_scores("lS", 0)
                for i in range(RH):
                    pe.wait_ge(*k.free("rS", i))
                    b = k.bank("rS", i)
                    mm(b[:, 0:T], kr[:, i, 0:P], qr[:, i, :], start=True, stop=True, skip_group_check=True)
                    mm(b[:, T:3 * P], kr[:, i, P:T], qr[:, i, P:T], start=True, stop=True, skip_group_check=True)\
                        .then_inc(k.fill_sem("rS", i), 1)
                all_values("l", "lexp", 0)
                pe.wait_ge(*k.free("rO", 0))
                pe.wait_ge(*k.free("rO", 1))
                for i in range(RH):
                    pe.wait_ge(*k.emptied("rS", i))
                    c = slice(i * P, (i + 1) * P)
                    three_blocks(k.bank("rO", 0)[:, c], k.bank("rO", 1)[:, c], rS[:, i, :], vr[:, 0, c], vr[:, 1, c])
                pe.drain().then_inc(k.fill_sem("rO", 0), 1)
                pe.drain().then_inc(k.fill_sem("rO", 1), 1)
                pe.wait_ge(S("ocat"), l + 1)
                transposes(k, "oT", h)
                for i in range(4):
                    pe.wait_ge(*k.emptied("oT", i))
                by_token(k, "nout", 0, 0)
                by_token(k, "nout", 1, 2)
                pe.wait_ge(S("pre2"), l * 4 + 3)
                transposes(k, "xT", h)
                pe.wait_ge(S("memT"), l + 1)
                for i in range(2):
                    by_feature(k, "xk", i, 2 * i, src=memT)
                for i in range(2):
                    by_token(k, "xv", i, 2 * i, src=memT)
                for i in range(4):
                    pe.wait_ge(*k.emptied("xT", i))
                for i in range(2):
                    by_feature(k, "xq", i, 2 * i)
                for i in range(4):
                    pe.wait_ge(*k.emptied("xk", i))
                    pe.wait_ge(*k.emptied("xv", i))
                for i in range(XH):
                    pe.wait_ge(*k.emptied("xq", i))
                    pe.wait_ge(*k.free("xS", i))
                    for t in range(TT):
                        for c in range(2):
                            m = mm(k.bank("xS", i)[:, t * T:(t + 1) * T], qx[:, 2 * i + c, t * P:(t + 1) * P],
                                   kx[:, 2 * i + c, :], start=(c == 0), stop=(c == 1), skip_group_check=True)
                    m.then_inc(k.fill_sem("xS", i), 1)
                for i in range(XH):
                    pe.wait_ge(S("xprob"), l * XH + (i + 1))
                    pe.wait_ge(*k.free("xPT", i))
                    for j in range(4):
                        m = nc.tensor.transpose(k.bank("xPT", i)[:, j * P:(j + 1) * P],
                                                Px[:, i, (j % 2) * T + (j // 2) * P:][:, 0:P], ident)
                    m.then_inc(k.fill_sem("xPT", i), 1)
                for i in range(XH):
                    pe.wait_ge(*k.emptied("xPT", i))
                    pe.wait_ge(*k.free("xO", i))
                    for e in range(2):
                        for c in range(2):
                            v0 = i * 2 * P + e * P
                            m = mm(k.bank("xO", i)[:, e * T:(e + 1) * T], vx[:, c, v0:v0 + P],
                                   PTx[:, i, c * T:(c + 1) * T], start=(c == 0), stop=(c == 1),
                                   skip_group_check=True)
                    m.then_inc(k.fill_sem("xO", i), 1)
                for i in range(XH):
                    pe.wait_ge(*k.emptied("xO", i))
                by_token(k, "xo", 0, 0)
                by_token(k, "xo", 1, 2)
                ffn("f2", 3)

        @block.scalar
        def _(act):
            f = nc.scalar.activation

            def root(tag, value):
                act.wait_ge(S(tag + "_inv_var"), value)
                f(RS, RR, ACT.Sqrt).then_inc(S(tag + "_rstd"), 1)

            def take(k, name, i, dst, func=ACT.Copy, src=None, **kw):
                act.wait_ge(*k.filled(name, i))
                f(dst, k.bank(name, i) if src is None else src, func, **kw).then_inc(k.empty_sem(name, i), 1)

            def softmax_exp(buf, heads, neg, total, ready, value, done):
                act.wait_ge(S(ready), value)
                for i in range(heads):
                    for t in range(TT):
                        s = buf[:, i, 0:P] if t == 0 else buf[:, i, P:3 * P]
                        j = t * heads + i
                        m = f(s, s, ACT.Exp, bias=st[:, neg + j:neg + j + 1], accum_out=st[:, total + j:total + j + 1])
                m.then_inc(S(done), 1)

            act.dma_start(cst[:, :], a["const1"]).then_inc(S("const_in"), 16)
            act.dma_start(craw, a["c"]).then_inc(S("c_in"), 16)
            act.dma_start(x[:, :, :], a["x"][0].rearrange("(a p) n -> p a n", a=TT)).then_inc(S("x_in"), 16)
            act.wait_ge(S("c_in"), 16)
            f(cT, craw, ACT.Silu).then_inc(S("cond"), 1)
            with act.Fori(0, DEPTH) as l:
                k = at(first, l)
                act.wait_ge(S("first_done"), l + 1)
                act.dma_start(rowp[:, :], a["row1"][bass.ds(l, 1), :].broadcast_to([P, R1["end"]]))\
                    .then_inc(S("par1_in"), 16)
                act.dma_start(colp[:, 0:K1["end"]], a["col1"][bass.ds(l, 1)].rearrange("o p n -> p (o n)"))\
                    .then_inc(S("par1_in"), 16)
                act.wait_ge(S("mod_zero"), l + 1)
                act.dma_start(mod[0:1, :], a["ada_b"][bass.ds(l, 1), :]).then_inc(S("mod_bias"), 16)
                for i in range(12):
                    take(k, "ada", i, mod[:, i * NBLK:(i + 1) * NBLK])
                act.wait_ge(S("par1_in"), l * 32 + 32)
                f(stat(168, 8), rowp[:, R1["alog"]:R1["alog"] + 8], ACT.Exp).then_inc(S("exp_a"), 1)
                root("one", l * 3 + 1)
                for i in (1, 3):
                    take(k, "hT", i, hT[:, 2 * i:2 * i + 2, :])
                for t in range(TT):
                    take(k, "win", t, zs[:, t, :], ACT.Silu)
                act.wait_ge(S("xpad0"), l + 1)
                for i in range(4):
                    take(k, "win", 2 + i, xpad[:, 2 * i:2 * i + 2, 3:259])
                act.wait_ge(S("conv"), l + 1)
                f(conv[:, :, :], conv[:, :, :], ACT.Silu).then_inc(S("conv_silu"), 1)
                act.wait_ge(S("sp_abs"), l + 1)
                f(stat(72, 16), stat(56, 16), ACT.Exp, scale=-1.0).then_inc(S("sp_exp"), 1)
                act.wait_ge(S("sp_one"), l + 1)
                f(stat(120, 16), stat(88, 16), ACT.Ln).then_inc(S("sp_log"), 1)
                softmax_exp(mP, ATT_H, 184, 192, "mmax", l + 1, "mexp")
                softmax_exp(sP, ATT_H, 208, 216, "smax", l + 1, "sexp")
                f(stat(224, 8), stat(224, 8), ACT.Exp).then_inc(S("sink_exp"), 1)
                for i in range(ATT_H):
                    take(k, "mPT", i, mPT[:, i, :], src=k.bank("mPT", i)[:, 0:384])
                for i in range(ATT_H):
                    take(k, "sPT", i, sPT[:, i, :], src=k.bank("sPT", i)[:, 0:384])
                for i in range(SSD_H):
                    name, j = ("seg01", i) if i < 2 else ("seg", i - 2)
                    if i >= 2:
                        act.wait_ge(S("m_ssd"), l * SSD_H + (i - 1))
                    take(k, name, j, Ldec[:, i % 2, :], ACT.Exp, src=k.bank(name, j)[:, 0:384])
                root("one", l * 3 + 2)
                for i in (1, 3):
                    take(k, "yT", i, hT[:, 2 * i:2 * i + 2, :])
                root("one", l * 3 + 3)
                for i in (1, 3):
                    take(k, "h2T", i, hT[:, 2 * i:2 * i + 2, :])
                for i in range(1, 8, 2):
                    take(k, "wq", i, qT[:, 2 * i:2 * i + 2, :])
                for i in range(1, 8, 2):
                    take(k, "s", i, sc[:, 4 * i:4 * i + 4, :])
                for i in range(4):
                    act.wait_ge(*k.emptied("h2T", i))
                f(hT_up[:, :, :], hT[:, :, :], ACT.Copy).then_inc(S("hT_up"), 1)
                act.wait_ge(S("gmax"), l + 1)
                f(gate, gate, ACT.Exp).then_inc(S("gexp"), 1)
                for hf in range(2):
                    if hf == 0:
                        act.wait_ge(*k.slot_over(2))
                        act.wait_ge(*k.slot_over(3))
                    else:
                        act.wait_ge(S("gated"), l * 64 + 32)
                    with act.Fori(0, 8) as it:
                        for b in range(4):
                            act.wait_ge(*k.filled(f"G{hf}", b, it))
                            f(G[:, bass.ds(it * 32 + 8 * b, 8), :], k.bank(f"G{hf}", b), ACT.Copy)\
                                .then_inc(k.empty_sem(f"G{hf}", b), 1)
                    with act.Fori(0, TURNS) as it:
                        e = experts(l, hf, it)
                        for r in range(4):
                            act.wait_ge(*e.landed(r))
                            act.wait_ge(*e.split_free(r))
                            f(upper[:, r % 2, :], raw[:, r, :], ACT.Copy).then_inc(upper_ready, 1)
                            if r >= 2:
                                u = r - 2
                                act.wait_ge(*k.filled(f"U{hf}", u, it))
                                f(gact[:, u, :, :], k.bank(f"U{hf}", u), ACT.Gelu).then_inc(k.empty_sem(f"U{hf}", u), 1)
            act.wait_ge(S("first_done"), DEPTH + 1)
            act.dma_start(h[:, :, :], a["mem"][0].rearrange("(a p) n -> p a n", a=TT)).then_inc(S("mem_in"), 16)
            act.dma_start(mod[:, 0:D], a["final_g"].rearrange("(o n) -> o n", o=1).broadcast_to([P, D]))\
                .then_inc(S("fin_in"), 16)
            act.dma_start(rowp[:, 0:3072], a["const2"][:, 0:3072]).then_inc(S("const2_in"), 16)
            act.dma_start(work[:, 14832:14832 + 1536], a["const2"][:, C2["ret"]:C2["end"]])\
                .then_inc(S("const2_in"), 16)
            act.dma_start(mod[:, R2["end"]:R2["end"] + 484], a["const2"][:, C2["cbias"]:C2["ret"]])\
                .then_inc(S("const2_in"), 16)
            root("mid", 1)
            root("mid", 2)
            k = at(mid, 0)
            for i in (1, 3):
                take(k, "mT", i, memnT[:, 2 * i:2 * i + 2, :])

            with act.Fori(0, DEPTH) as l:
                k = at(second, l)
                act.wait_ge(S("second_done"), l + 1)
                act.wait_ge(S("mid_done"), 1)
                act.dma_start(mod[:, 0:R2["end"]], a["row2"][bass.ds(l, 1), :].broadcast_to([P, R2["end"]]))\
                    .then_inc(S("par2_in"), 16)
                act.dma_start(colp[:, 0:K2["end"]], a["col2"][bass.ds(l, 1)].rearrange("o p n -> p (o n)"))\
                    .then_inc(S("par2_in"), 16)

                def ffn(name, r):
                    root("two", l * 10 + r)
                    for i in range(6):
                        ch = 4 if i < 5 else 2
                        for j in range(ch // 2):
                            act.wait_ge(*k.filled(name + "gu", 4 * i + j))
                            if i:
                                act.wait_ge(*k.emptied(name + "gu", 4 * i - 2 + j))
                            f(sgate[:, j, :], k.bank(name + "gu", 4 * i + j), ACT.Silu)\
                                .then_inc(k.empty_sem(name + "gu", 4 * i + j), 1)
                    for i in range(4):
                        take(k, name + "d", i, h[:, i % 2, (i // 2) * NBLK:(i // 2 + 1) * NBLK])
                    root("two", l * 10 + (r + 1))

                ffn("f1", 1)
                root("two", l * 10 + 3)
                for i in range(2):
                    take(k, "nin", i, qn[:, 2 * i:2 * i + 2, :], scale=HD ** -0.5)
                for i in range(4, 10):
                    dst = (kk, qr, kr)[(i - 4) // 2]
                    c = 2 * (i % 2)
                    take(k, "nin", i, dst[:, c:c + 2, :])
                for t in range(TT):
                    take(k, "nin", 12 + t, gr[:, t, :], ACT.Silu)
                for t in range(TT):
                    act.wait_ge(*k.filled("nin", 14 + t))
                    f(stat(152 + 24 * t, 24), k.bank("nin", 14 + t)[:, 256:280], ACT.Sigmoid)
                    f(vt2[:, t, 0:256], k.bank("nin", 14 + t)[:, 0:256], ACT.Copy)\
                        .then_inc(k.empty_sem("nin", 14 + t), 1)
                act.wait_ge(*k.filled("hid"))
                f(hidc[0:30, :], k.bank("hid")[0:30, :], ACT.Silu).then_inc(k.empty_sem("hid"), 1)
                act.wait_ge(S("cmax"), l + 1)
                f(cS[:, :], cS[:, :], ACT.Exp).then_inc(S("cexp"), 1)
                softmax_exp(sA, NSA_H, 40, 56, "wmax", l + 1, "wexp")
                for i in range(NSA_H):
                    take(k, "wPT", i, PT[:, i, :], src=k.bank("wPT", i)[:, 0:384])
                softmax_exp(sA, NSA_H, 88, 104, "lmax", l + 1, "lexp")
                for i in range(NSA_H):
                    if i == 0:
                        act.wait_ge(*k.filled("wO", 1))
                    take(k, "lPT", i, PT[:, i, :], src=k.bank("lPT", i)[:, 0:384])
                root("two", l * 10 + 4)
                root("two", l * 10 + 5)
                for i in (1, 3):
                    take(k, "oT", i, hT[:, 2 * i:2 * i + 2, :])
                for i in range(4):
                    take(k, "nout", i, h[:, i % 2, (i // 2) * NBLK:(i // 2 + 1) * NBLK])
                root("two", l * 10 + 6)
                root("two", l * 10 + 7)
                for i in range(4):
                    take(k, "xk", i, kx[:, 2 * i:2 * i + 2, :])
                for i in range(4):
                    take(k, "xv", i, vx[:, i % 2, (i // 2) * NBLK:(i // 2 + 1) * NBLK])
                for i in range(4):
                    take(k, "xq", i, qx[:, 2 * i:2 * i + 2, :], scale=(2 * P) ** -0.5)
                for i in range(XH):
                    act.wait_ge(S("xmax"), l * XH + (i + 1))
                    for t in range(TT):
                        j = 2 * i + t
                        m = f(Px[:, i, t * T:(t + 1) * T], k.bank("xS", i)[:, t * T:(t + 1) * T], ACT.Exp,
                              bias=st[:, 272 + j:273 + j], accum_out=st[:, 280 + j:281 + j])
                    m.then_inc(k.empty_sem("xS", i), 1)
                for i in range(XH):
                    take(k, "xPT", i, PTx[:, i, :])
                for i in range(4):
                    take(k, "xo", i, h[:, i % 2, (i // 2) * NBLK:(i // 2 + 1) * NBLK])
                root("two", l * 10 + 8)
                ffn("f2", 9)

        @block.vector
        def _(v):
            def mean_squares(parts, n):
                for j, (src, junk) in enumerate(parts):
                    v.tensor_tensor_reduce(out=junk, in0=src, in1=src, scale=1.0 / n[j], scalar=0.0, op0=ALU.mult,
                                           op1=ALU.add, accum_out=SS[:, j:j + 1])

            def rstd(tag, value, eps):
                v.drain()
                v.tensor_scalar(RR, SS, eps, None, ALU.add)
                v.drain()
                v.reciprocal(RR, RR).then_inc(S(tag + "_inv_var"), 1)
                v.wait_ge(S(tag + "_rstd"), value)

            def take(k, name, i, dst, src=None, scale=1.0):
                v.wait_ge(*k.filled(name, i))
                v.tensor_scalar(dst, k.bank(name, i) if src is None else src, scale, None, ALU.mult)\
                    .then_inc(k.empty_sem(name, i), 1)

            def masked_max(k, name, i, bias, buf, heads, top):
                v.wait_ge(*k.filled(name, i))
                v.sem_inc(S("held"), 1)
                for t in range(TT):
                    c = slice(0, P) if t == 0 else slice(P, 3 * P)
                    j = top + t * heads + i
                    m = v.tensor_tensor_reduce(out=buf[:, i, c], in0=k.bank(name, i)[:, c], in1=bias[:, c],
                                               scale=1.0, scalar=LOWEST, op0=ALU.add, op1=ALU.max,
                                               accum_out=st[:, j:j + 1])
                m.then_inc(k.empty_sem(name, i), 1)

            v.wait_ge(S("const_in"), 16)
            v.wait_ge(S("x_in"), 16)
            v.wait_ge(S("cond"), 1)
            v.memset(SS, 1.0)
            v.memset(RS, 1.0)
            v.drain()
            with v.Fori(0, DEPTH) as l:
                k = at(first, l)
                v.drain()
                v.memset(mod[:, :], 0.0).then_inc(S("mod_zero"), 1)
                v.memset(xpad[:, :, 0:3], 0.0).then_inc(S("xpad0"), 1)
                v.wait_ge(S("mod_bias"), l * 16 + 16)
                for i in range(12):
                    v.wait_ge(*k.landed("ada", i))
                    w = k.tile("ada", i).rearrange("p (c n) -> p c n", c=KC)
                    acc = mod[:, i * NBLK:(i + 1) * NBLK]
                    for c in range(KC):
                        if c:
                            v.drain()
                        m = v.scalar_tensor_tensor(out=acc, in0=w[:, c, :], scalar=cT[:, c:c + 1], in1=acc,
                                                   op0=ALU.mult, op1=ALU.add)
                    m.then_inc(S("ada_acc"), 1)
                    v.drain().then_inc(k.used_sem("ada", i), 1)

                def ada_norm(g0, shift, value, signal):
                    mean_squares([(x[:, t, :], h[:, t, :]) for t in range(TT)], [D] * TT)
                    rstd("one", value, EPS1)
                    for t in range(TT):
                        v.scalar_tensor_tensor(out=h[:, t, :], in0=x[:, t, :], scalar=RS[:, t:t + 1],
                                               in1=rowp[:, g0:g0 + D], op0=ALU.mult, op1=ALU.mult)
                    v.drain()
                    for t in range(TT):
                        v.scalar_tensor_tensor(out=h[:, t, :], in0=mod[:, shift + D:shift + 2 * D], scalar=1.0,
                                               in1=h[:, t, :], op0=ALU.add, op1=ALU.mult)
                    v.drain()
                    for t in range(TT):
                        m = v.tensor_tensor(h[:, t, :], h[:, t, :], mod[:, shift:shift + D], ALU.add)
                    m.then_inc(S(signal), 1)

                v.wait_ge(S("par1_in"), l * 32 + 32)
                for i in range(12):
                    v.wait_ge(*k.emptied("ada", i))
                ada_norm(R1["n1"], 0, l * 3 + 1, "h1")
                for i in (0, 2):
                    take(k, "hT", i, hT[:, 2 * i:2 * i + 2, :])
                for i in range(4):
                    v.wait_ge(*k.emptied("win", 2 + i))
                for tap in range(4):
                    if tap:
                        v.drain()
                    for c in range(8):
                        w = colp[:, K1["cw"] + 4 * c + tap:][:, 0:1]
                        if tap == 0:
                            m = v.tensor_scalar(conv[:, c, :], xpad[:, c, 0:T], w,
                                                colp[:, K1["cb"] + c:K1["cb"] + c + 1], ALU.mult, ALU.add)
                        else:
                            m = v.scalar_tensor_tensor(out=conv[:, c, :], in0=xpad[:, c, tap:tap + T], scalar=w,
                                                       in1=conv[:, c, :], op0=ALU.mult, op1=ALU.add)
                m.then_inc(S("conv"), 1)
                take(k, "win", 6, mqk[:, 0:2, :], scale=HD ** -0.5)
                take(k, "win", 7, mqk[:, 2:4, :])
                take(k, "win", 8, sqk[:, 0:2, :], scale=HD ** -0.5)
                take(k, "win", 9, sqk[:, 2:4, :])
                for t in range(TT):
                    take(k, "win", 10 + t, vt[:, t, :], src=k.bank("win", 10 + t)[:, 0:392])
                r, nr, ab, u, y, d_, ln, dt, aa = (stat(24 + 16 * j, 16) for j in range(9))
                eq = nr
                v.drain()
                v.tensor_tensor(halves(24, 8), vt[:, :, 384:392], row(rowp[:, R1["dtb"]:R1["dtb"] + 8], TT), ALU.add)
                v.drain()
                v.tensor_scalar(nr, r, -1.0, None, ALU.mult)
                v.drain()
                v.tensor_tensor(ab, r, nr, ALU.max).then_inc(S("sp_abs"), 1)
                v.wait_ge(S("sp_exp"), l + 1)
                v.tensor_scalar(y, u, 1.0, None, ALU.add).then_inc(S("sp_one"), 1)
                v.drain()
                v.tensor_scalar(eq, y, 1.0, None, ALU.is_equal)
                v.drain()
                v.scalar_tensor_tensor(out=d_, in0=y, scalar=-1.0, in1=eq, op0=ALU.add, op1=ALU.add)
                v.drain()
                v.reciprocal(d_, d_)
                v.wait_ge(S("sp_log"), l + 1)
                v.tensor_tensor(ln, ln, eq, ALU.add)
                v.drain()
                v.tensor_tensor(ln, ln, u, ALU.mult)
                v.drain()
                v.tensor_tensor(ln, ln, d_, ALU.mult)
                v.drain()
                v.scalar_tensor_tensor(out=dt, in0=r, scalar=0.0, in1=ln, op0=ALU.max, op1=ALU.add)
                v.drain()
                v.wait_ge(S("exp_a"), l + 1)
                v.scalar_tensor_tensor(out=halves(152, 8), in0=halves(136, 8), scalar=-1.0,
                                       in1=row(stat(168, 8), TT), op0=ALU.mult, op1=ALU.mult)
                for i in range(ATT_H):
                    masked_max(k, "mS", i, caus, mP, ATT_H, 176)
                v.drain()
                v.tensor_scalar(stat(184, 8), stat(176, 8), -1.0, None, ALU.mult).then_inc(S("mmax"), 1)
                for i in range(ATT_H):
                    masked_max(k, "sS", i, band, sP, ATT_H, 200)
                sink = row(rowp[:, R1["sink"]:R1["sink"] + ATT_H], TT)
                v.drain()
                v.tensor_tensor(halves(200, 4), halves(200, 4), sink, ALU.max)
                v.drain()
                v.tensor_tensor(halves(224, 4), sink, halves(200, 4), ALU.subtract)
                v.tensor_scalar(stat(208, 8), stat(200, 8), -1.0, None, ALU.mult).then_inc(S("smax"), 1)
                for t in range(TT):
                    v.wait_ge(*k.filled("xs", t))
                    v.tensor_tensor(xdt[:, t, :].rearrange("p (h d) -> p h d", d=HD),
                                    k.bank("xs", t).rearrange("p (h d) -> p h d", d=HD),
                                    column(stat(136 + 8 * t, 8), HD), ALU.mult)
                    v.tensor_tensor(xs[:, t, :].rearrange("p (h d) -> p h d", d=HD),
                                    k.bank("xs", t).rearrange("p (h d) -> p h d", d=HD),
                                    column(rowp[:, R1["dsk"]:R1["dsk"] + 8], HD), ALU.mult)\
                        .then_inc(k.empty_sem("xs", t), 1)
                for g_ in range(2):
                    v.wait_ge(*k.filled("cb", g_))
                    v.tensor_tensor(cbm[:, g_, :], k.bank("cb", g_)[:, 0:384], keep, ALU.mult)\
                        .then_inc(k.empty_sem("cb", g_), 1)

                def seg_in(i):
                    if i >= 2:
                        v.wait_ge(*k.filled("seg01" if i < 4 else "seg", i - 2 if i < 4 else i - 4))
                    b = Aseg[:, i % 2, :]
                    v.tensor_scalar(b[:, 0:P], strict, stat(152 + i, 1), None, ALU.mult)
                    v.tensor_scalar(b[:, P:2 * P], strict, stat(160 + i, 1), None, ALU.mult)
                    v.tensor_scalar(b[:, 2 * P:3 * P], ones, stat(160 + i, 1), None, ALU.mult)\
                        .then_inc(S("seg_in"), 1)

                seg_in(0)
                seg_in(1)
                v.wait_ge(S("mexp"), l + 1)
                v.wait_ge(S("sink_exp"), l + 1)
                v.tensor_tensor(stat(216, 8), stat(216, 8), stat(224, 8), ALU.add)
                v.reciprocal(stat(232, 8), stat(192, 8))
                v.drain()
                v.reciprocal(stat(240, 8), stat(216, 8))
                v.drain()
                for name, c0, rc in (("mO", 512, 232), ("sO", 768, 240)):
                    v.wait_ge(*k.filled(name))
                    for t in range(TT):
                        m = v.tensor_tensor(h[:, t, c0:c0 + 256].rearrange("p (h d) -> p h d", d=HD),
                                            k.bank(name)[:, t * T:(t + 1) * T].rearrange("p (h d) -> p h d", d=HD),
                                            column(stat(rc + 4 * t, 4), HD), ALU.mult)
                    m.then_inc(k.empty_sem(name), 1)
                for i in range(SSD_H):
                    v.wait_ge(*k.emptied("seg01" if i < 2 else "seg", i if i < 2 else i - 2))
                    if i >= 4:
                        v.wait_ge(S("y_head"), l * SSD_H + (i - 3))
                    v.tensor_tensor(Mssd[:, i % 4, :], Ldec[:, i % 2, :], cbm[:, i // 4, :], ALU.mult)\
                        .then_inc(S("m_ssd"), 1)
                    if i + 2 < SSD_H:
                        seg_in(i + 2)
                for t in range(TT):
                    v.wait_ge(*k.filled("y", t))
                    v.tensor_tensor(h[:, t, 0:SSD_W], k.bank("y", t), xs[:, t, :], ALU.add)\
                        .then_inc(k.empty_sem("y", t), 1)
                v.drain()
                for t in range(TT):
                    v.tensor_tensor(h[:, t, 0:SSD_W], h[:, t, 0:SSD_W], zs[:, t, :], ALU.mult)
                v.drain()
                parts = [(t, c0, n, g0) for c0, n, g0 in ((0, SSD_W, R1["ssd"]), (512, 256, R1["moba"]),
                                                          (768, 256, R1["swa"])) for t in range(TT)]
                mean_squares([(h[:, t, c0:c0 + n], tmpA[:, t, 0:n]) for t, c0, n, _ in parts[0:2]], [SSD_W] * 2)
                v.drain()
                for j, (t, c0, n, _) in enumerate(parts[2:]):
                    v.tensor_tensor_reduce(out=tmpA[:, j // 2, (j % 2) * 256:(j % 2 + 1) * 256],
                                           in0=h[:, t, c0:c0 + n], in1=h[:, t, c0:c0 + n], scale=1.0 / n, scalar=0.0,
                                           op0=ALU.mult, op1=ALU.add, accum_out=SS[:, 2 + j:3 + j])
                rstd("one", l * 3 + 2, EPS1)
                for j, (t, c0, n, g0) in enumerate(parts):
                    m = v.scalar_tensor_tensor(out=h[:, t, c0:c0 + n], in0=h[:, t, c0:c0 + n], scalar=RS[:, j:j + 1],
                                               in1=rowp[:, g0:g0 + n], op0=ALU.mult, op1=ALU.mult)
                m.then_inc(S("ycat"), 1)
                for i in (0, 2):
                    take(k, "yT", i, hT[:, 2 * i:2 * i + 2, :])

                def add_gated(name, gate0, bank_of):
                    for i in range(4):
                        nb, t = bank_of(i)
                        c = slice(nb * NBLK, (nb + 1) * NBLK)
                        v.drain()
                        v.wait_ge(*k.filled(name, i))
                        v.tensor_tensor(tmpA[:, i % 2, :], k.bank(name, i), mod[:, gate0:][:, c], ALU.mult)\
                            .then_inc(k.empty_sem(name, i), 1)
                        v.drain()
                        v.tensor_tensor(x[:, t, c], x[:, t, c], tmpA[:, i % 2, :], ALU.add)
                    v.drain()

                add_gated("wout", 2 * D, lambda i: (i // 2, i % 2))
                ada_norm(R1["n2"], 3 * D, l * 3 + 3, "h2")
                for i in (0, 2):
                    take(k, "h2T", i, hT[:, 2 * i:2 * i + 2, :])
                for i in range(0, 8, 2):
                    take(k, "wq", i, qT[:, 2 * i:2 * i + 2, :])
                for i in range(0, 8, 2):
                    take(k, "s", i, sc[:, 4 * i:4 * i + 4, :])
                for i in range(8):
                    v.wait_ge(*k.emptied("s", i))
                v.sem_inc(S("held"), 1)

                def best_16(groups, s, s_left, val, idx):
                    for g_ in range(groups):
                        v.max(val[:, g_, 0:8], s[:, g_, :])
                    v.drain()
                    for g_ in range(groups):
                        v.max_index(idx[:, g_, 0:8], val[:, g_, 0:8], s[:, g_, :])
                        v.match_replace(s_left[:, g_, :], val[:, g_, 0:8], s[:, g_, :], LOWEST)
                    v.drain()
                    for g_ in range(groups):
                        v.max(val[:, g_, 8:16], s_left[:, g_, :])
                    v.drain()
                    for g_ in range(groups):
                        v.max_index(idx[:, g_, 8:16], val[:, g_, 8:16], s_left[:, g_, :])
                    v.drain()

                best_16(32, sc, sc2, V16, I16u)
                v.tensor_copy(I16[:, :, :], I16u[:, :, :])
                pair = V16.rearrange("p (g e) k -> p g e k", e=2)
                for g_ in range(16):
                    v.tensor_tensor(cand[:, g_, :].rearrange("p (a b) -> p a b", b=PK), column(pair[:, g_, 0, :], PK),
                                    row(pair[:, g_, 1, :], PK), ALU.add)
                v.drain()
                best_16(16, cand, sc_c, Vc, Cu)
                v.tensor_tensor(gate, Vc[:, :, :], Vc[:, :, 0:1].broadcast_to([P, 16, PK]), ALU.subtract)\
                    .then_inc(S("gmax"), 1)
                v.tensor_single_scalar(Cd[:, 0, :], Cu.rearrange("p g k -> p (g k)"), 4, ALU.logical_shift_right)
                v.tensor_single_scalar(Cd[:, 1, :], Cu.rearrange("p g k -> p (g k)"), 15, ALU.bitwise_and)
                v.drain()
                v.tensor_copy(Cf[:, :, :], Cd[:, :, :])
                v.wait_ge(S("gexp"), l + 1)
                v.tensor_reduce(stat(248, 16), gate, AX.X, ALU.add)
                v.drain()
                v.reciprocal(stat(248, 16), stat(248, 16))
                v.drain()
                v.tensor_tensor(gate, gate,
                                column(stat(248, 16), PK), ALU.mult)
                keys = I16.rearrange("p (g e) k -> p g e k", e=2)
                for e in range(2):
                    v.drain()
                    v.tensor_tensor(onehot[:, :, :], column(Cf[:, e, :], PK), row(iota[:, 0:PK], 256), ALU.is_equal)
                    v.drain()
                    for g_ in range(16):
                        o = onehot[:, g_ * PK:(g_ + 1) * PK, :]
                        v.tensor_tensor(o, o, row(keys[:, g_, e, :], PK), ALU.mult)
                    v.drain()
                    m = v.tensor_reduce(E3[:, e, :], onehot[:, :, :], AX.X, ALU.add)
                m.then_inc(S("chosen"), 1)
                take(k, "eT", 0, ET[:, 0:2, :])
                take(k, "eT", 1, ET[:, 2, :], src=k.bank("eT", 1)[:, 0:T])
                v.drain()
                for hf in range(2):
                    if hf == 1:
                        for r in range(2):
                            v.wait_ge(*experts(l, 1, 0).split_free(r))
                        v.sem_inc(S("held"), 1)
                    with v.Fori(0, 8) as it:
                        for b in range(4):
                            v.wait_ge(*two_groups_before(k, hf, b, it))
                            t8 = bass.ds(it * 32 + 8 * b, 8)
                            v.tensor_tensor(hotB[:, b % 2, :, :], row(iota[:, hf * HALF:(hf + 1) * HALF], 8),
                                            column(ET[:, 1, t8], HALF), ALU.is_equal).then_inc(S("marked"), 1)
                            v.tensor_tensor(hotA[:, b % 2, :, :], row(iota, 8), column(ET[:, 0, t8], P), ALU.is_equal)\
                                .then_inc(S("hotA"), 1)
                    with v.Fori(0, TURNS) as it:
                        e = experts(l, hf, it)
                        for r in range(4):
                            v.wait_ge(*e.upper(r))
                            lower_part(v, r, slice(0, EXPERTS // 2))
                            if r >= 2:
                                u = r - 2
                                v.wait_ge(*k.emptied(f"U{hf}", u, it))
                                gates = G[:, :, bass.ds(it * 4 + 2 * u, 2)].rearrange("p t i -> p i t")
                                v.tensor_tensor(hid_up[:, u, :, :], gact[:, u, :, :], gates, ALU.mult)
                                v.tensor_tensor(gact[:, u, :, :], gact[:, u, :, :], gates, ALU.mult)
                                v.drain()
                                v.tensor_tensor(hid_lo[:, u, :, :], gact[:, u, :, :],
                                                hid_up[:, u, :, :].bitcast(F32), ALU.subtract)\
                                    .then_inc(S("gated"), 1)
                add_gated("acc", 5 * D, lambda i: (i % 2, i // 2))
                v.drain().then_inc(S("first_done"), 1)

            v.wait_ge(S("fin_in"), 16)
            v.wait_ge(S("mem_in"), 16)
            mean_squares([(x[:, t, :], scr[:, 2048 + t * D:2048 + (t + 1) * D]) for t in range(TT)], [D] * TT)
            rstd("mid", 1, EPS1)
            for t in range(TT):
                v.scalar_tensor_tensor(out=x[:, t, :], in0=x[:, t, :], scalar=RS[:, t:t + 1], in1=mod[:, 0:D],
                                       op0=ALU.mult, op1=ALU.mult)
            v.drain()
            mean_squares([(h[:, t, :], scr[:, 2048 + t * D:2048 + (t + 1) * D]) for t in range(TT)], [D] * TT)
            rstd("mid", 2, EPS2)
            for t in range(TT):
                m = v.tensor_scalar(h[:, t, :], h[:, t, :], RS[:, t:t + 1], None, ALU.mult)
            m.then_inc(S("memn"), 1)
            k = at(mid, 0)
            for i in (0, 2):
                take(k, "mT", i, memnT[:, 2 * i:2 * i + 2, :])
            for i in (1, 3):
                v.wait_ge(*k.emptied("mT", i))
            v.wait_ge(S("const2_in"), 48)
            v.memset(cPad[:, :], 0.0)
            v.memset(hidrep.rearrange("p k g n -> p (k g n)"), 0.0)
            v.drain().then_inc(S("mid_done"), 1)

            with v.Fori(0, DEPTH) as l:
                k = at(second, l)

                def pre_norm(value, n):
                    mean_squares([(x[:, t, :], h[:, t, :]) for t in range(TT)], [D] * TT)
                    rstd("two", value, EPS2)
                    for t in range(TT):
                        m = v.tensor_scalar(h[:, t, :], x[:, t, :], RS[:, t:t + 1], None, ALU.mult)
                    m.then_inc(S("pre2"), 1)

                def gains(name, g0):
                    for i in range(4):
                        v.wait_ge(*k.filled(name, i))
                        for e in range(2):
                            c = 2 * i + e
                            m = v.tensor_scalar(hT[:, c, :], k.bank(name, i)[:, e * T:(e + 1) * T],
                                                colp[:, g0 + c:g0 + c + 1], None, ALU.mult)
                        m.then_inc(k.empty_sem(name, i), 1)

                def post_norm(name, value, g0, factor):
                    for i in range(4):
                        v.wait_ge(*k.emptied(name, i))
                    mean_squares([(h[:, t, :], scr[:, 2048 + t * D:2048 + (t + 1) * D]) for t in range(TT)], [D] * TT)
                    rstd("two", value, EPS2)
                    for t in range(TT):
                        v.scalar_tensor_tensor(out=h[:, t, :], in0=h[:, t, :], scalar=RS[:, t:t + 1],
                                               in1=mod[:, g0:g0 + D], op0=ALU.mult, op1=ALU.mult)
                    v.drain()
                    for t in range(TT):
                        v.scalar_tensor_tensor(out=x[:, t, :], in0=h[:, t, :], scalar=factor, in1=x[:, t, :],
                                               op0=ALU.mult, op1=ALU.add)
                    v.drain()

                def ffn(name, n, r):
                    pre_norm(l * 10 + r, n)
                    gains(name + "T", K2[name])
                    for i in range(6):
                        ch = 4 if i < 5 else 2
                        for j in range(ch // 2):
                            v.wait_ge(*k.emptied(name + "gu", 4 * i + j))
                            up = 4 * i + ch // 2 + j
                            v.wait_ge(*k.filled(name + "gu", up))
                            c = 4 * i + 2 * j
                            v.tensor_tensor(hidT[:, c:c + 2, :].rearrange("p c t -> p (c t)"), k.bank(name + "gu", up),
                                            sgate[:, j, :], ALU.mult).then_inc(k.empty_sem(name + "gu", up), 1)
                    post_norm(name + "d", l * 10 + (r + 1), R2[name], 0.5)

                v.wait_ge(S("par2_in"), l * 32 + 32)
                ffn("f1", 0, 1)
                pre_norm(l * 10 + 3, 1)
                gains("nT", K2["mix"])
                for s in range(2):
                    i = 2 + s
                    v.wait_ge(*k.filled("nin", i))
                    b = k.bank("nin", i).rearrange("p (g t) -> p g t", g=2)
                    v.tensor_copy(Z[0:HD, 2 * s:2 * s + 2, :], b[0:HD])
                    v.tensor_copy(Z[HD:P, 2 * s:2 * s + 2, 0:T - 1], b[HD:P, :, 1:T]).then_inc(k.empty_sem("nin", i), 1)
                v.drain()
                for s in range(2):
                    for j in range(JP):
                        zj = Z[:, 2 * s:2 * s + 2, 2 * j:2 * j + 16 * (NCMP - 1) + 1:16]
                        pe_ = colp[:, K2["pe"] + s * JP + j:][:, 0:1]
                        m = v.tensor_scalar(Zp[:, s, j, :].rearrange("p (g n) -> p g n", g=2), zj, pe_, None, ALU.add)
                m.then_inc(S("zp"), 1)
                for t in range(TT):
                    take(k, "nin", 10 + t, vr[:, t, :])
                v.wait_ge(*k.filled("hidT"))
                v.tensor_copy(hidcT[:, 0:60], k.bank("hidT")[:, 0:60])
                for c in range(2):
                    for g_ in range(2):
                        src = k.bank("hidT")[:, 60 + c * 30 + g_ * NCMP:][:, 0:NCMP]
                        m = v.tensor_copy(hidrep[:, c, g_, :].rearrange("p (r n) -> p r n", r=4)[:, :, 0:NCMP],
                                          row(src, 4))
                m.then_inc(k.empty_sem("hidT"), 1)
                v.wait_ge(*k.filled("kc"))
                v.tensor_copy(kcT[:, 0:30], k.bank("kc")[:, 0:30])
                for g_ in range(2):
                    for r_ in range(4):
                        m = v.tensor_scalar(vcbd[:, g_, r_, :], k.bank("kc")[:, P + g_ * HD:P + (g_ + 1) * HD],
                                            mod[:, R2["end"] + 480 + r_:][:, 0:1], None, ALU.mult)
                m.then_inc(k.empty_sem("kc"), 1)
                cb3 = mod[:, R2["end"]:R2["end"] + 240]
                cm3 = mod[:, R2["end"] + 240:R2["end"] + 480]
                c3 = cS.rearrange("p (r n) -> p r n", n=NCMP)
                v.wait_ge(*k.filled("cS"))
                v.tensor_tensor(cS, k.bank("cS")[:, 0:240], cb3, ALU.add).then_inc(k.empty_sem("cS"), 1)
                v.drain()
                v.tensor_reduce(stat(120, 16), c3, AX.X, ALU.max)
                v.drain()
                v.tensor_tensor(c3, c3, column(stat(120, 16), NCMP), ALU.subtract).then_inc(S("cmax"), 1)
                v.wait_ge(S("cexp"), l + 1)
                v.tensor_tensor(cS, cS, cm3, ALU.mult)
                v.drain()
                v.tensor_reduce(stat(136, 16), c3, AX.X, ALU.add)
                v.drain()
                v.tensor_scalar(stat(136, 16), stat(136, 16), 1e-30, None, ALU.max)
                v.drain()
                v.reciprocal(stat(136, 16), stat(136, 16))
                v.drain()
                v.tensor_tensor(cPad.rearrange("p (r n) -> p r n", n=32)[:, :, 0:NCMP], c3,
                                column(stat(136, 16), NCMP), ALU.mult).then_inc(S("cprob"), 1)

                def maxima(name, top, signal):
                    for i in range(NSA_H):
                        masked_max(k, name, i, alibi[:, i, :], sA, NSA_H, top)
                    v.drain()
                    v.tensor_scalar(stat(top + 16, 16), stat(top, 16), -1.0, None, ALU.mult).then_inc(S(signal), 1)

                maxima("wS", 24, "wmax")
                v.wait_ge(*k.filled("cPT"))
                v.tensor_copy(cPT[:, :], k.bank("cPT")).then_inc(k.empty_sem("cPT"), 1)
                sig = stat(152, 48).rearrange("p (a e) -> p a e", e=3)
                fac = stat(200, 48).rearrange("p (b a) -> p b a", b=3)
                v.tensor_copy(fac[:, 0, :], sig[:, :, 0])

                def combine(name, br):
                    for t in range(TT):
                        v.wait_ge(*k.filled(name, t))
                        src = k.bank(name, t).rearrange("p (h d) -> p h d", d=HD)
                        fa = column(fac[:, br, t * NSA_H:(t + 1) * NSA_H], HD)
                        if br == 0:
                            dst = onsa[:, t, :].rearrange("p (h d) -> p h d", d=HD)
                            v.tensor_tensor(dst, src, fa, ALU.mult).then_inc(k.empty_sem(name, t), 1)
                        else:
                            v.tensor_tensor(tmpB[:, t, :].rearrange("p (h d) -> p h d", d=HD), src, fa, ALU.mult)\
                                .then_inc(k.empty_sem(name, t), 1)
                            v.drain()
                            v.tensor_tensor(onsa[:, t, :], onsa[:, t, :], tmpB[:, t, :], ALU.add)
                    v.drain()

                v.drain()
                v.wait_ge(*k.filled("cO", 1))
                combine("cO", 0)
                v.wait_ge(S("wexp"), l + 1)
                v.reciprocal(stat(56, 16), stat(56, 16))
                v.drain()
                v.tensor_tensor(fac[:, 2, :], sig[:, :, 2], stat(56, 16), ALU.mult)
                v.drain()
                v.wait_ge(*k.filled("wPT", NSA_H - 1))
                combine("wO", 2)
                maxima("lS", 72, "lmax")
                for i in range(RH):
                    v.wait_ge(*k.filled("rS", i))
                    v.tensor_tensor(rS[:, i, :], k.bank("rS", i)[:, 0:384], retm[:, i, :], ALU.mult)\
                        .then_inc(k.empty_sem("rS", i), 1)
                v.wait_ge(S("lexp"), l + 1)
                v.reciprocal(stat(104, 16), stat(104, 16))
                v.drain()
                v.tensor_tensor(fac[:, 1, :], sig[:, :, 1], stat(104, 16), ALU.mult)
                v.drain()
                combine("lO", 1)
                mean_squares([(onsa[:, t, :], tmpB[:, t, :]) for t in range(TT)], [512] * TT)
                rstd("two", l * 10 + 4, EPS2)
                for t in range(TT):
                    v.scalar_tensor_tensor(out=h[:, t, 0:512], in0=onsa[:, t, :], scalar=RS[:, t:t + 1],
                                           in1=mod[:, R2["nsa"]:R2["nsa"] + 512], op0=ALU.mult, op1=ALU.mult)
                for t in range(TT):
                    v.wait_ge(*k.filled("rO", t))
                    v.tensor_copy(h[:, t, 512:D], k.bank("rO", t)).then_inc(k.empty_sem("rO", t), 1)
                ro = [h[:, t, 512:D].rearrange("p (h d) -> p h d", d=P) for t in range(TT)]
                v.drain()
                for t in range(TT):
                    v.tensor_reduce(stat(248 + 4 * t, 4), ro[t], AX.X, ALU.add)
                v.drain()
                v.tensor_scalar(stat(248, 8), stat(248, 8), 1.0 / P, None, ALU.mult)
                v.drain()
                for t in range(TT):
                    v.tensor_tensor(ro[t], ro[t], column(stat(248 + 4 * t, 4), P), ALU.subtract)
                v.drain()
                for t in range(TT):
                    v.tensor_tensor(tmpB[:, t, :], h[:, t, 512:D], h[:, t, 512:D], ALU.mult)
                v.drain()
                for t in range(TT):
                    v.tensor_reduce(stat(256 + 4 * t, 4), tmpB[:, t, :].rearrange("p (h d) -> p h d", d=P), AX.X,
                                    ALU.add)
                v.drain()
                v.tensor_scalar(SS, stat(256, 8), 1.0 / P, None, ALU.mult)
                rstd("two", l * 10 + 5, EPS2)
                for t in range(TT):
                    v.tensor_tensor(ro[t], ro[t], column(RS[:, 4 * t:4 * t + 4], P), ALU.mult)
                v.drain()
                for t in range(TT):
                    v.tensor_tensor(h[:, t, 512:D], h[:, t, 512:D], mod[:, R2["ret"]:R2["ret"] + 512], ALU.mult)
                v.drain()
                for t in range(TT):
                    v.wait_ge(*k.emptied("nin", 12 + t))
                    m = v.tensor_tensor(h[:, t, 512:D], h[:, t, 512:D], gr[:, t, :], ALU.mult)
                m.then_inc(S("ocat"), 1)
                for i in (0, 2):
                    take(k, "oT", i, hT[:, 2 * i:2 * i + 2, :])
                post_norm("nout", l * 10 + 6, R2["mix"], 1.0)
                pre_norm(l * 10 + 7, 2)
                for c in range(KC):
                    m = v.tensor_scalar(memT[:, c, :], memnT[:, c, :], colp[:, K2["mem"] + c:K2["mem"] + c + 1], None,
                                        ALU.mult)
                m.then_inc(S("memT"), 1)
                gains("xT", K2["xa"])
                for i in range(XH):
                    v.wait_ge(*k.filled("xS", i))
                    v.tensor_reduce(stat(264 + 2 * i, 2), k.bank("xS", i).rearrange("p (t n) -> p t n", t=TT), AX.X,
                                    ALU.max)
                    v.drain()
                    v.tensor_scalar(stat(272 + 2 * i, 2), stat(264 + 2 * i, 2), -1.0, None, ALU.mult)\
                        .then_inc(S("xmax"), 1)
                for i in range(XH):
                    v.wait_ge(*k.emptied("xS", i))
                    v.reciprocal(stat(288 + 2 * i, 2), stat(280 + 2 * i, 2))
                    v.drain()
                    for t in range(TT):
                        p_ = Px[:, i, t * T:(t + 1) * T]
                        m = v.tensor_scalar(p_, p_, stat(288 + 2 * i + t, 1), None, ALU.mult)
                    m.then_inc(S("xprob"), 1)
                for i in range(XH):
                    take(k, "xO", i, hT[:, 2 * i:2 * i + 2, :])
                post_norm("xo", l * 10 + 8, R2["xa"], 1.0)
                ffn("f2", 3, 9)
                v.drain().then_inc(S("second_done"), 1)


def constants_first():
    i = np.arange(P)
    s, t = i[:, None], i[None, :]
    c = np.zeros((P, C_END), np.float32)
    c[:, C_ID:C_STRICT] = s == t
    c[:, C_STRICT:C_KEEP] = s > t
    c[:, C_KEEP:C_CAUS] = np.concatenate([s <= t, s < P + t, s <= t], 1)
    ok = s >= t
    c[:, C_CAUS:C_CAUS + 384] = np.where(np.concatenate([ok, s >= t - P, ok], 1), 0.0, NEG)
    c[:, C_BAND:C_BAND + 384] = np.where(np.concatenate([ok, t > s, ok], 1), 0.0, NEG)
    c[:, C_IOTA:C_END] = t
    return c


def constants_second():
    i = np.arange(P)
    q, key = i[:, None], i[None, :]
    c = np.zeros((P, C2["end"]), np.float32)
    slopes = (2.0 ** (-8.0 * np.arange(1, NSA_H + 1) / NSA_H)).astype(np.float32)
    dist = np.concatenate([q - key, P + q - key, q - key], 1)
    for j in range(NSA_H):
        c[:, 384 * j:384 * (j + 1)] = np.where(dist >= 0, -slopes[j] * dist.astype(np.float32), NEG)
    start = np.arange(NCMP) * 16
    for t in range(TT):
        tok = t * P + i[:, None]
        ok = start[None, :] + 31 <= tok
        away = (tok - (start[None, :] + 15.5)).astype(np.float32)
        for j in range(NSA_H):
            o = (t * NSA_H + j) * NCMP
            c[:, C2["cbias"] + o:C2["cbias"] + o + NCMP] = np.where(ok, -slopes[j] * away, NEG)
            c[:, C2["cmask"] + o:C2["cmask"] + o + NCMP] = ok
    c[:, C2["bmask"]:C2["ret"]] = i[:, None] // 32 == np.arange(4)[None, :]
    log_g = np.log(1.0 - np.exp2(-5.0 - np.arange(RH, dtype=np.float64)))
    away = np.concatenate([key - q, P + key - q, key - q], 1).astype(np.float64)
    for j in range(RH):
        c[:, C2["ret"] + 384 * j:C2["ret"] + 384 * (j + 1)] = np.where(
            away >= 0, np.exp(np.maximum(away, 0) * log_g[j]), 0.0) * float(P) ** -0.5
    return c


def weight_tiles(w, rows=D):
    kk, n = w.shape
    kg, nb = -(-kk // D), -(-n // NBLK)
    full = np.zeros((kg * D, nb * NBLK), w.dtype)
    full[:kk, :n] = w
    return full.reshape(kg, KC, P, nb, NBLK).transpose(3, 0, 2, 1, 4).reshape(nb * kg, P, TILE)


def twice(w, n):
    return np.concatenate([w[:, HD * (j // 2):HD * (j // 2 + 1)] for j in range(2 * n)], 1)


def kernel(**inputs):
    import concourse.bacc as _bacc
    from concourse.bass_utils import run_bass_kernel_spmd as _run

    p = {n: np.asarray(v) for n, v in inputs.items()}
    cat = np.concatenate
    experts, stream1, stream2, row1, col1, row2, col2 = [], [], [], [], [], [], []
    for l in range(DEPTH):
        w = p["w_in"][l]
        z, xbc, dt, mq, mk, mv, sq, sk, sv = np.split(w, np.cumsum([512, 1024, 8, 256, 256, 256, 256, 128]), 1)
        w = cat([z, xbc, mq, mk, sq, twice(sk, 2), mv, sv, dt], 1)
        stream1.append(cat([weight_tiles(p["ada_w"][l]), weight_tiles(w), weight_tiles(p["w_out"][l]),
                            weight_tiles(p["peer_wq"][l])]))
        peer = np.empty((2 * TURNS, 2, 2, P, EXPERTS), np.float32)
        u = p["peer_u"][l].reshape(NKEYS, 2 * TURNS, 2, 2, KC, P)
        peer[:, 0] = u.transpose(1, 2, 5, 4, 3, 0).reshape(2 * TURNS, 2, P, EXPERTS)
        v = p["peer_v"][l].reshape(NKEYS, 2 * TURNS, 2, 2 * D)
        peer[:, 1] = v.transpose(1, 2, 0, 3)
        experts.append(peer.reshape(8 * TURNS, P, EXPERTS))
        row1.append(cat([p[n][l] for n in ("norm1_g", "norm2_g", "ssd_norm_g", "moba_norm_g", "swa_norm_g",
                                           "dt_bias", "a_log", "d_skip", "swa_sinks")]))
        cw = p["conv_w"][l].reshape(4, 8, P).transpose(2, 1, 0).reshape(P, 32)
        cb = p["conv_b"][l].reshape(8, P).T
        col1.append(cat([cw, cb, p["peer_k1"][l].T, p["peer_k2"][l].T], 1))

        gate_up = [weight_tiles(p[f"ffn{f}_w_{s}_2"][l]) for f in (1, 2) for s in ("gate", "up")]
        gu = [np.stack([gate_up[2 * f], gate_up[2 * f + 1]], 1).reshape(12, P, TILE) for f in range(2)]
        w = p["w_in_2"][l]
        q, kc, vc, ks, vs, kw, vw, ga, qr, kr, vr, gr = np.split(w, np.cumsum([512] + [128] * 6 + [24] + [512] * 3), 1)
        w = cat([q, twice(kc, 2), twice(vc, 2), twice(ks, 2), twice(kw, 2), qr, kr, vr, gr, vs, vw, ga], 1)
        cw1 = p["cmp_w1_2"][l].reshape(2, JP, P, 256).transpose(0, 2, 1, 3).reshape(2, P, TILE)
        stream2.append(cat([gu[0], weight_tiles(p["ffn1_w_down_2"][l]), weight_tiles(w), cw1,
                            weight_tiles(p["w_out_2"][l]), weight_tiles(p["xa_wk_2"][l]),
                            weight_tiles(p["xa_wv_2"][l]), weight_tiles(p["xa_wq_2"][l]),
                            weight_tiles(p["xa_wo_2"][l]), gu[1], weight_tiles(p["ffn2_w_down_2"][l])]))
        row2.append(cat([p[n + "_2"][l] for n in ("ffn1_post_g", "mix_post_g", "xa_post_g", "ffn2_post_g",
                                                  "nsa_out_g", "ret_gn_g")]))
        cols = [p[n + "_2"][l].reshape(KC, P).T for n in ("ffn1_pre_g", "mix_pre_g", "xa_pre_g", "xa_mem_g",
                                                          "ffn2_pre_g")]
        pe = p["cmp_pe_2"][l].reshape(2, JP, P).transpose(2, 0, 1).reshape(P, 32)
        w2 = p["cmp_w2_2"][l].reshape(2, 2, P, HD).transpose(2, 0, 1, 3).reshape(P, 256)
        col2.append(cat(cols + [pe, w2], 1))
    arrays = {
        "x": p["x"], "c": p["c"].reshape(KC, P).T, "mem": p["mem_2"], "final_g": p["final_g"], "ada_b": p["ada_b"],
        "experts": np.stack(experts), "stream1": np.stack(stream1), "stream2": np.stack(stream2), "row1": np.stack(row1), "col1": np.stack(col1),
        "row2": np.stack(row2), "col2": np.stack(col2), "const1": constants_first(), "const2": constants_second(),
    }
    arrays = {n: np.ascontiguousarray(v) for n, v in arrays.items()}
    nc = _bacc.Bacc("TRN2", target_bir_lowering=False, num_devices=1, dynamic_dma_scratch_size=1024)
    aps = {n: nc.dram_tensor("in_" + n, v.shape, F32, kind="ExternalInput").ap() for n, v in arrays.items()}
    out = nc.dram_tensor("out", (1, T, D), F32, kind="ExternalOutput").ap()
    two_mixers_and_peer_then_nsa_retention_memory(nc, aps, out)
    r = _run(nc, [{"in_" + n: v for n, v in arrays.items()}], core_ids=[0])
    return r.results[0]["out"]
```

```python
from contextlib import ExitStack

import concourse.bass as bass
import numpy as np
from concourse import mybir

F32 = mybir.dt.float32
F32R = mybir.dt.float32r
U32 = mybir.dt.uint32
ALU = mybir.AluOpType
ACT = mybir.ActivationFunctionType
AX = mybir.AxisListType

P = 128
DEPTH = 2
D = 1024
T = 256
TT = T // P
KC = D // P
NBLK = 512
TILE = KC * NBLK
RING = 4
ADA_DVE = 6
PART = TILE // 2
NEG = -1e30
LOWEST = -3.0e38

HD = 64
SSD_H = 8
SSD_W = SSD_H * HD
ATT_H = 4
PH, PK, NKEYS = 8, 16, 128
HALF = NKEYS // 2
TURNS = HALF // 4
GROUPS = T // 8
EPS1, EPS2 = 1e-5, 1e-6

D_FF = 2816
FC = D_FF // P
NSA_H, NSA_G = 8, 2
NCMP = (T - 32) // 16 + 1
JP = 16
RH = 4
XH = 4

C_ID, C_STRICT, C_KEEP, C_CAUS, C_BAND, C_IOTA, C_END = np.cumsum([0, 128, 128, 384, 256, 384, 128]).tolist()
R1 = dict(zip(["n1", "n2", "ssd", "moba", "swa", "dtb", "alog", "dsk", "sink", "end"],
              np.cumsum([0, D, D, SSD_W, 256, 256, 8, 8, 8, 4]).tolist()))
K1 = dict(zip(["cw", "cb", "k1", "k2", "end"], np.cumsum([0, 32, 8, 128, 128]).tolist()))
R2 = dict(zip(["f1", "mix", "xa", "f2", "nsa", "ret", "end"], np.cumsum([0, D, D, D, D, 512, 512]).tolist()))
K2 = dict(zip(["f1", "mix", "xa", "mem", "f2", "pe", "w2", "end"], np.cumsum([0, 8, 8, 8, 8, 8, 32, 256]).tolist()))
C2 = dict(zip(["alibi", "cbias", "cmask", "bmask", "ret", "end"],
              np.cumsum([0, NSA_H * 384, 240, 240, 4, RH * 384]).tolist()))


class Plan:

    def __init__(self, banks_before, tiles_before):
        self.bank_base = banks_before
        self.tile_base = tiles_before
        self.count = [0] * 8
        self.next = 0
        self.fills = {}
        self.tiles = {}

    def fill(self, name, n, bank=None, times=1):
        for i in range(n):
            b = self.next if bank is None else bank + i
            if bank is None:
                self.next = (b + 1) % 8
            self.fills[name, i] = (b, self.count[b])
            self.count[b] += times

    def tile(self, name, n):
        for i in range(n):
            self.tiles[name, i] = len(self.tiles)


def plan_first():
    p = Plan([0] * 8, 0)
    p.tile("ada", 12)
    p.tile("win", 6)
    p.tile("wout", 2)
    p.tile("wq", 4)
    p.fill("ada", 12)
    p.fill("hT", 4)
    p.fill("win", 12)
    p.fill("mS", ATT_H)
    p.fill("sS", ATT_H)
    p.fill("xs", 2)
    p.fill("cb", 2)
    p.fill("mPT", ATT_H)
    p.fill("mO", 1)
    p.fill("sPT", ATT_H)
    p.fill("sO", 1)
    p.fill("seg01", 2)
    p.fill("y", 2)
    p.fill("seg", 6)
    p.fill("yT", 4)
    p.fill("wout", 4)
    p.fill("h2T", 4)
    p.fill("wq", 8)
    p.fill("s", 8)
    p.fill("eT", 2)
    for hf in range(2):
        p.fill(f"G{hf}", 4, bank=0, times=GROUPS // 2)
        if hf == 0:
            p.fill("acc", 4, bank=4)
        p.fill(f"U{hf}", 2, bank=0, times=TURNS)
    p.per_slot = len(p.tiles) // RING
    assert len(p.tiles) % RING == 0
    return p


def plan_second(first):
    p = Plan([DEPTH * c for c in first.count], 0)
    for f in ("f1", "f2"):
        if f == "f2":
            for name, n in (("nin", 16), ("cw1", 4), ("nout", 4), ("xk", 4), ("xv", 4), ("xq", 4), ("xo", 4)):
                p.tile(name, n)
            p.fill("nT", 4)
            p.fill("nin", 16)
            p.fill("hid", 1)
            p.fill("hidT", 1)
            p.fill("kc", 1)
            p.fill("cS", 1)
            p.fill("wS", NSA_H)
            p.fill("cPT", 1)
            p.fill("cO", 2)
            p.fill("wPT", NSA_H)
            p.fill("wO", 2)
            p.fill("lS", NSA_H)
            p.fill("rS", RH)
            p.fill("lPT", NSA_H)
            p.fill("lO", 2)
            p.fill("rO", 2)
            p.fill("oT", 4)
            p.fill("nout", 4)
            p.fill("xT", 4)
            p.fill("xk", 4)
            p.fill("xv", 4)
            p.fill("xq", 4)
            p.fill("xS", XH)
            p.fill("xPT", XH)
            p.fill("xO", XH)
            p.fill("xo", 4)
        p.tile(f + "gu", FC)
        p.tile(f + "d", 12)
        p.fill(f + "T", 4)
        p.fill(f + "gu", FC)
        p.fill(f + "d", 4)
    assert len(p.tiles) % 4 == 0
    return p




class At:

    def __init__(self, plan, l, banks_filled, banks_emptied, tiles_landed, tiles_used, ps, ring):
        self.plan, self.l = plan, l
        self.bf, self.be, self.tl, self.tu = banks_filled, banks_emptied, tiles_landed, tiles_used
        self.ps, self.ring = ps, ring

    def bank(self, name, i=0):
        return self.ps[:, self.plan.fills[name, i][0], :]

    def _use(self, name, i, it):
        b, n = self.plan.fills[name, i]
        return b, self.l * self.plan.count[b] + it + (self.plan.bank_base[b] + n)

    def free(self, name, i=0, it=0):
        b, n = self._use(name, i, it)
        return self.be[b], n + 1

    def filled(self, name, i=0, it=0):
        b, n = self._use(name, i, it)
        return self.bf[b], n + 1

    def emptied(self, name, i=0, it=0):
        b, n = self._use(name, i, it)
        return self.be[b], n + 2

    def fill_sem(self, name, i=0):
        return self.bf[self.plan.fills[name, i][0]]

    def empty_sem(self, name, i=0):
        return self.be[self.plan.fills[name, i][0]]

    def _tile(self, name, i, it):
        n = self.plan.tiles[name, i]
        return n % RING, self.l * self.plan.per_slot + it + (self.plan.tile_base + n // RING)

    def tile(self, name, i):
        return self.ring[:, self.plan.tiles[name, i] % RING, :]

    def landed(self, name, i):
        s, n = self._tile(name, i, 0)
        return self.tl[s], 16 * n + 16

    def slot_free(self, name, i):
        s, n = self._tile(name, i, 0)
        return self.tu[s], n + 1

    def used_sem(self, name, i):
        return self.tu[self.plan.tiles[name, i] % RING]

    def land_sem(self, name, i):
        return self.tl[self.plan.tiles[name, i] % RING]

    def slot_over(self, slot):
        return self.tu[slot], self.l * self.plan.per_slot + (self.plan.tile_base + self.plan.per_slot + 1)


class Parted:

    def __init__(self, turn, landed, parted, used, upper_ready):
        self.turn = turn
        self._landed, self._parted, self._used, self._upper = landed, parted, used, upper_ready

    def landed(self, r):
        return self._landed[r], 16 * self.turn + 16

    def raw_free(self, r):
        return self._parted[r], 2 * self.turn + 1

    def parted(self, r):
        return self._parted[r], 2 * self.turn + 3

    def split_free(self, r):
        return self._used[r % 2], 2 * self.turn + (r // 2 + 1)

    def used_sem(self, r):
        return self._used[r % 2]

    def upper(self, r):
        return self._upper, 4 * self.turn + (r + 1)


def column(ap, n):
    a = ap.shape[1]
    return ap.rearrange("p (a o) -> p a o", o=1).broadcast_to([ap.shape[0], a, n])


def row(ap, n):
    a = ap.shape[1]
    return ap.rearrange("p (o a) -> p o a", o=1).broadcast_to([ap.shape[0], n, a])


def two_mixers_and_peer_then_nsa_retention_memory(nc, a, out):
    first = plan_first()
    mid = Plan([DEPTH * c for c in first.count], 0)
    mid.fill("mT", 4)
    second = plan_second(first)
    second.bank_base = [b + c for b, c in zip(second.bank_base, mid.count)]

    ctx = ExitStack()
    with ctx:
        def sb(name, n, dt=F32):
            return ctx.enter_context(nc.sbuf_tensor(name, [P, n], dt))

        def sem(name):
            return ctx.enter_context(nc.semaphore(name))

        ring_at = -(-nc.sbuf_base // 32) * 32
        ring = ctx.enter_context(nc.sbuf_tensor("weights", [P, RING, TILE], F32))
        work_at = -(-nc.sbuf_base // 32) * 32
        work = sb("work", 16384)
        scr_at = -(-nc.sbuf_base // 32) * 32
        scr = sb("scr", 6144)
        mod_at = -(-nc.sbuf_base // 32) * 32
        mod = sb("mod", 6 * D)
        x = ctx.enter_context(nc.sbuf_tensor("x_res", [P, TT, D], F32))
        h_at = -(-nc.sbuf_base // 32) * 32
        h = ctx.enter_context(nc.sbuf_tensor("h", [P, TT, D], F32))
        hT_at = -(-nc.sbuf_base // 32) * 32
        hT = ctx.enter_context(nc.sbuf_tensor("hT", [P, KC, T], F32))
        cst = sb("cst", C_END)
        rowp = sb("rowp", R1["end"])
        colp = sb("colp", K2["end"])
        st = sb("stats", 384)
        ps = ctx.enter_context(nc.psum_tensor("ps", [P, 8, NBLK], F32))

        banks_filled = [sem(f"bank{b}_filled") for b in range(8)]
        banks_emptied = [sem(f"bank{b}_emptied") for b in range(8)]
        tiles_landed = [sem(f"slot{s}_landed") for s in range(RING)]
        tiles_used = [sem(f"slot{s}_used") for s in range(RING)]
        raw_landed = [sem(f"raw{r}_landed") for r in range(4)]
        raw_parted = [sem(f"raw{r}_parted") for r in range(4)]
        parts_used = [sem(f"parts{s}_used") for s in range(2)]
        upper_ready = sem("upper_ready")
        signals = {}

        def S(name):
            if name not in signals:
                signals[name] = sem(name)
            return signals[name]

        def at(plan, l):
            return At(plan, l, banks_filled, banks_emptied, tiles_landed, tiles_used, ps, ring)

        def parted(turn):
            return Parted(turn, raw_landed, raw_parted, parts_used, upper_ready)

        def experts(l, hf, it):
            return parted(l * (2 * TURNS) + it + TURNS * hf)

        def weights(l, n):
            return parted(l * (len(second.tiles) // 4) + (2 * TURNS * DEPTH + n // 4)), n % 4

        ident = cst[:, C_ID:C_ID + P]
        strict = cst[:, C_STRICT:C_STRICT + P]
        keep = cst[:, C_KEEP:C_KEEP + 384]
        tri, tri_ones, ones = keep[:, 0:P], keep[:, 0:2 * P], keep[:, P:2 * P]
        caus = cst[:, C_CAUS:C_CAUS + 384]
        band = cst[:, C_BAND:C_BAND + 384]
        zeros = caus[:, P:2 * P]
        iota = cst[:, C_IOTA:C_IOTA + P]

        def view(buf, at_, n, pat=None, **kw):
            v = buf[:, at_:at_ + n]
            return v.rearrange(pat, **kw) if pat else v

        xpad = view(work, 0, 8 * 259, "p (c t) -> p c t", c=8)
        conv = view(work, 2072, 2048, "p (c t) -> p c t", c=8)
        zs = view(work, 4120, 1024, "p (a n) -> p a n", a=TT)
        mqk = view(work, 5144, 1024, "p (c t) -> p c t", c=4)
        sqk = view(work, 6168, 1024, "p (c t) -> p c t", c=4)
        vt = view(work, 7192, 784, "p (a n) -> p a n", a=TT)
        cbm = view(work, 7976, 768, "p (g n) -> p g n", g=2)
        mP = view(work, 8744, 1536, "p (h n) -> p h n", h=ATT_H)
        sP = view(work, 10280, 1536, "p (h n) -> p h n", h=ATT_H)
        mPT = view(work, 11816, 1536, "p (h n) -> p h n", h=ATT_H)
        sPT = view(work, 13352, 1536, "p (h n) -> p h n", h=ATT_H)
        xs = view(scr, 0, 1024, "p (a n) -> p a n", a=TT)
        xdt = view(scr, 1024, 1024, "p (a n) -> p a n", a=TT)
        Aseg = view(scr, 2048, 768, "p (b n) -> p b n", b=2)
        Ldec = view(scr, 2816, 768, "p (b n) -> p b n", b=2)
        Mssd = view(scr, 3584, 1536, "p (b n) -> p b n", b=4)
        tmpA = view(scr, 5120, 1024, "p (b n) -> p b n", b=2)
        ada_bias = work[0:1, 8744:8744 + 6 * D]
        qT = view(work, 0, 4096, "p (c t) -> p c t", c=16)
        sc = view(work, 4096, 4096, "p (g n) -> p g n", g=32)
        sc2 = view(work, 8192, 4096, "p (g n) -> p g n", g=32)
        cand = view(work, 12288, 4096, "p (g n) -> p g n", g=16)
        sc_c = view(work, 4096, 4096, "p (g n) -> p g n", g=16)
        onehot = view(work, 0, 4096, "p (g j) -> p g j", j=16)
        V16 = view(scr, 0, 512, "p (g k) -> p g k", g=32)
        I16u = view(scr, 512, 512).bitcast(U32).rearrange("p (g k) -> p g k", g=32)
        I16 = view(scr, 1024, 512, "p (g k) -> p g k", g=32)
        Vc = view(scr, 1536, 256, "p (g k) -> p g k", g=16)
        Cu = view(scr, 1792, 256).bitcast(U32).rearrange("p (g k) -> p g k", g=16)
        Cd = view(scr, 2048, 512).bitcast(U32).rearrange("p (g k) -> p g k", g=2)
        Cf = view(scr, 2560, 512, "p (g k) -> p g k", g=2)
        E3 = view(scr, 3072, 768, "p (a t) -> p a t", a=3)
        gate = E3[:, 2, :].rearrange("p (g k) -> p g k", k=PK)
        ET = view(scr, 3840, 768, "p (a t) -> p a t", a=3)
        G = view(work, 0, 16384, "p (t i) -> p t i", i=HALF)
        marks = view(scr, 4608, 1024, "p (b t i) -> p b t i", b=2, t=8)
        gact = view(scr, 5120, 1024, "p (u c t) -> p u c t", u=2, c=2)

        def parts_at(name, shape, at_):
            return nc.alloc_sbuf_tensor_at(name, shape, F32R, offset=at_)

        raw = ring[:, 0:2, :].rearrange("p s (r n) -> p (s r) n", r=2)
        upper = parts_at("weights_upper", [P, 2, PART], ring_at + 4 * 2 * TILE)
        lower = parts_at("weights_lower", [P, 2, PART], ring_at + 4 * 3 * TILE)
        hT_up = parts_at("hT_upper", [P, KC, T], mod_at)
        hT_lo = parts_at("hT_lower", [P, KC, T], mod_at + 4 * KC * T)
        hotA = parts_at("first_key", [P, 2, 8, P], h_at)
        hotB = parts_at("second_key_gate", [P, 2, 8, 2, HALF], scr_at)
        g_up = parts_at("gate_upper", [P, T], scr_at + 4 * 2048)
        g_lo = view(scr, 2304, T)
        hid_up = parts_at("hidden_upper", [P, 2, 2, T], h_at)
        hid_lo = parts_at("hidden_lower", [P, 2, 2, T], h_at + 4 * 4 * T)

        hT2 = parts_at("hT2_upper", [P, KC, T], hT_at), parts_at("hT2_lower", [P, KC, T], work_at + 4 * 12288)
        hid2 = (parts_at("ffn_upper", [P, FC, T], work_at),
                parts_at("ffn_lower", [P, FC, T], work_at + 4 * FC * T))
        Zp2 = (parts_at("positions_upper", [P, 2, JP, 30], work_at + 4 * 7728),
               parts_at("positions_lower", [P, 2, JP, 30], work_at + 4 * 8688))
        memT2 = (parts_at("memT_upper", [P, KC, T], work_at),
                 parts_at("memT_lower", [P, KC, T], work_at + 4 * 10240))
        sgate = view(scr, 2048, 1024, "p (b n) -> p b n", b=2)
        qn = view(work, 0, 1024, "p (c t) -> p c t", c=4)
        Z = view(work, 1024, 1024, "p (c t) -> p c t", c=4)
        kk = view(work, 2048, 1024, "p (c t) -> p c t", c=4)
        qr = view(work, 3072, 1024, "p (c t) -> p c t", c=4)
        kr = view(work, 4096, 1024, "p (c t) -> p c t", c=4)
        vr = view(work, 5120, 1024, "p (a n) -> p a n", a=TT)
        gr = view(work, 6144, 1024, "p (a n) -> p a n", a=TT)
        vt2 = view(work, 7168, 560, "p (a n) -> p a n", a=TT)
        sA = view(work, 8688, 3072, "p (h n) -> p h n", h=NSA_H)
        PT = view(work, 11760, 3072, "p (h n) -> p h n", h=NSA_H)
        retm = view(work, 14832, RH * 384, "p (h n) -> p h n", h=RH)
        memnT = view(scr, 0, 2048, "p (c t) -> p c t", c=KC)
        tmpB = view(scr, 2048, 1024, "p (b n) -> p b n", b=2)
        onsa = view(scr, 3072, 1024, "p (a n) -> p a n", a=TT)
        hidc = view(scr, 4096, 512)
        hidcT = view(scr, 4608, 128)
        hidrep = view(scr, 4736, 512, "p (k g n) -> p k g n", k=2, g=2)
        kcT = view(scr, 5248, 32)
        vcbd = view(scr, 5280, 512, "p (g r d) -> p g r d", g=2, r=4)
        cS = view(scr, 5792, 240)
        cPad = view(mod, R2["end"] + 484, 512)
        cPT = view(scr, 3072, 512)
        qx = view(work, 2048, 2048, "p (c t) -> p c t", c=KC)
        kx = view(work, 4096, 2048, "p (c t) -> p c t", c=KC)
        vx = view(work, 6144, 2048, "p (a n) -> p a n", a=TT)
        Px = view(work, 8192, 2048, "p (h n) -> p h n", h=XH)
        PTx = view(work, 10240, 2048, "p (h n) -> p h n", h=XH)
        alibi = view(rowp, 0, 3072, "p (h n) -> p h n", h=NSA_H)
        rS = hT[:, 0:6, :].rearrange("p c t -> p (c t)").rearrange("p (h n) -> p h n", h=RH)

        SS, RR, RS = st[:, 0:8], st[:, 8:16], st[:, 16:24]

        def stat(i, n):
            return st[:, i:i + n]

        def halves(i, n):
            return st[:, i:i + TT * n].rearrange("p (a n) -> p a n", a=TT)

        cT = stat(300, 8)
        craw = stat(308, 8)

        block = ctx.enter_context(nc.Block())

        def lower_part(eng, r, c):
            return eng.tensor_tensor(lower[:, r % 2, c], raw[:, r, c], upper[:, r % 2, c].bitcast(F32), ALU.subtract)\
                .then_inc(raw_parted[r], 1)

        @block.sync
        def _(sp):
            def load(k, name, i, src):
                sp.wait_ge(*k.slot_free(name, i))
                sp.dma_start(k.tile(name, i), src).then_inc(k.land_sem(name, i), 16)

            def experts_over(e, slot):
                if slot < 2:
                    sp.wait_ge(*e.raw_free(2 * slot))
                    sp.wait_ge(*e.raw_free(2 * slot + 1))
                elif slot < RING:
                    sp.wait_ge(*e.split_free(0))
                    sp.wait_ge(*e.split_free(1))
                sp.sem_inc(S("held"), 1)

            with sp.Fori(0, DEPTH) as l:
                k = at(first, l)
                e = experts(l, 0, 0)
                for (name, i), n in first.tiles.items():
                    experts_over(e, n)
                    load(k, name, i, a["stream1"][bass.ds(l, 1), n].rearrange("o p n -> p (o n)"))
                sp.wait_ge(*k.slot_over(0))
                sp.wait_ge(*k.slot_over(1))
                sp.sem_inc(S("held"), 1)
                for hf in range(2):
                    with sp.Fori(0, TURNS) as it:
                        e = experts(l, hf, it)
                        for r in range(4):
                            sp.wait_ge(*e.raw_free(r))
                            src = a["experts"][bass.ds(l, 1), bass.ds(it * 4 + (4 * TURNS * hf + r), 1)]
                            sp.dma_start(raw[:, r, :], src.rearrange("o q p n -> p (o q n)"))\
                                .then_inc(raw_landed[r], 16)
            with sp.Fori(0, DEPTH) as l:
                for n in range(len(second.tiles)):
                    e, r = weights(l, n)
                    sp.wait_ge(*e.raw_free(r))
                    sp.dma_start(raw[:, r, :], a["stream2"][bass.ds(l, 1), n].rearrange("o p n -> p (o n)"))\
                        .then_inc(raw_landed[r], 16)
            sp.wait_ge(S("second_done"), DEPTH + 1)
            sp.dma_start(out[0].rearrange("(a p) n -> p a n", a=TT), x[:, :, :]).then_inc(S("stored"), 16)
            sp.wait_ge(S("stored"), 16)

        @block.gpsimd
        def _(g):
            for b in range(8):
                g.sem_inc(banks_emptied[b], 1)
            for s in range(RING):
                g.sem_inc(tiles_used[s], 1)
            g.sem_inc(S("first_done"), 1)
            g.sem_inc(S("second_done"), 1)
            for r in range(4):
                g.sem_inc(raw_parted[r], 1)
            for s in range(2):
                g.sem_inc(parts_used[s], 1)
            with g.Fori(0, DEPTH) as l:
                k = at(first, l)
                g.wait_ge(S("hT_up"), l + 1)
                g.tensor_tensor(hT_lo[:, :, :], hT[:, :, :], hT_up[:, :, :].bitcast(F32), ALU.subtract)\
                    .then_inc(S("hT_lo"), 1)
                for hf in range(2):
                    with g.Fori(0, GROUPS // 2) as it:
                        for b in range(2):
                            g.wait_ge(S("marked"), l * 64 + it * 2 + (32 * hf + b + 1))
                            t8 = bass.ds(it * 16 + 8 * b, 8)
                            for part, gates in enumerate((g_up[:, :].bitcast(F32), g_lo)):
                                m = g.tensor_tensor(hotB[:, b, :, part, :], marks[:, b, :, :],
                                                    column(gates[:, t8], HALF), ALU.mult)
                            m.then_inc(S("hotB"), 1)
                    with g.Fori(0, TURNS) as it:
                        e = experts(l, hf, it)
                        for r in range(4):
                            g.wait_ge(*e.upper(r))
                            lower_part(g, r, slice(PART // 2, PART))

            with g.Fori(0, DEPTH * len(second.tiles) // 4) as it:
                e = parted(it + 2 * TURNS * DEPTH)
                for r in range(4):
                    g.wait_ge(*e.upper(r))
                    lower_part(g, r, slice(PART // 2, PART))

        @block.tensor
        def _(pe):
            mm = nc.tensor.matmul

            def transposes(k, name, src):
                for i in range(4):
                    pe.wait_ge(*k.free(name, i))
                    for j in range(4):
                        c, t = 2 * i + j // 2, j % 2
                        m = nc.tensor.transpose(k.bank(name, i)[:, j * P:(j + 1) * P],
                                                src[:, t, c * P:(c + 1) * P], ident)
                    m.then_inc(k.fill_sem(name, i), 1)

            def by_token(k, name, tile, fill, cols=NBLK, w=None, src=hT):
                pe.wait_ge(*k.landed(name, tile))
                w = k.tile(name, tile).rearrange("p (c n) -> p c n", c=KC)
                for t in range(TT):
                    pe.wait_ge(*k.free(name, fill + t))
                    for c in range(KC):
                        m = mm(k.bank(name, fill + t)[:, 0:cols], src[:, c, t * P:(t + 1) * P], w[:, c, 0:cols],
                               start=(c == 0), stop=(c == KC - 1))
                    if t == TT - 1:
                        m.then_inc(k.fill_sem(name, fill + t), 1)
                    else:
                        m.then_inc(k.fill_sem(name, fill + t), 1)
                pe.drain().then_inc(k.used_sem(name, tile), 1)

            def by_feature(k, name, tile, fill, chunks=4, src=hT):
                pe.wait_ge(*k.landed(name, tile))
                w = k.tile(name, tile).rearrange("p (c n) -> p c n", c=KC)
                for j in range(chunks // 2):
                    pe.wait_ge(*k.free(name, fill + j))
                    for e in range(2):
                        for c in range(KC):
                            m = mm(k.bank(name, fill + j)[:, e * T:(e + 1) * T],
                                   w[:, c, (2 * j + e) * P:(2 * j + e + 1) * P], src[:, c, :],
                                   start=(c == 0), stop=(c == KC - 1), skip_group_check=True)
                    m.then_inc(k.fill_sem(name, fill + j), 1)
                pe.drain().then_inc(k.used_sem(name, tile), 1)

            def three_passes(src):
                return (lower, src[0]), (upper, src[1]), (upper, src[0])

            def parts_by_feature(k, l, name, i, src=hT2):
                e_, r = weights(l, k.plan.tiles[name, i])
                pe.wait_ge(*e_.parted(r))
                pe.wait_ge(*k.free(name, i))
                for e in range(2):
                    for n, (w, s_) in enumerate(three_passes(src)):
                        w = w[:, r % 2, :].rearrange("p (c n) -> p c n", c=KC)
                        for c in range(KC):
                            m = mm(k.bank(name, i)[:, e * T:(e + 1) * T], w[:, c, e * P:(e + 1) * P], s_[:, c, :],
                                   start=(n == 0 and c == 0), stop=(n == 2 and c == KC - 1), skip_group_check=True)
                m.then_inc(k.fill_sem(name, i), 1)
                pe.drain().then_inc(e_.used_sem(r), 1)

            def parts_by_token(k, l, name, tile, fill, tiles=2, chunks=KC, cols=NBLK, src=hT2):
                for t in range(TT):
                    pe.wait_ge(*k.free(name, fill + t))
                for i in range(tiles):
                    e_, r = weights(l, k.plan.tiles[name, tile + i])
                    pe.wait_ge(*e_.parted(r))
                    mine = range(4 * i, min(4 * i + 4, chunks))
                    for t in range(TT):
                        for n, (w, s_) in enumerate(three_passes(src)):
                            w = w[:, r % 2, :].rearrange("p (c n) -> p c n", c=4)
                            for c in mine:
                                m = mm(k.bank(name, fill + t)[:, 0:cols], s_[:, c, t * P:(t + 1) * P],
                                       w[:, c - 4 * i, 0:cols], start=(n == 0 and c == 0),
                                       stop=(n == 2 and c == chunks - 1))
                        if i == tiles - 1:
                            m.then_inc(k.fill_sem(name, fill + t), 1)
                    if i == tiles - 1:
                        pe.drain().then_inc(e_.used_sem(r), 1)
                    else:
                        m.then_inc(e_.used_sem(r), 1)

            def scores(k, name, i, q, kt):
                pe.wait_ge(*k.free(name, i))
                b = k.bank(name, i)
                mm(b[:, 0:P], q[:, 0:P], kt[:, 0:P], start=True, stop=True, skip_group_check=True)
                mm(b[:, P:3 * P], q[:, P:T], kt, start=True, stop=True, skip_group_check=True)\
                    .then_inc(k.fill_sem(name, i), 1)

            def turn(k, name, i, src):
                pe.wait_ge(*k.free(name, i))
                for j in range(3):
                    m = nc.tensor.transpose(k.bank(name, i)[:, j * P:(j + 1) * P], src[:, j * P:(j + 1) * P], ident)
                m.then_inc(k.fill_sem(name, i), 1)

            def three_blocks(b0, b1, pt, v0, v1, start=True):
                mm(b0, pt[:, 0:P], v0, start=start, stop=True, skip_group_check=True)
                mm(b1, pt[:, P:2 * P], v0, start=start, stop=False, skip_group_check=True)
                return mm(b1, pt[:, 2 * P:3 * P], v1, start=False, stop=True, skip_group_check=True)

            pe.wait_ge(S("const_in"), 16)
            pe.wait_ge(S("cond"), 1)
            with pe.Fori(0, DEPTH) as l:
                k = at(first, l)
                for i in range(12):
                    pe.wait_ge(*k.landed("ada", i))
                    pe.wait_ge(*k.free("ada", i))
                    w = k.tile("ada", i).rearrange("p (c n) -> p c n", c=KC)
                    for c in range(ADA_DVE, KC):
                        mm(k.bank("ada", i), cT[:, c:c + 1].broadcast_to([P, P]), w[:, c, :], start=(c == ADA_DVE),
                           stop=False)
                    if i == 0:
                        pe.wait_ge(S("mod_bias"), l * 16 + 16)
                        pe.sem_inc(S("held"), 1)
                    mm(k.bank("ada", i), ones[0:1, :], ada_bias[:, i * NBLK:(i + 1) * NBLK], start=False, stop=False)
                    pe.wait_ge(S("ada_acc"), l * 12 + (i + 1))
                    mm(k.bank("ada", i), ones, mod[:, i * NBLK:(i + 1) * NBLK], start=False, stop=True)\
                        .then_inc(k.fill_sem("ada", i), 1)
                    pe.drain().then_inc(k.used_sem("ada", i), 1)
                pe.wait_ge(S("h1"), l + 1)
                transposes(k, "hT", h)
                for i in range(4):
                    pe.wait_ge(*k.emptied("hT", i))
                by_token(k, "win", 0, 0)
                for i in range(1, 5):
                    by_feature(k, "win", i, 2 * i)
                by_token(k, "win", 5, 10, cols=392)
                pe.wait_ge(*k.emptied("win", 6))
                pe.wait_ge(*k.emptied("win", 7))
                for i in range(ATT_H):
                    q0 = HD * (i % 2)
                    scores(k, "mS", i, mqk[q0:q0 + HD, i // 2, :], mqk[q0:q0 + HD, 2 + i // 2, :])
                pe.wait_ge(*k.emptied("win", 8))
                pe.wait_ge(*k.emptied("win", 9))
                for i in range(ATT_H):
                    q0 = HD * (i % 2)
                    scores(k, "sS", i, sqk[q0:q0 + HD, i // 2, :], sqk[q0:q0 + HD, 2 + i // 2, :])
                pe.wait_ge(S("conv_silu"), l + 1)
                for t in range(TT):
                    pe.wait_ge(*k.free("xs", t))
                    for c in range(4):
                        m = nc.tensor.transpose(k.bank("xs", t)[:, c * P:(c + 1) * P],
                                                conv[:, c, t * P:(t + 1) * P], ident)
                    m.then_inc(k.fill_sem("xs", t), 1)
                for g_ in range(2):
                    pe.wait_ge(*k.free("cb", g_))
                    b = k.bank("cb", g_)
                    mm(b[:, 0:T], conv[:, 4 + g_, 0:P], conv[:, 6 + g_, :], start=True, stop=True,
                       skip_group_check=True)
                    mm(b[:, T:3 * P], conv[:, 4 + g_, P:T], conv[:, 6 + g_, P:T], start=True, stop=True,
                       skip_group_check=True).then_inc(k.fill_sem("cb", g_), 1)
                pe.wait_ge(S("mexp"), l + 1)
                for i in range(ATT_H):
                    turn(k, "mPT", i, mP[:, i, :])
                pe.wait_ge(*k.free("mO"))
                pe.wait_ge(*k.emptied("win", 10))
                pe.wait_ge(*k.emptied("win", 11))
                for i in range(ATT_H):
                    pe.wait_ge(*k.emptied("mPT", i))
                    b = k.bank("mO")
                    m = three_blocks(b[:, i * HD:(i + 1) * HD], b[:, T + i * HD:T + (i + 1) * HD], mPT[:, i, :],
                                     vt[:, 0, i * HD:(i + 1) * HD], vt[:, 1, i * HD:(i + 1) * HD])
                m.then_inc(k.fill_sem("mO"), 1)
                pe.wait_ge(S("sexp"), l + 1)
                for i in range(ATT_H):
                    turn(k, "sPT", i, sP[:, i, :])
                pe.wait_ge(*k.free("sO"))
                for i in range(ATT_H):
                    pe.wait_ge(*k.emptied("sPT", i))
                    b = k.bank("sO")
                    c = 256 + (i // 2) * HD
                    m = three_blocks(b[:, i * HD:(i + 1) * HD], b[:, T + i * HD:T + (i + 1) * HD], sPT[:, i, :],
                                     vt[:, 0, c:c + HD], vt[:, 1, c:c + HD])
                m.then_inc(k.fill_sem("sO"), 1)

                def seg(i):
                    name, j = ("seg01", i) if i < 2 else ("seg", i - 2)
                    pe.wait_ge(S("seg_in"), l * SSD_H + (i + 1))
                    pe.wait_ge(*k.free(name, j))
                    b = k.bank(name, j)
                    mm(b[:, 0:T], Aseg[:, i % 2, 0:P], tri_ones, start=True, stop=False, skip_group_check=True)
                    mm(b[:, P:T], Aseg[:, i % 2, 2 * P:3 * P], tri, start=False, stop=True, skip_group_check=True)
                    mm(b[:, T:3 * P], Aseg[:, i % 2, P:2 * P], tri, start=True, stop=True, skip_group_check=True)\
                        .then_inc(k.fill_sem(name, j), 1)

                def ssd_y(i):
                    pe.wait_ge(S("m_ssd"), l * SSD_H + (i + 1))
                    c = slice(i * HD, (i + 1) * HD)
                    three_blocks(k.bank("y", 0)[:, c], k.bank("y", 1)[:, c], Mssd[:, i % 4, :],
                                 xdt[:, 0, c], xdt[:, 1, c]).then_inc(S("y_head"), 1)

                seg(0)
                seg(1)
                pe.wait_ge(*k.free("y", 0))
                pe.wait_ge(*k.free("y", 1))
                for i in range(SSD_H):
                    ssd_y(i)
                    if i + 2 < SSD_H:
                        seg(i + 2)
                pe.drain().then_inc(k.fill_sem("y", 0), 1)
                pe.drain().then_inc(k.fill_sem("y", 1), 1)
                pe.wait_ge(S("ycat"), l + 1)
                transposes(k, "yT", h)
                for i in range(4):
                    pe.wait_ge(*k.emptied("yT", i))
                by_token(k, "wout", 0, 0)
                by_token(k, "wout", 1, 2)
                pe.wait_ge(S("h2"), l + 1)
                transposes(k, "h2T", h)
                for i in range(4):
                    pe.wait_ge(*k.emptied("h2T", i))
                for i in range(4):
                    by_feature(k, "wq", i, 2 * i)
                for i in range(8):
                    pe.wait_ge(*k.emptied("wq", i))
                for i in range(8):
                    t, hp = i // 4, i % 4
                    pe.wait_ge(*k.free("s", i))
                    for j in range(4):
                        c = 4 * hp + j
                        key = colp[:, K1["k1" if j % 2 == 0 else "k2"]:][:, 0:P]
                        m = mm(k.bank("s", i)[:, j * P:(j + 1) * P], qT[:, c, t * P:(t + 1) * P], key,
                               start=True, stop=True, skip_group_check=True)
                    m.then_inc(k.fill_sem("s", i), 1)
                pe.wait_ge(S("chosen"), l + 1)
                for i in range(2):
                    pe.wait_ge(*k.free("eT", i))
                    for j in range(4 - 2 * i):
                        m = nc.tensor.transpose(k.bank("eT", i)[:, j * P:(j + 1) * P],
                                                E3[:, 2 * i + j // 2, (j % 2) * P:(j % 2 + 1) * P], ident)
                    m.then_inc(k.fill_sem("eT", i), 1)
                for hf in range(2):
                    with pe.Fori(0, GROUPS // 2) as it:
                        for b in range(2):
                            pe.wait_ge(S("hotA"), l * 64 + it * 2 + (32 * hf + b + 1))
                            pe.wait_ge(S("hotB"), l * 64 + it * 2 + (32 * hf + b + 1))
                            for j in range(2):
                                pe.wait_ge(*k.free(f"G{hf}", 2 * b + j, it))
                                for t in range(4):
                                    m = mm(k.bank(f"G{hf}", 2 * b + j)[:, t * P:(t + 1) * P],
                                           hotA[:, b, 4 * j + t, :],
                                           hotB[:, b, 4 * j + t, :, :].rearrange("p a i -> p (a i)"),
                                           start=True, stop=True, skip_group_check=True)
                                m.then_inc(k.fill_sem(f"G{hf}", 2 * b + j), 1)
                    if hf == 0:
                        for i in range(4):
                            pe.wait_ge(*k.free("acc", i))
                            mm(k.bank("acc", i), zeros, cst[:, 0:NBLK], start=True, stop=False,
                               skip_group_check=True)
                    if hf == 0:
                        pe.wait_ge(S("hT_lo"), l + 1)
                        pe.sem_inc(S("held"), 1)
                    with pe.Fori(0, TURNS) as it:
                        x_ = experts(l, hf, it)
                        for u in range(2):
                            pe.wait_ge(*x_.parted(u))
                            pe.wait_ge(*k.free(f"U{hf}", u, it))
                            for e in range(2):
                                for p_, (w, src) in enumerate(three_passes((hT_up, hT_lo))):
                                    w = w[:, u, :].rearrange("p (c n) -> p c n", c=KC)
                                    for c in range(KC):
                                        m = mm(k.bank(f"U{hf}", u)[:, e * T:(e + 1) * T],
                                               w[:, c, e * P:(e + 1) * P], src[:, c, :],
                                               start=(p_ == 0 and c == 0), stop=(p_ == 2 and c == KC - 1),
                                               skip_group_check=True)
                            m.then_inc(k.fill_sem(f"U{hf}", u), 1)
                            pe.drain().then_inc(x_.used_sem(u), 1)
                        for u in range(2):
                            pe.wait_ge(*x_.parted(2 + u))
                            pe.wait_ge(S("gated"), l * 64 + it * 2 + (32 * hf + u + 1))
                            for w, src in three_passes((hid_up, hid_lo)):
                                w = w[:, u, :].rearrange("p (c n) -> p c n", c=2)
                                for c in range(2):
                                    for t in range(TT):
                                        for dh in range(2):
                                            m = mm(k.bank("acc", 2 * t + dh), src[:, u, c, t * P:(t + 1) * P],
                                                   w[:, c, dh * NBLK:(dh + 1) * NBLK], start=False, stop=False,
                                                   skip_group_check=True)
                            m.then_inc(x_.used_sem(2 + u), 1)
                for i in range(4):
                    mm(k.bank("acc", i)[:, 0:2], zeros, cst[:, 0:2], start=False, stop=True,
                       skip_group_check=True).then_inc(k.fill_sem("acc", i), 1)

            pe.wait_ge(S("memn"), 1)
            transposes(at(mid, 0), "mT", h)

            with pe.Fori(0, DEPTH) as l:
                k = at(second, l)

                def ffn(f, n):
                    pe.wait_ge(S("pre2"), l * 4 + (n + 1))
                    transposes(k, f + "T", h)
                    for i in range(4):
                        pe.wait_ge(*k.emptied(f + "T", i))
                    for i in range(FC):
                        parts_by_feature(k, l, f + "gu", i)
                    for i in range(FC - 8, FC):
                        pe.wait_ge(*k.emptied(f + "gu", i))
                    for nb in range(2):
                        parts_by_token(k, l, f + "d", 6 * nb, 2 * nb, tiles=6, chunks=FC, src=hid2)

                ffn("f1", 0)
                pe.wait_ge(S("pre2"), l * 4 + 2)
                transposes(k, "nT", h)
                for i in range(4):
                    pe.wait_ge(*k.emptied("nT", i))
                for i in range(10):
                    parts_by_feature(k, l, "nin", i)
                parts_by_token(k, l, "nin", 10, 10)
                parts_by_token(k, l, "nin", 12, 12)
                parts_by_token(k, l, "nin", 14, 14, cols=280)
                pe.wait_ge(S("zp"), l + 1)
                pe.wait_ge(*k.free("hid"))
                for i in range(4):
                    s = i // 2
                    e_, r = weights(l, second.tiles["cw1", i])
                    pe.wait_ge(*e_.parted(r))
                    for n, (w, z) in enumerate(three_passes(Zp2)):
                        w = w[:, r % 2, :].rearrange("p (j n) -> p j n", j=JP // 2)
                        for j in range(JP // 2):
                            m = mm(k.bank("hid")[0:30, s * T:(s + 1) * T], z[:, s, JP // 2 * (i % 2) + j, :],
                                   w[:, j, :], start=(i % 2 == 0 and n == 0 and j == 0),
                                   stop=(i % 2 == 1 and n == 2 and j == JP // 2 - 1), skip_group_check=True)
                    if i == 3:
                        m.then_inc(k.fill_sem("hid"), 1)
                        pe.drain().then_inc(e_.used_sem(r), 1)
                    else:
                        m.then_inc(e_.used_sem(r), 1)
                pe.wait_ge(*k.free("hidT"))
                pe.wait_ge(*k.emptied("hid"))
                pe.sem_inc(S("held"), 1)
                for j in range(4):
                    m = nc.tensor.transpose(k.bank("hidT")[:, j * 30:(j + 1) * 30], hidc[0:30, j * P:(j + 1) * P],
                                            ident[0:30, 0:30])
                m.then_inc(k.fill_sem("hidT"), 1)
                pe.wait_ge(*k.free("kc"))
                pe.wait_ge(*k.emptied("hidT"))
                w2 = colp[:, K2["w2"]:K2["end"]].rearrange("p (s k d) -> p s k d", s=2, k=2)
                b = k.bank("kc")
                for half in range(2):
                    for c in range(2):
                        mm(b[half * HD:(half + 1) * HD, 0:30], w2[:, 0, c, :], hidcT[:, c * 30:(c + 1) * 30],
                           start=(c == 0), stop=(c == 1), skip_group_check=True)
                for g_ in range(2):
                    for c in range(2):
                        m = mm(b[:, P + g_ * HD:P + (g_ + 1) * HD], hidrep[:, c, g_, :], w2[:, 1, c, :],
                               start=(c == 0), stop=(c == 1), skip_group_check=True)
                m.then_inc(k.fill_sem("kc"), 1)
                pe.wait_ge(*k.free("cS"))
                pe.wait_ge(*k.emptied("kc"))
                for odd in range(2):
                    if odd:
                        pe.drain()
                    for t, i in ((t, i) for t in range(TT) for i in range(odd, NSA_H, 2)):
                        q0 = HD * (i % 2)
                        c = (t * NSA_H + i) * NCMP
                        g_ = i // 4
                        m = mm(k.bank("cS")[:, c:c + NCMP], qn[q0:q0 + HD, i // 2, t * P:(t + 1) * P],
                               kcT[q0:q0 + HD, g_ * NCMP:(g_ + 1) * NCMP], start=True, stop=True,
                               skip_group_check=True)
                m.then_inc(k.fill_sem("cS"), 1)
                for i in range(8, 16):
                    pe.wait_ge(*k.emptied("nin", i))

                def all_scores(name, c0):
                    for i in range(NSA_H):
                        q0 = HD * (i % 2)
                        scores(k, name, i, qn[q0:q0 + HD, i // 2, :], kk[q0:q0 + HD, c0 + i // 4, :])

                def all_values(name, exp_signal, c0):
                    pe.wait_ge(S(exp_signal), l + 1)
                    for i in range(NSA_H):
                        turn(k, name + "PT", i, sA[:, i, :])
                    pe.wait_ge(*k.free(name + "O", 0))
                    pe.wait_ge(*k.free(name + "O", 1))
                    for i in range(NSA_H):
                        pe.wait_ge(*k.emptied(name + "PT", i))
                        c = c0 + (i // 4) * HD
                        m = three_blocks(k.bank(name + "O", 0)[:, i * HD:(i + 1) * HD],
                                         k.bank(name + "O", 1)[:, i * HD:(i + 1) * HD], PT[:, i, :],
                                         vt2[:, 0, c:c + HD], vt2[:, 1, c:c + HD])
                    pe.drain().then_inc(k.fill_sem(name + "O", 0), 1)
                    pe.drain().then_inc(k.fill_sem(name + "O", 1), 1)

                all_scores("wS", 2)
                pe.wait_ge(S("cprob"), l + 1)
                pe.wait_ge(*k.free("cPT"))
                for j in range(4):
                    m = nc.tensor.transpose(k.bank("cPT")[:, j * P:(j + 1) * P], cPad[:, j * P:(j + 1) * P], ident)
                m.then_inc(k.fill_sem("cPT"), 1)
                pe.wait_ge(*k.emptied("cPT"))
                for t in range(TT):
                    pe.wait_ge(*k.free("cO", t))
                    for g_ in range(2):
                        m = mm(k.bank("cO", t)[:, g_ * T:(g_ + 1) * T], cPT[:, (2 * t + g_) * P:(2 * t + g_ + 1) * P],
                               vcbd[:, g_, :, :].rearrange("p r d -> p (r d)"), start=True, stop=True,
                               skip_group_check=True)
                    m.then_inc(k.fill_sem("cO", t), 1)
                all_values("w", "wexp", 2 * HD)
                all_scores("lS", 0)
                for i in range(RH):
                    pe.wait_ge(*k.free("rS", i))
                    b = k.bank("rS", i)
                    mm(b[:, 0:T], kr[:, i, 0:P], qr[:, i, :], start=True, stop=True, skip_group_check=True)
                    mm(b[:, T:3 * P], kr[:, i, P:T], qr[:, i, P:T], start=True, stop=True, skip_group_check=True)\
                        .then_inc(k.fill_sem("rS", i), 1)
                all_values("l", "lexp", 0)
                pe.wait_ge(*k.free("rO", 0))
                pe.wait_ge(*k.free("rO", 1))
                for i in range(RH):
                    pe.wait_ge(*k.emptied("rS", i))
                    c = slice(i * P, (i + 1) * P)
                    three_blocks(k.bank("rO", 0)[:, c], k.bank("rO", 1)[:, c], rS[:, i, :], vr[:, 0, c], vr[:, 1, c])
                pe.drain().then_inc(k.fill_sem("rO", 0), 1)
                pe.drain().then_inc(k.fill_sem("rO", 1), 1)
                pe.wait_ge(S("ocat"), l + 1)
                transposes(k, "oT", h)
                for i in range(4):
                    pe.wait_ge(*k.emptied("oT", i))
                parts_by_token(k, l, "nout", 0, 0)
                parts_by_token(k, l, "nout", 2, 2)
                pe.wait_ge(S("pre2"), l * 4 + 3)
                transposes(k, "xT", h)
                pe.wait_ge(S("memT"), l + 1)
                for i in range(4):
                    parts_by_feature(k, l, "xk", i, src=memT2)
                for i in (0, 2):
                    parts_by_token(k, l, "xv", i, i, src=memT2)
                for i in range(4):
                    pe.wait_ge(*k.emptied("xT", i))
                for i in range(4):
                    parts_by_feature(k, l, "xq", i)
                for i in range(4):
                    pe.wait_ge(*k.emptied("xk", i))
                    pe.wait_ge(*k.emptied("xv", i))
                for i in range(XH):
                    pe.wait_ge(*k.emptied("xq", i))
                    pe.wait_ge(*k.free("xS", i))
                    for t in range(TT):
                        for c in range(2):
                            m = mm(k.bank("xS", i)[:, t * T:(t + 1) * T], qx[:, 2 * i + c, t * P:(t + 1) * P],
                                   kx[:, 2 * i + c, :], start=(c == 0), stop=(c == 1), skip_group_check=True)
                    m.then_inc(k.fill_sem("xS", i), 1)
                for i in range(XH):
                    pe.wait_ge(S("xprob"), l * XH + (i + 1))
                    pe.wait_ge(*k.free("xPT", i))
                    for j in range(4):
                        m = nc.tensor.transpose(k.bank("xPT", i)[:, j * P:(j + 1) * P],
                                                Px[:, i, (j % 2) * T + (j // 2) * P:][:, 0:P], ident)
                    m.then_inc(k.fill_sem("xPT", i), 1)
                for i in range(XH):
                    pe.wait_ge(*k.emptied("xPT", i))
                    pe.wait_ge(*k.free("xO", i))
                    for e in range(2):
                        for c in range(2):
                            v0 = i * 2 * P + e * P
                            m = mm(k.bank("xO", i)[:, e * T:(e + 1) * T], vx[:, c, v0:v0 + P],
                                   PTx[:, i, c * T:(c + 1) * T], start=(c == 0), stop=(c == 1),
                                   skip_group_check=True)
                    m.then_inc(k.fill_sem("xO", i), 1)
                for i in range(XH):
                    pe.wait_ge(*k.emptied("xO", i))
                parts_by_token(k, l, "xo", 0, 0)
                parts_by_token(k, l, "xo", 2, 2)
                ffn("f2", 3)

        @block.scalar
        def _(act):
            f = nc.scalar.activation

            def root(tag, value):
                act.wait_ge(S(tag + "_inv_var"), value)
                f(RS, RR, ACT.Sqrt).then_inc(S(tag + "_rstd"), 1)

            def take(k, name, i, dst, func=ACT.Copy, src=None, **kw):
                act.wait_ge(*k.filled(name, i))
                f(dst, k.bank(name, i) if src is None else src, func, **kw).then_inc(k.empty_sem(name, i), 1)

            def softmax_exp(buf, heads, neg, total, ready, value, done):
                act.wait_ge(S(ready), value)
                for i in range(heads):
                    for t in range(TT):
                        s = buf[:, i, 0:P] if t == 0 else buf[:, i, P:3 * P]
                        j = t * heads + i
                        m = f(s, s, ACT.Exp, bias=st[:, neg + j:neg + j + 1], accum_out=st[:, total + j:total + j + 1])
                m.then_inc(S(done), 1)

            act.dma_start(craw, a["c"]).then_inc(S("c_in"), 16)
            act.dma_start(cst[:, :], a["const1"]).then_inc(S("const_in"), 16)
            act.wait_ge(S("c_in"), 16)
            f(cT, craw, ACT.Silu).then_inc(S("cond"), 1)
            act.dma_start(x[:, :, :], a["x"][0].rearrange("(a p) n -> p a n", a=TT)).then_inc(S("x_in"), 16)
            with act.Fori(0, DEPTH) as l:
                k = at(first, l)
                act.wait_ge(S("first_done"), l + 1)
                act.dma_start(ada_bias, a["ada_b"][bass.ds(l, 1), :]).then_inc(S("mod_bias"), 16)
                act.dma_start(rowp[:, :], a["row1"][bass.ds(l, 1), :].broadcast_to([P, R1["end"]]))\
                    .then_inc(S("par1_in"), 16)
                act.dma_start(colp[:, 0:K1["end"]], a["col1"][bass.ds(l, 1)].rearrange("o p n -> p (o n)"))\
                    .then_inc(S("par1_in"), 16)
                for i in range(12):
                    if i == RING:
                        act.wait_ge(S("par1_in"), l * 32 + 32)
                        f(stat(168, 8), rowp[:, R1["alog"]:R1["alog"] + 8], ACT.Exp).then_inc(S("exp_a"), 1)
                        root("one", l * 3 + 1)
                    take(k, "ada", i, mod[:, i * NBLK:(i + 1) * NBLK])
                for i in (1, 3):
                    take(k, "hT", i, hT[:, 2 * i:2 * i + 2, :])
                for t in range(TT):
                    take(k, "win", t, zs[:, t, :], ACT.Silu)
                act.wait_ge(S("xpad0"), l + 1)
                for i in range(4):
                    take(k, "win", 2 + i, xpad[:, 2 * i:2 * i + 2, 3:259])
                act.wait_ge(S("conv"), l + 1)
                f(conv[:, :, :], conv[:, :, :], ACT.Silu).then_inc(S("conv_silu"), 1)
                act.wait_ge(S("sp_abs"), l + 1)
                f(stat(72, 16), stat(56, 16), ACT.Exp, scale=-1.0).then_inc(S("sp_exp"), 1)
                act.wait_ge(S("sp_one"), l + 1)
                f(stat(120, 16), stat(88, 16), ACT.Ln).then_inc(S("sp_log"), 1)
                softmax_exp(mP, ATT_H, 184, 192, "mmax", l + 1, "mexp")
                softmax_exp(sP, ATT_H, 208, 216, "smax", l + 1, "sexp")
                f(stat(224, 8), stat(224, 8), ACT.Exp).then_inc(S("sink_exp"), 1)
                for i in range(ATT_H):
                    take(k, "mPT", i, mPT[:, i, :], src=k.bank("mPT", i)[:, 0:384])
                for i in range(ATT_H):
                    take(k, "sPT", i, sPT[:, i, :], src=k.bank("sPT", i)[:, 0:384])
                for i in range(SSD_H):
                    name, j = ("seg01", i) if i < 2 else ("seg", i - 2)
                    if i >= 2:
                        act.wait_ge(S("m_ssd"), l * SSD_H + (i - 1))
                    take(k, name, j, Ldec[:, i % 2, :], ACT.Exp, src=k.bank(name, j)[:, 0:384])
                root("one", l * 3 + 2)
                for i in (1, 3):
                    take(k, "yT", i, hT[:, 2 * i:2 * i + 2, :])
                root("one", l * 3 + 3)
                for i in (1, 3):
                    take(k, "h2T", i, hT[:, 2 * i:2 * i + 2, :])
                for i in range(1, 8, 2):
                    take(k, "wq", i, qT[:, 2 * i:2 * i + 2, :])
                for i in range(1, 8, 2):
                    take(k, "s", i, sc[:, 4 * i:4 * i + 4, :])
                for i in range(4):
                    act.wait_ge(*k.emptied("h2T", i))
                f(hT_up[:, :, :], hT[:, :, :], ACT.Copy).then_inc(S("hT_up"), 1)
                act.wait_ge(S("gmax"), l + 1)
                f(gate, gate, ACT.Exp).then_inc(S("gexp"), 1)
                act.wait_ge(*k.slot_over(2))
                act.wait_ge(*k.slot_over(3))
                for hf in range(2):
                    if hf == 1:
                        act.wait_ge(S("gated"), l * 64 + 32)
                    with act.Fori(0, GROUPS // 2) as it:
                        for b in range(4):
                            act.wait_ge(*k.filled(f"G{hf}", b, it))
                            f(G[:, bass.ds(it * 16 + 4 * b, 4), :],
                              k.bank(f"G{hf}", b).rearrange("p (t a i) -> p t a i", t=4, a=2)[:, :, 0, :],
                              ACT.Copy).then_inc(S("gates_up"), 1)
                    with act.Fori(0, TURNS) as it:
                        e = experts(l, hf, it)
                        for r in range(4):
                            act.wait_ge(*e.landed(r))
                            act.wait_ge(*e.split_free(r))
                            f(upper[:, r % 2, :], raw[:, r, :], ACT.Copy).then_inc(upper_ready, 1)
                            if r >= 2:
                                u = r - 2
                                act.wait_ge(*k.filled(f"U{hf}", u, it))
                                f(gact[:, u, :, :], k.bank(f"U{hf}", u), ACT.Gelu).then_inc(k.empty_sem(f"U{hf}", u), 1)
            act.wait_ge(S("first_done"), DEPTH + 1)
            act.dma_start(h[:, :, :], a["mem"][0].rearrange("(a p) n -> p a n", a=TT)).then_inc(S("mem_in"), 16)
            act.dma_start(mod[:, 0:D], a["final_g"].rearrange("(o n) -> o n", o=1).broadcast_to([P, D]))\
                .then_inc(S("fin_in"), 16)
            act.dma_start(rowp[:, 0:3072], a["const2"][:, 0:3072]).then_inc(S("const2_in"), 16)
            act.dma_start(work[:, 14832:14832 + 1536], a["const2"][:, C2["ret"]:C2["end"]])\
                .then_inc(S("const2_in"), 16)
            act.dma_start(mod[:, R2["end"]:R2["end"] + 484], a["const2"][:, C2["cbias"]:C2["ret"]])\
                .then_inc(S("const2_in"), 16)
            root("mid", 1)
            root("mid", 2)
            k = at(mid, 0)
            for i in (1, 3):
                take(k, "mT", i, memnT[:, 2 * i:2 * i + 2, :])

            def upper_part(e, r):
                act.wait_ge(*e.landed(r))
                act.wait_ge(*e.split_free(r))
                f(upper[:, r % 2, :], raw[:, r, :], ACT.Copy).then_inc(upper_ready, 1)

            with act.Fori(0, DEPTH) as l:
                k = at(second, l)

                def ahead(name, first_, n=1):
                    for i in range(first_, first_ + n):
                        if second.tiles[name, i] + 2 < len(second.tiles):
                            upper_part(*weights(l, second.tiles[name, i] + 2))

                for n in range(2):
                    upper_part(*weights(l, n))
                act.wait_ge(S("second_done"), l + 1)
                act.wait_ge(S("mid_done"), 1)
                act.dma_start(mod[:, 0:R2["end"]], a["row2"][bass.ds(l, 1), :].broadcast_to([P, R2["end"]]))\
                    .then_inc(S("par2_in"), 16)
                act.dma_start(colp[:, 0:K2["end"]], a["col2"][bass.ds(l, 1)].rearrange("o p n -> p (o n)"))\
                    .then_inc(S("par2_in"), 16)

                def ffn(name, r):
                    root("two", l * 10 + r)
                    for i in range(0, FC, 2):
                        ahead(name + "gu", i)
                        act.wait_ge(*k.filled(name + "gu", i))
                        if i >= 4:
                            act.wait_ge(*k.emptied(name + "gu", i - 3))
                        f(sgate[:, i // 2 % 2, :], k.bank(name + "gu", i), ACT.Silu)\
                            .then_inc(k.empty_sem(name + "gu", i), 1)
                        ahead(name + "gu", i + 1)
                    for i in range(4):
                        if i % 2 == 0:
                            ahead(name + "d", 3 * i, 6)
                        take(k, name + "d", i, h[:, i % 2, (i // 2) * NBLK:(i // 2 + 1) * NBLK])
                    root("two", l * 10 + (r + 1))

                ffn("f1", 1)
                root("two", l * 10 + 3)
                for i in range(2):
                    ahead("nin", i)
                    take(k, "nin", i, qn[:, 2 * i:2 * i + 2, :], scale=HD ** -0.5)
                ahead("nin", 2, 2)
                for i in range(4, 10):
                    dst = (kk, qr, kr)[(i - 4) // 2]
                    c = 2 * (i % 2)
                    ahead("nin", i)
                    take(k, "nin", i, dst[:, c:c + 2, :])
                ahead("nin", 10, 4)
                for t in range(TT):
                    take(k, "nin", 12 + t, gr[:, t, :], ACT.Silu)
                ahead("nin", 14, 2)
                for t in range(TT):
                    act.wait_ge(*k.filled("nin", 14 + t))
                    f(stat(152 + 24 * t, 24), k.bank("nin", 14 + t)[:, 256:280], ACT.Sigmoid)
                    f(vt2[:, t, 0:256], k.bank("nin", 14 + t)[:, 0:256], ACT.Copy)\
                        .then_inc(k.empty_sem("nin", 14 + t), 1)
                ahead("cw1", 0, 4)
                act.wait_ge(*k.filled("hid"))
                f(hidc[0:30, :], k.bank("hid")[0:30, :], ACT.Silu).then_inc(k.empty_sem("hid"), 1)
                act.wait_ge(S("cmax"), l + 1)
                f(cS[:, :], cS[:, :], ACT.Exp).then_inc(S("cexp"), 1)
                softmax_exp(sA, NSA_H, 40, 56, "wmax", l + 1, "wexp")
                for i in range(NSA_H):
                    take(k, "wPT", i, PT[:, i, :], src=k.bank("wPT", i)[:, 0:384])
                softmax_exp(sA, NSA_H, 88, 104, "lmax", l + 1, "lexp")
                for i in range(NSA_H):
                    if i == 0:
                        act.wait_ge(*k.filled("wO", 1))
                    take(k, "lPT", i, PT[:, i, :], src=k.bank("lPT", i)[:, 0:384])
                root("two", l * 10 + 4)
                root("two", l * 10 + 5)
                for i in range(4):
                    if i % 2 == 0:
                        ahead("nout", i, 2)
                    take(k, "nout", i, h[:, i % 2, (i // 2) * NBLK:(i // 2 + 1) * NBLK])
                root("two", l * 10 + 6)
                root("two", l * 10 + 7)
                for i in range(4):
                    ahead("xk", i)
                    take(k, "xk", i, kx[:, 2 * i:2 * i + 2, :])
                for i in range(4):
                    if i % 2 == 0:
                        ahead("xv", i, 2)
                    take(k, "xv", i, vx[:, i % 2, (i // 2) * NBLK:(i // 2 + 1) * NBLK])
                for i in range(4):
                    ahead("xq", i)
                    take(k, "xq", i, qx[:, 2 * i:2 * i + 2, :], scale=(2 * P) ** -0.5)
                for i in range(XH):
                    act.wait_ge(S("xmax"), l * XH + (i + 1))
                    for t in range(TT):
                        j = 2 * i + t
                        m = f(Px[:, i, t * T:(t + 1) * T], k.bank("xS", i)[:, t * T:(t + 1) * T], ACT.Exp,
                              bias=st[:, 272 + j:273 + j], accum_out=st[:, 280 + j:281 + j])
                    m.then_inc(k.empty_sem("xS", i), 1)
                for i in range(XH):
                    take(k, "xPT", i, PTx[:, i, :])
                for i in range(4):
                    if i % 2 == 0:
                        ahead("xo", i, 2)
                    take(k, "xo", i, h[:, i % 2, (i // 2) * NBLK:(i // 2 + 1) * NBLK])
                root("two", l * 10 + 8)
                ffn("f2", 9)

        @block.vector
        def _(v):
            def mean_squares(parts, n):
                for j, (src, junk) in enumerate(parts):
                    v.tensor_tensor_reduce(out=junk, in0=src, in1=src, scale=1.0 / n[j], scalar=0.0, op0=ALU.mult,
                                           op1=ALU.add, accum_out=SS[:, j:j + 1])

            def rstd(tag, value, eps):
                v.drain()
                v.tensor_scalar(RR, SS, eps, None, ALU.add)
                v.drain()
                v.reciprocal(RR, RR).then_inc(S(tag + "_inv_var"), 1)
                v.wait_ge(S(tag + "_rstd"), value)

            def take(k, name, i, dst, src=None, scale=1.0):
                v.wait_ge(*k.filled(name, i))
                v.tensor_scalar(dst, k.bank(name, i) if src is None else src, scale, None, ALU.mult)\
                    .then_inc(k.empty_sem(name, i), 1)

            def masked_max(k, name, i, bias, buf, heads, top):
                v.wait_ge(*k.filled(name, i))
                v.sem_inc(S("held"), 1)
                for t in range(TT):
                    c = slice(0, P) if t == 0 else slice(P, 3 * P)
                    j = top + t * heads + i
                    m = v.tensor_tensor_reduce(out=buf[:, i, c], in0=k.bank(name, i)[:, c], in1=bias[:, c],
                                               scale=1.0, scalar=LOWEST, op0=ALU.add, op1=ALU.max,
                                               accum_out=st[:, j:j + 1])
                m.then_inc(k.empty_sem(name, i), 1)

            v.wait_ge(S("const_in"), 16)
            v.wait_ge(S("cond"), 1)
            v.memset(SS, 1.0)
            v.memset(RS, 1.0)
            v.drain()
            with v.Fori(0, DEPTH) as l:
                k = at(first, l)
                v.drain()
                v.memset(xpad[:, :, 0:3], 0.0).then_inc(S("xpad0"), 1)
                def normed(g0, value):
                    mean_squares([(x[:, t, :], h[:, t, :]) for t in range(TT)], [D] * TT)
                    rstd("one", value, EPS1)
                    for t in range(TT):
                        v.scalar_tensor_tensor(out=h[:, t, :], in0=x[:, t, :], scalar=RS[:, t:t + 1],
                                               in1=rowp[:, g0:g0 + D], op0=ALU.mult, op1=ALU.mult)
                    v.drain()

                def modulated(shift, signal):
                    for t in range(TT):
                        v.scalar_tensor_tensor(out=h[:, t, :], in0=mod[:, shift + D:shift + 2 * D], scalar=1.0,
                                               in1=h[:, t, :], op0=ALU.add, op1=ALU.mult)
                    v.drain()
                    for t in range(TT):
                        m = v.tensor_tensor(h[:, t, :], h[:, t, :], mod[:, shift:shift + D], ALU.add)
                    m.then_inc(S(signal), 1)

                for i in range(12):
                    if i == RING:
                        v.wait_ge(S("par1_in"), l * 32 + 32)
                        v.wait_ge(S("x_in"), 16)
                        v.sem_inc(S("held"), 1)
                        normed(R1["n1"], l * 3 + 1)
                    v.wait_ge(*k.landed("ada", i))
                    w = k.tile("ada", i).rearrange("p (c n) -> p c n", c=KC)
                    acc = mod[:, i * NBLK:(i + 1) * NBLK]
                    v.tensor_scalar(acc, w[:, 0, :], cT[:, 0:1], None, ALU.mult)
                    for c in range(1, ADA_DVE):
                        v.drain()
                        m = v.scalar_tensor_tensor(out=acc, in0=w[:, c, :], scalar=cT[:, c:c + 1], in1=acc,
                                                   op0=ALU.mult, op1=ALU.add)
                    m.then_inc(S("ada_acc"), 1)

                for i in range(12):
                    v.wait_ge(*k.emptied("ada", i))
                modulated(0, "h1")
                for i in (0, 2):
                    take(k, "hT", i, hT[:, 2 * i:2 * i + 2, :])
                for i in range(4):
                    v.wait_ge(*k.emptied("win", 2 + i))
                for tap in range(4):
                    if tap:
                        v.drain()
                    for c in range(8):
                        w = colp[:, K1["cw"] + 4 * c + tap:][:, 0:1]
                        if tap == 0:
                            m = v.tensor_scalar(conv[:, c, :], xpad[:, c, 0:T], w,
                                                colp[:, K1["cb"] + c:K1["cb"] + c + 1], ALU.mult, ALU.add)
                        else:
                            m = v.scalar_tensor_tensor(out=conv[:, c, :], in0=xpad[:, c, tap:tap + T], scalar=w,
                                                       in1=conv[:, c, :], op0=ALU.mult, op1=ALU.add)
                m.then_inc(S("conv"), 1)
                take(k, "win", 6, mqk[:, 0:2, :], scale=HD ** -0.5)
                take(k, "win", 7, mqk[:, 2:4, :])
                take(k, "win", 8, sqk[:, 0:2, :], scale=HD ** -0.5)
                take(k, "win", 9, sqk[:, 2:4, :])
                for t in range(TT):
                    take(k, "win", 10 + t, vt[:, t, :], src=k.bank("win", 10 + t)[:, 0:392])
                r, nr, ab, u, y, d_, ln, dt, aa = (stat(24 + 16 * j, 16) for j in range(9))
                eq = nr
                v.drain()
                v.tensor_tensor(halves(24, 8), vt[:, :, 384:392], row(rowp[:, R1["dtb"]:R1["dtb"] + 8], TT), ALU.add)
                v.drain()
                v.tensor_scalar(nr, r, -1.0, None, ALU.mult)
                v.drain()
                v.tensor_tensor(ab, r, nr, ALU.max).then_inc(S("sp_abs"), 1)
                v.wait_ge(S("sp_exp"), l + 1)
                v.tensor_scalar(y, u, 1.0, None, ALU.add).then_inc(S("sp_one"), 1)
                v.drain()
                v.tensor_scalar(eq, y, 1.0, None, ALU.is_equal)
                v.drain()
                v.scalar_tensor_tensor(out=d_, in0=y, scalar=-1.0, in1=eq, op0=ALU.add, op1=ALU.add)
                v.drain()
                v.reciprocal(d_, d_)
                v.wait_ge(S("sp_log"), l + 1)
                v.tensor_tensor(ln, ln, eq, ALU.add)
                v.drain()
                v.tensor_tensor(ln, ln, u, ALU.mult)
                v.drain()
                v.tensor_tensor(ln, ln, d_, ALU.mult)
                v.drain()
                v.scalar_tensor_tensor(out=dt, in0=r, scalar=0.0, in1=ln, op0=ALU.max, op1=ALU.add)
                v.drain()
                v.wait_ge(S("exp_a"), l + 1)
                v.scalar_tensor_tensor(out=halves(152, 8), in0=halves(136, 8), scalar=-1.0,
                                       in1=row(stat(168, 8), TT), op0=ALU.mult, op1=ALU.mult)
                for i in range(ATT_H):
                    masked_max(k, "mS", i, caus, mP, ATT_H, 176)
                v.drain()
                v.tensor_scalar(stat(184, 8), stat(176, 8), -1.0, None, ALU.mult).then_inc(S("mmax"), 1)
                for i in range(ATT_H):
                    masked_max(k, "sS", i, band, sP, ATT_H, 200)
                sink = row(rowp[:, R1["sink"]:R1["sink"] + ATT_H], TT)
                v.drain()
                v.tensor_tensor(halves(200, 4), halves(200, 4), sink, ALU.max)
                v.drain()
                v.tensor_tensor(halves(224, 4), sink, halves(200, 4), ALU.subtract)
                v.tensor_scalar(stat(208, 8), stat(200, 8), -1.0, None, ALU.mult).then_inc(S("smax"), 1)
                for t in range(TT):
                    v.wait_ge(*k.filled("xs", t))
                    v.tensor_tensor(xdt[:, t, :].rearrange("p (h d) -> p h d", d=HD),
                                    k.bank("xs", t).rearrange("p (h d) -> p h d", d=HD),
                                    column(stat(136 + 8 * t, 8), HD), ALU.mult)
                    v.tensor_tensor(xs[:, t, :].rearrange("p (h d) -> p h d", d=HD),
                                    k.bank("xs", t).rearrange("p (h d) -> p h d", d=HD),
                                    column(rowp[:, R1["dsk"]:R1["dsk"] + 8], HD), ALU.mult)\
                        .then_inc(k.empty_sem("xs", t), 1)
                for g_ in range(2):
                    v.wait_ge(*k.filled("cb", g_))
                    v.tensor_tensor(cbm[:, g_, :], k.bank("cb", g_)[:, 0:384], keep, ALU.mult)\
                        .then_inc(k.empty_sem("cb", g_), 1)

                def seg_in(i):
                    if i >= 2:
                        v.wait_ge(*k.filled("seg01" if i < 4 else "seg", i - 2 if i < 4 else i - 4))
                    b = Aseg[:, i % 2, :]
                    v.tensor_scalar(b[:, 0:P], strict, stat(152 + i, 1), None, ALU.mult)
                    v.tensor_scalar(b[:, P:2 * P], strict, stat(160 + i, 1), None, ALU.mult)
                    v.tensor_scalar(b[:, 2 * P:3 * P], ones, stat(160 + i, 1), None, ALU.mult)\
                        .then_inc(S("seg_in"), 1)

                seg_in(0)
                seg_in(1)
                v.wait_ge(S("mexp"), l + 1)
                v.wait_ge(S("sink_exp"), l + 1)
                v.tensor_tensor(stat(216, 8), stat(216, 8), stat(224, 8), ALU.add)
                v.reciprocal(stat(232, 8), stat(192, 8))
                v.drain()
                v.reciprocal(stat(240, 8), stat(216, 8))
                v.drain()
                for name, c0, rc in (("mO", 512, 232), ("sO", 768, 240)):
                    v.wait_ge(*k.filled(name))
                    for t in range(TT):
                        m = v.tensor_tensor(h[:, t, c0:c0 + 256].rearrange("p (h d) -> p h d", d=HD),
                                            k.bank(name)[:, t * T:(t + 1) * T].rearrange("p (h d) -> p h d", d=HD),
                                            column(stat(rc + 4 * t, 4), HD), ALU.mult)
                    m.then_inc(k.empty_sem(name), 1)
                for i in range(SSD_H):
                    v.wait_ge(*k.emptied("seg01" if i < 2 else "seg", i if i < 2 else i - 2))
                    if i >= 4:
                        v.wait_ge(S("y_head"), l * SSD_H + (i - 3))
                    v.tensor_tensor(Mssd[:, i % 4, :], Ldec[:, i % 2, :], cbm[:, i // 4, :], ALU.mult)\
                        .then_inc(S("m_ssd"), 1)
                    if i + 2 < SSD_H:
                        seg_in(i + 2)
                for t in range(TT):
                    v.wait_ge(*k.filled("y", t))
                    v.tensor_tensor(h[:, t, 0:SSD_W], k.bank("y", t), xs[:, t, :], ALU.add)\
                        .then_inc(k.empty_sem("y", t), 1)
                v.drain()
                for t in range(TT):
                    v.tensor_tensor(h[:, t, 0:SSD_W], h[:, t, 0:SSD_W], zs[:, t, :], ALU.mult)
                v.drain()
                parts = [(t, c0, n, g0) for c0, n, g0 in ((0, SSD_W, R1["ssd"]), (512, 256, R1["moba"]),
                                                          (768, 256, R1["swa"])) for t in range(TT)]
                mean_squares([(h[:, t, c0:c0 + n], tmpA[:, t, 0:n]) for t, c0, n, _ in parts[0:2]], [SSD_W] * 2)
                v.drain()
                for j, (t, c0, n, _) in enumerate(parts[2:]):
                    v.tensor_tensor_reduce(out=tmpA[:, j // 2, (j % 2) * 256:(j % 2 + 1) * 256],
                                           in0=h[:, t, c0:c0 + n], in1=h[:, t, c0:c0 + n], scale=1.0 / n, scalar=0.0,
                                           op0=ALU.mult, op1=ALU.add, accum_out=SS[:, 2 + j:3 + j])
                rstd("one", l * 3 + 2, EPS1)
                for j, (t, c0, n, g0) in enumerate(parts):
                    m = v.scalar_tensor_tensor(out=h[:, t, c0:c0 + n], in0=h[:, t, c0:c0 + n], scalar=RS[:, j:j + 1],
                                               in1=rowp[:, g0:g0 + n], op0=ALU.mult, op1=ALU.mult)
                m.then_inc(S("ycat"), 1)
                for i in (0, 2):
                    take(k, "yT", i, hT[:, 2 * i:2 * i + 2, :])

                def add_gated(name, gate0, bank_of):
                    for i in range(4):
                        nb, t = bank_of(i)
                        c = slice(nb * NBLK, (nb + 1) * NBLK)
                        v.drain()
                        v.wait_ge(*k.filled(name, i))
                        v.tensor_tensor(tmpA[:, i % 2, :], k.bank(name, i), mod[:, gate0:][:, c], ALU.mult)\
                            .then_inc(k.empty_sem(name, i), 1)
                        v.drain()
                        v.tensor_tensor(x[:, t, c], x[:, t, c], tmpA[:, i % 2, :], ALU.add)
                    v.drain()

                add_gated("wout", 2 * D, lambda i: (i // 2, i % 2))
                normed(R1["n2"], l * 3 + 3)
                modulated(3 * D, "h2")
                for i in (0, 2):
                    take(k, "h2T", i, hT[:, 2 * i:2 * i + 2, :])
                for i in range(0, 8, 2):
                    take(k, "wq", i, qT[:, 2 * i:2 * i + 2, :])
                for i in range(0, 8, 2):
                    take(k, "s", i, sc[:, 4 * i:4 * i + 4, :])
                for i in range(8):
                    v.wait_ge(*k.emptied("s", i))
                v.sem_inc(S("held"), 1)

                def best_16(groups, s, s_left, val, idx):
                    for g_ in range(groups):
                        v.max(val[:, g_, 0:8], s[:, g_, :])
                    v.drain()
                    for g_ in range(groups):
                        v.max_index(idx[:, g_, 0:8], val[:, g_, 0:8], s[:, g_, :])
                        v.match_replace(s_left[:, g_, :], val[:, g_, 0:8], s[:, g_, :], LOWEST)
                    v.drain()
                    for g_ in range(groups):
                        v.max(val[:, g_, 8:16], s_left[:, g_, :])
                    v.drain()
                    for g_ in range(groups):
                        v.max_index(idx[:, g_, 8:16], val[:, g_, 8:16], s_left[:, g_, :])
                    v.drain()

                best_16(32, sc, sc2, V16, I16u)
                v.tensor_copy(I16[:, :, :], I16u[:, :, :])
                pair = V16.rearrange("p (g e) k -> p g e k", e=2)
                for g_ in range(16):
                    v.tensor_tensor(cand[:, g_, :].rearrange("p (a b) -> p a b", b=PK), column(pair[:, g_, 0, :], PK),
                                    row(pair[:, g_, 1, :], PK), ALU.add)
                v.drain()
                best_16(16, cand, sc_c, Vc, Cu)
                v.tensor_tensor(gate, Vc[:, :, :], Vc[:, :, 0:1].broadcast_to([P, 16, PK]), ALU.subtract)\
                    .then_inc(S("gmax"), 1)
                v.tensor_single_scalar(Cd[:, 0, :], Cu.rearrange("p g k -> p (g k)"), 4, ALU.logical_shift_right)
                v.tensor_single_scalar(Cd[:, 1, :], Cu.rearrange("p g k -> p (g k)"), 15, ALU.bitwise_and)
                v.drain()
                v.tensor_copy(Cf[:, :, :], Cd[:, :, :])
                v.wait_ge(S("gexp"), l + 1)
                v.tensor_reduce(stat(248, 16), gate, AX.X, ALU.add)
                v.drain()
                v.reciprocal(stat(248, 16), stat(248, 16))
                v.drain()
                v.tensor_tensor(gate, gate,
                                column(stat(248, 16), PK), ALU.mult)
                keys = I16.rearrange("p (g e) k -> p g e k", e=2)
                for e in range(2):
                    v.drain()
                    v.tensor_tensor(onehot[:, :, :], column(Cf[:, e, :], PK), row(iota[:, 0:PK], 256), ALU.is_equal)
                    v.drain()
                    for g_ in range(16):
                        o = onehot[:, g_ * PK:(g_ + 1) * PK, :]
                        v.tensor_tensor(o, o, row(keys[:, g_, e, :], PK), ALU.mult)
                    v.drain()
                    m = v.tensor_reduce(E3[:, e, :], onehot[:, :, :], AX.X, ALU.add)
                m.then_inc(S("chosen"), 1)
                take(k, "eT", 0, ET[:, 0:2, :])
                take(k, "eT", 1, ET[:, 2, :], src=k.bank("eT", 1)[:, 0:T])
                v.drain()
                v.tensor_copy(g_up[:, :], ET[:, 2, :])
                v.drain()
                v.tensor_tensor(g_lo, ET[:, 2, :], g_up[:, :].bitcast(F32), ALU.subtract)
                v.drain()
                for hf in range(2):
                    if hf == 1:
                        for r in range(2):
                            v.wait_ge(*experts(l, 1, 0).split_free(r))
                        v.sem_inc(S("held"), 1)

                    def spread(it, b):
                        v.wait_ge(*k.filled(f"G{hf}", 2 * b + 1, it - 1))
                        t8 = bass.ds(it * 16 + 8 * b, 8)
                        v.tensor_tensor(marks[:, b, :, :], row(iota[:, hf * HALF:(hf + 1) * HALF], 8),
                                        column(ET[:, 1, t8], HALF), ALU.is_equal).then_inc(S("marked"), 1)
                        v.tensor_tensor(hotA[:, b, :, :], row(iota, 8), column(ET[:, 0, t8], P), ALU.is_equal)\
                            .then_inc(S("hotA"), 1)

                    def collect(it, b):
                        for j in range(2):
                            v.wait_ge(S("gates_up"), l * 128 + it * 4 + (64 * hf + 2 * b + j + 1))
                            both = k.bank(f"G{hf}", 2 * b + j).rearrange("p (t a i) -> p t a i", t=4, a=2)
                            g_ = G[:, bass.ds(it * 16 + (8 * b + 4 * j), 4), :]
                            v.tensor_tensor(g_, g_, both[:, :, 1, :], ALU.add)\
                                .then_inc(k.empty_sem(f"G{hf}", 2 * b + j), 1)

                    spread(0, 0)
                    spread(0, 1)
                    with v.Fori(0, GROUPS // 2 - 1) as it:
                        for b in range(2):
                            spread(it + 1, b)
                            collect(it, b)
                    collect(GROUPS // 2 - 1, 0)
                    collect(GROUPS // 2 - 1, 1)
                    v.drain()
                    with v.Fori(0, TURNS) as it:
                        e = experts(l, hf, it)
                        for r in range(4):
                            v.wait_ge(*e.upper(r))
                            lower_part(v, r, slice(0, PART // 2))
                            if r >= 2:
                                u = r - 2
                                v.wait_ge(*k.emptied(f"U{hf}", u, it))
                                gates = G[:, :, bass.ds(it * 4 + 2 * u, 2)].rearrange("p t i -> p i t")
                                v.tensor_tensor(hid_up[:, u, :, :], gact[:, u, :, :], gates, ALU.mult)
                                v.tensor_tensor(gact[:, u, :, :], gact[:, u, :, :], gates, ALU.mult)
                                v.drain()
                                v.tensor_tensor(hid_lo[:, u, :, :], gact[:, u, :, :],
                                                hid_up[:, u, :, :].bitcast(F32), ALU.subtract)\
                                    .then_inc(S("gated"), 1)
                add_gated("acc", 5 * D, lambda i: (i % 2, i // 2))
                v.drain().then_inc(S("first_done"), 1)

            v.wait_ge(S("fin_in"), 16)
            v.wait_ge(S("mem_in"), 16)
            mean_squares([(x[:, t, :], scr[:, 2048 + t * D:2048 + (t + 1) * D]) for t in range(TT)], [D] * TT)
            rstd("mid", 1, EPS1)
            for t in range(TT):
                v.scalar_tensor_tensor(out=x[:, t, :], in0=x[:, t, :], scalar=RS[:, t:t + 1], in1=mod[:, 0:D],
                                       op0=ALU.mult, op1=ALU.mult)
            v.drain()
            mean_squares([(h[:, t, :], scr[:, 2048 + t * D:2048 + (t + 1) * D]) for t in range(TT)], [D] * TT)
            rstd("mid", 2, EPS2)
            for t in range(TT):
                m = v.tensor_scalar(h[:, t, :], h[:, t, :], RS[:, t:t + 1], None, ALU.mult)
            m.then_inc(S("memn"), 1)
            k = at(mid, 0)
            for i in (0, 2):
                take(k, "mT", i, memnT[:, 2 * i:2 * i + 2, :])
            for i in (1, 3):
                v.wait_ge(*k.emptied("mT", i))
            v.wait_ge(S("const2_in"), 48)
            v.memset(cPad[:, :], 0.0)
            v.memset(hidrep.rearrange("p k g n -> p (k g n)"), 0.0)
            v.drain().then_inc(S("mid_done"), 1)

            with v.Fori(0, DEPTH) as l:
                k = at(second, l)

                def ahead(name, first_, n=1):
                    for i in range(first_, first_ + n):
                        if second.tiles[name, i] + 2 < len(second.tiles):
                            lower_of(*weights(l, second.tiles[name, i] + 2))

                def lower_of(e, r):
                    v.wait_ge(*e.upper(r))
                    lower_part(v, r, slice(0, PART // 2))

                for n in range(2):
                    lower_of(*weights(l, n))

                def pre_norm(value, n):
                    mean_squares([(x[:, t, :], h[:, t, :]) for t in range(TT)], [D] * TT)
                    rstd("two", value, EPS2)
                    for t in range(TT):
                        m = v.tensor_scalar(h[:, t, :], x[:, t, :], RS[:, t:t + 1], None, ALU.mult)
                    m.then_inc(S("pre2"), 1)

                def gains(name, g0):
                    for i in range(4):
                        v.wait_ge(*k.filled(name, i))
                        v.sem_inc(S("held"), 1)
                        for c in (2 * i, 2 * i + 1):
                            v.tensor_scalar(hT2[0][:, c, :], k.bank(name, i)[:, (c % 2) * T:(c % 2 + 1) * T],
                                            colp[:, g0 + c:g0 + c + 1], None, ALU.mult)
                        v.drain()
                        for c in (2 * i, 2 * i + 1):
                            m = v.scalar_tensor_tensor(out=hT2[1][:, c, :],
                                                       in0=k.bank(name, i)[:, (c % 2) * T:(c % 2 + 1) * T],
                                                       scalar=colp[:, g0 + c:g0 + c + 1],
                                                       in1=hT2[0][:, c, :].bitcast(F32), op0=ALU.mult,
                                                       op1=ALU.subtract)
                        m.then_inc(k.empty_sem(name, i), 1)

                def parts(name):
                    for i in range(4):
                        c = slice(2 * i, 2 * i + 2)
                        b = k.bank(name, i).rearrange("p (c t) -> p c t", c=2)
                        v.wait_ge(*k.filled(name, i))
                        v.tensor_scalar(hT2[0][:, c, :], b, 1.0, None, ALU.mult)
                        v.drain()
                        v.tensor_tensor(hT2[1][:, c, :], b, hT2[0][:, c, :].bitcast(F32), ALU.subtract)\
                            .then_inc(k.empty_sem(name, i), 1)

                def post_norm(name, value, g0, factor):
                    for i in range(4):
                        v.wait_ge(*k.emptied(name, i))
                    mean_squares([(h[:, t, :], scr[:, 2048 + t * D:2048 + (t + 1) * D]) for t in range(TT)], [D] * TT)
                    rstd("two", value, EPS2)
                    for t in range(TT):
                        v.scalar_tensor_tensor(out=h[:, t, :], in0=h[:, t, :], scalar=RS[:, t:t + 1],
                                               in1=mod[:, g0:g0 + D], op0=ALU.mult, op1=ALU.mult)
                    v.drain()
                    for t in range(TT):
                        v.scalar_tensor_tensor(out=x[:, t, :], in0=h[:, t, :], scalar=factor, in1=x[:, t, :],
                                               op0=ALU.mult, op1=ALU.add)
                    v.drain()

                def ffn(name, n, r):
                    pre_norm(l * 10 + r, n)
                    gains(name + "T", K2[name])
                    for i in range(0, FC, 2):
                        ahead(name + "gu", i, 2)
                        v.wait_ge(*k.emptied(name + "gu", i))
                        v.wait_ge(*k.filled(name + "gu", i + 1))
                        gate_, up_ = sgate[:, i // 2 % 2, :], k.bank(name + "gu", i + 1)
                        v.tensor_tensor(hid2[0][:, i:i + 2, :].rearrange("p c t -> p (c t)"), up_, gate_, ALU.mult)
                        v.tensor_tensor(gate_, up_, gate_, ALU.mult)
                        v.drain()
                        v.tensor_tensor(hid2[1][:, i:i + 2, :].rearrange("p c t -> p (c t)"), gate_,
                                        hid2[0][:, i:i + 2, :].bitcast(F32).rearrange("p c t -> p (c t)"),
                                        ALU.subtract).then_inc(k.empty_sem(name + "gu", i + 1), 1)
                    ahead(name + "d", 0, 12)
                    post_norm(name + "d", l * 10 + (r + 1), R2[name], 0.5)

                v.wait_ge(S("par2_in"), l * 32 + 32)
                ffn("f1", 0, 1)
                pre_norm(l * 10 + 3, 1)
                gains("nT", K2["mix"])
                ahead("nin", 0, 2)
                for s in range(2):
                    i = 2 + s
                    ahead("nin", i)
                    v.wait_ge(*k.filled("nin", i))
                    b = k.bank("nin", i).rearrange("p (g t) -> p g t", g=2)
                    v.tensor_copy(Z[0:HD, 2 * s:2 * s + 2, :], b[0:HD])
                    v.tensor_copy(Z[HD:P, 2 * s:2 * s + 2, 0:T - 1], b[HD:P, :, 1:T]).then_inc(k.empty_sem("nin", i), 1)
                v.drain()
                for i in range(4, 12):
                    ahead("nin", i)
                    four = [divmod(4 * (i - 4) + j, JP) for j in range(4)]

                    def position(s, j):
                        return (Z[:, 2 * s:2 * s + 2, 2 * j:2 * j + 16 * (NCMP - 1) + 1:16],
                                colp[:, K2["pe"] + s * JP + j:][:, 0:1],
                                [z[:, s, j, :].rearrange("p (g n) -> p g n", g=2) for z in Zp2])

                    for s, j in four:
                        zj, pe_, (z_up, _) = position(s, j)
                        v.tensor_scalar(z_up, zj, pe_, None, ALU.add)
                    v.drain()
                    for s, j in four:
                        zj, pe_, (z_up, z_lo) = position(s, j)
                        m = v.scalar_tensor_tensor(out=z_lo, in0=zj, scalar=pe_, in1=z_up.bitcast(F32), op0=ALU.add,
                                                   op1=ALU.subtract)
                m.then_inc(S("zp"), 1)
                for t in range(TT):
                    take(k, "nin", 10 + t, vr[:, t, :])
                ahead("nin", 12, 4)
                ahead("cw1", 0, 4)
                v.wait_ge(*k.filled("hidT"))
                v.tensor_copy(hidcT[:, 0:60], k.bank("hidT")[:, 0:60])
                for c in range(2):
                    for g_ in range(2):
                        src = k.bank("hidT")[:, 60 + c * 30 + g_ * NCMP:][:, 0:NCMP]
                        m = v.tensor_copy(hidrep[:, c, g_, :].rearrange("p (r n) -> p r n", r=4)[:, :, 0:NCMP],
                                          row(src, 4))
                m.then_inc(k.empty_sem("hidT"), 1)
                v.wait_ge(*k.filled("kc"))
                v.tensor_copy(kcT[:, 0:30], k.bank("kc")[:, 0:30])
                for g_ in range(2):
                    for r_ in range(4):
                        m = v.tensor_scalar(vcbd[:, g_, r_, :], k.bank("kc")[:, P + g_ * HD:P + (g_ + 1) * HD],
                                            mod[:, R2["end"] + 480 + r_:][:, 0:1], None, ALU.mult)
                m.then_inc(k.empty_sem("kc"), 1)
                cb3 = mod[:, R2["end"]:R2["end"] + 240]
                cm3 = mod[:, R2["end"] + 240:R2["end"] + 480]
                c3 = cS.rearrange("p (r n) -> p r n", n=NCMP)
                v.wait_ge(*k.filled("cS"))
                v.tensor_tensor(cS, k.bank("cS")[:, 0:240], cb3, ALU.add).then_inc(k.empty_sem("cS"), 1)
                v.drain()
                v.tensor_reduce(stat(120, 16), c3, AX.X, ALU.max)
                v.drain()
                v.tensor_tensor(c3, c3, column(stat(120, 16), NCMP), ALU.subtract).then_inc(S("cmax"), 1)
                v.wait_ge(S("cexp"), l + 1)
                v.tensor_tensor(cS, cS, cm3, ALU.mult)
                v.drain()
                v.tensor_reduce(stat(136, 16), c3, AX.X, ALU.add)
                v.drain()
                v.tensor_scalar(stat(136, 16), stat(136, 16), 1e-30, None, ALU.max)
                v.drain()
                v.reciprocal(stat(136, 16), stat(136, 16))
                v.drain()
                v.tensor_tensor(cPad.rearrange("p (r n) -> p r n", n=32)[:, :, 0:NCMP], c3,
                                column(stat(136, 16), NCMP), ALU.mult).then_inc(S("cprob"), 1)

                def maxima(name, top, signal):
                    for i in range(NSA_H):
                        masked_max(k, name, i, alibi[:, i, :], sA, NSA_H, top)
                    v.drain()
                    v.tensor_scalar(stat(top + 16, 16), stat(top, 16), -1.0, None, ALU.mult).then_inc(S(signal), 1)

                maxima("wS", 24, "wmax")
                v.wait_ge(*k.filled("cPT"))
                v.tensor_copy(cPT[:, :], k.bank("cPT")).then_inc(k.empty_sem("cPT"), 1)
                sig = stat(152, 48).rearrange("p (a e) -> p a e", e=3)
                fac = stat(200, 48).rearrange("p (b a) -> p b a", b=3)
                v.tensor_copy(fac[:, 0, :], sig[:, :, 0])

                def combine(name, br):
                    for t in range(TT):
                        v.wait_ge(*k.filled(name, t))
                        src = k.bank(name, t).rearrange("p (h d) -> p h d", d=HD)
                        fa = column(fac[:, br, t * NSA_H:(t + 1) * NSA_H], HD)
                        if br == 0:
                            dst = onsa[:, t, :].rearrange("p (h d) -> p h d", d=HD)
                            v.tensor_tensor(dst, src, fa, ALU.mult).then_inc(k.empty_sem(name, t), 1)
                        else:
                            v.tensor_tensor(tmpB[:, t, :].rearrange("p (h d) -> p h d", d=HD), src, fa, ALU.mult)\
                                .then_inc(k.empty_sem(name, t), 1)
                            v.drain()
                            v.tensor_tensor(onsa[:, t, :], onsa[:, t, :], tmpB[:, t, :], ALU.add)
                    v.drain()

                v.drain()
                v.wait_ge(*k.filled("cO", 1))
                combine("cO", 0)
                v.wait_ge(S("wexp"), l + 1)
                v.reciprocal(stat(56, 16), stat(56, 16))
                v.drain()
                v.tensor_tensor(fac[:, 2, :], sig[:, :, 2], stat(56, 16), ALU.mult)
                v.drain()
                v.wait_ge(*k.filled("wPT", NSA_H - 1))
                combine("wO", 2)
                maxima("lS", 72, "lmax")
                for i in range(RH):
                    v.wait_ge(*k.filled("rS", i))
                    v.tensor_tensor(rS[:, i, :], k.bank("rS", i)[:, 0:384], retm[:, i, :], ALU.mult)\
                        .then_inc(k.empty_sem("rS", i), 1)
                v.wait_ge(S("lexp"), l + 1)
                v.reciprocal(stat(104, 16), stat(104, 16))
                v.drain()
                v.tensor_tensor(fac[:, 1, :], sig[:, :, 1], stat(104, 16), ALU.mult)
                v.drain()
                combine("lO", 1)
                mean_squares([(onsa[:, t, :], tmpB[:, t, :]) for t in range(TT)], [512] * TT)
                rstd("two", l * 10 + 4, EPS2)
                for t in range(TT):
                    v.scalar_tensor_tensor(out=h[:, t, 0:512], in0=onsa[:, t, :], scalar=RS[:, t:t + 1],
                                           in1=mod[:, R2["nsa"]:R2["nsa"] + 512], op0=ALU.mult, op1=ALU.mult)
                for t in range(TT):
                    v.wait_ge(*k.filled("rO", t))
                    v.tensor_copy(h[:, t, 512:D], k.bank("rO", t)).then_inc(k.empty_sem("rO", t), 1)
                ro = [h[:, t, 512:D].rearrange("p (h d) -> p h d", d=P) for t in range(TT)]
                v.drain()
                for t in range(TT):
                    v.tensor_reduce(stat(248 + 4 * t, 4), ro[t], AX.X, ALU.add)
                v.drain()
                v.tensor_scalar(stat(248, 8), stat(248, 8), 1.0 / P, None, ALU.mult)
                v.drain()
                for t in range(TT):
                    v.tensor_tensor(ro[t], ro[t], column(stat(248 + 4 * t, 4), P), ALU.subtract)
                v.drain()
                for t in range(TT):
                    v.tensor_tensor(tmpB[:, t, :], h[:, t, 512:D], h[:, t, 512:D], ALU.mult)
                v.drain()
                for t in range(TT):
                    v.tensor_reduce(stat(256 + 4 * t, 4), tmpB[:, t, :].rearrange("p (h d) -> p h d", d=P), AX.X,
                                    ALU.add)
                v.drain()
                v.tensor_scalar(SS, stat(256, 8), 1.0 / P, None, ALU.mult)
                rstd("two", l * 10 + 5, EPS2)
                for t in range(TT):
                    v.tensor_tensor(ro[t], ro[t], column(RS[:, 4 * t:4 * t + 4], P), ALU.mult)
                v.drain()
                for t in range(TT):
                    v.tensor_tensor(h[:, t, 512:D], h[:, t, 512:D], mod[:, R2["ret"]:R2["ret"] + 512], ALU.mult)
                v.drain()
                for t in range(TT):
                    v.wait_ge(*k.emptied("nin", 12 + t))
                    m = v.tensor_tensor(h[:, t, 512:D], h[:, t, 512:D], gr[:, t, :], ALU.mult)
                m.then_inc(S("ocat"), 1)
                parts("oT")
                ahead("nout", 0, 4)
                post_norm("nout", l * 10 + 6, R2["mix"], 1.0)
                pre_norm(l * 10 + 7, 2)
                for c in range(KC):
                    v.tensor_scalar(memT2[0][:, c, :], memnT[:, c, :], colp[:, K2["mem"] + c:K2["mem"] + c + 1], None,
                                    ALU.mult)
                v.drain()
                for c in range(KC):
                    m = v.scalar_tensor_tensor(out=memT2[1][:, c, :], in0=memnT[:, c, :],
                                               scalar=colp[:, K2["mem"] + c:K2["mem"] + c + 1],
                                               in1=memT2[0][:, c, :].bitcast(F32), op0=ALU.mult, op1=ALU.subtract)
                m.then_inc(S("memT"), 1)
                gains("xT", K2["xa"])
                for name in ("xk", "xv", "xq"):
                    ahead(name, 0, 4)
                for i in range(XH):
                    v.wait_ge(*k.filled("xS", i))
                    v.tensor_reduce(stat(264 + 2 * i, 2), k.bank("xS", i).rearrange("p (t n) -> p t n", t=TT), AX.X,
                                    ALU.max)
                    v.drain()
                    v.tensor_scalar(stat(272 + 2 * i, 2), stat(264 + 2 * i, 2), -1.0, None, ALU.mult)\
                        .then_inc(S("xmax"), 1)
                for i in range(XH):
                    v.wait_ge(*k.emptied("xS", i))
                    v.reciprocal(stat(288 + 2 * i, 2), stat(280 + 2 * i, 2))
                    v.drain()
                    for t in range(TT):
                        p_ = Px[:, i, t * T:(t + 1) * T]
                        m = v.tensor_scalar(p_, p_, stat(288 + 2 * i + t, 1), None, ALU.mult)
                    m.then_inc(S("xprob"), 1)
                parts("xO")
                ahead("xo", 0, 4)
                post_norm("xo", l * 10 + 8, R2["xa"], 1.0)
                ffn("f2", 3, 9)
                v.drain().then_inc(S("second_done"), 1)


def constants_first():
    i = np.arange(P)
    s, t = i[:, None], i[None, :]
    c = np.zeros((P, C_END), np.float32)
    c[:, C_ID:C_STRICT] = s == t
    c[:, C_STRICT:C_KEEP] = s > t
    c[:, C_KEEP:C_CAUS] = np.concatenate([s <= t, s < P + t, s <= t], 1)
    ok = s >= t
    c[:, C_CAUS:C_CAUS + 384] = np.where(np.concatenate([ok, s >= t - P, ok], 1), 0.0, NEG)
    c[:, C_BAND:C_BAND + 384] = np.where(np.concatenate([ok, t > s, ok], 1), 0.0, NEG)
    c[:, C_IOTA:C_END] = t
    return c


def constants_second():
    i = np.arange(P)
    q, key = i[:, None], i[None, :]
    c = np.zeros((P, C2["end"]), np.float32)
    slopes = (2.0 ** (-8.0 * np.arange(1, NSA_H + 1) / NSA_H)).astype(np.float32)
    dist = np.concatenate([q - key, P + q - key, q - key], 1)
    for j in range(NSA_H):
        c[:, 384 * j:384 * (j + 1)] = np.where(dist >= 0, -slopes[j] * dist.astype(np.float32), NEG)
    start = np.arange(NCMP) * 16
    for t in range(TT):
        tok = t * P + i[:, None]
        ok = start[None, :] + 31 <= tok
        away = (tok - (start[None, :] + 15.5)).astype(np.float32)
        for j in range(NSA_H):
            o = (t * NSA_H + j) * NCMP
            c[:, C2["cbias"] + o:C2["cbias"] + o + NCMP] = np.where(ok, -slopes[j] * away, NEG)
            c[:, C2["cmask"] + o:C2["cmask"] + o + NCMP] = ok
    c[:, C2["bmask"]:C2["ret"]] = i[:, None] // 32 == np.arange(4)[None, :]
    log_g = np.log(1.0 - np.exp2(-5.0 - np.arange(RH, dtype=np.float64)))
    away = np.concatenate([key - q, P + key - q, key - q], 1).astype(np.float64)
    for j in range(RH):
        c[:, C2["ret"] + 384 * j:C2["ret"] + 384 * (j + 1)] = np.where(
            away >= 0, np.exp(np.maximum(away, 0) * log_g[j]), 0.0) * float(P) ** -0.5
    return c


def weight_tiles(w, rows=D):
    kk, n = w.shape
    kg, nb = -(-kk // D), -(-n // NBLK)
    full = np.zeros((kg * D, nb * NBLK), w.dtype)
    full[:kk, :n] = w
    return full.reshape(kg, KC, P, nb, NBLK).transpose(3, 0, 2, 1, 4).reshape(nb * kg, P, TILE)


def f_tiles(w):
    return w.reshape(KC, P, -1, 256).transpose(2, 1, 0, 3).reshape(-1, P, PART)


def t_tiles(w):
    kk, n = w.shape
    kg, nb = -(-kk // (4 * P)), -(-n // NBLK)
    full = np.zeros((kg * 4 * P, nb * NBLK), w.dtype)
    full[:kk, :n] = w
    return full.reshape(kg, 4, P, nb, NBLK).transpose(3, 0, 2, 1, 4).reshape(nb * kg, P, PART)


def twice(w, n):
    return np.concatenate([w[:, HD * (j // 2):HD * (j // 2 + 1)] for j in range(2 * n)], 1)


def kernel(**inputs):
    import concourse.bacc as _bacc
    from concourse.bass_utils import run_bass_kernel_spmd as _run

    p = {n: np.asarray(v) for n, v in inputs.items()}
    cat = np.concatenate
    experts, stream1, stream2, row1, col1, row2, col2 = [], [], [], [], [], [], []
    for l in range(DEPTH):
        w = p["w_in"][l]
        z, xbc, dt, mq, mk, mv, sq, sk, sv = np.split(w, np.cumsum([512, 1024, 8, 256, 256, 256, 256, 128]), 1)
        w = cat([z, xbc, mq, mk, sq, twice(sk, 2), mv, sv, dt], 1)
        stream1.append(cat([weight_tiles(p["ada_w"][l]), weight_tiles(w), weight_tiles(p["w_out"][l]),
                            weight_tiles(p["peer_wq"][l])]))
        peer = np.empty((2 * TURNS, 2, 2, P, PART), np.float32)
        u = p["peer_u"][l].reshape(NKEYS, 2 * TURNS, 2, 2, KC, P)
        peer[:, 0] = u.transpose(1, 2, 5, 4, 3, 0).reshape(2 * TURNS, 2, P, PART)
        v = p["peer_v"][l].reshape(NKEYS, 2 * TURNS, 2, 2 * D)
        peer[:, 1] = v.transpose(1, 2, 0, 3)
        experts.append(peer.reshape(8 * TURNS, P, PART))
        row1.append(cat([p[n][l] for n in ("norm1_g", "norm2_g", "ssd_norm_g", "moba_norm_g", "swa_norm_g",
                                           "dt_bias", "a_log", "d_skip", "swa_sinks")]))
        cw = p["conv_w"][l].reshape(4, 8, P).transpose(2, 1, 0).reshape(P, 32)
        cb = p["conv_b"][l].reshape(8, P).T
        col1.append(cat([cw, cb, p["peer_k1"][l].T, p["peer_k2"][l].T], 1))

        gu = [np.stack([f_tiles(p[f"ffn{f}_w_{s}_2"][l]) for s in ("gate", "up")], 1).reshape(FC, P, PART)
              for f in (1, 2)]
        w = p["w_in_2"][l]
        q, kc, vc, ks, vs, kw, vw, ga, qr, kr, vr, gr = np.split(w, np.cumsum([512] + [128] * 6 + [24] + [512] * 3), 1)
        w_f = cat([q, twice(kc, 2), twice(vc, 2), twice(ks, 2), twice(kw, 2), qr, kr], 1)
        w_t = cat([vr, gr, vs, vw, ga], 1)
        cw1 = p["cmp_w1_2"][l].reshape(4, JP // 2, P, 256).transpose(0, 2, 1, 3).reshape(4, P, PART)
        stream2.append(cat([gu[0], t_tiles(p["ffn1_w_down_2"][l]), f_tiles(w_f), t_tiles(w_t), cw1,
                            t_tiles(p["w_out_2"][l]), f_tiles(p["xa_wk_2"][l]), t_tiles(p["xa_wv_2"][l]),
                            f_tiles(p["xa_wq_2"][l]), t_tiles(p["xa_wo_2"][l]), gu[1],
                            t_tiles(p["ffn2_w_down_2"][l])]))
        row2.append(cat([p[n + "_2"][l] for n in ("ffn1_post_g", "mix_post_g", "xa_post_g", "ffn2_post_g",
                                                  "nsa_out_g", "ret_gn_g")]))
        cols = [p[n + "_2"][l].reshape(KC, P).T for n in ("ffn1_pre_g", "mix_pre_g", "xa_pre_g", "xa_mem_g",
                                                          "ffn2_pre_g")]
        pe = p["cmp_pe_2"][l].reshape(2, JP, P).transpose(2, 0, 1).reshape(P, 32)
        w2 = p["cmp_w2_2"][l].reshape(2, 2, P, HD).transpose(2, 0, 1, 3).reshape(P, 256)
        col2.append(cat(cols + [pe, w2], 1))
    arrays = {
        "x": p["x"], "c": p["c"].reshape(KC, P).T, "mem": p["mem_2"], "final_g": p["final_g"], "ada_b": p["ada_b"],
        "experts": np.stack(experts), "stream1": np.stack(stream1), "stream2": np.stack(stream2), "row1": np.stack(row1), "col1": np.stack(col1),
        "row2": np.stack(row2), "col2": np.stack(col2), "const1": constants_first(), "const2": constants_second(),
    }
    arrays = {n: np.ascontiguousarray(v) for n, v in arrays.items()}
    nc = _bacc.Bacc("TRN2", target_bir_lowering=False, num_devices=1, dynamic_dma_scratch_size=1024)
    aps = {n: nc.dram_tensor("in_" + n, v.shape, F32, kind="ExternalInput").ap() for n, v in arrays.items()}
    out = nc.dram_tensor("out", (1, T, D), F32, kind="ExternalOutput").ap()
    two_mixers_and_peer_then_nsa_retention_memory(nc, aps, out)
    r = _run(nc, [{"in_" + n: v for n, v in arrays.items()}], core_ids=[0])
    return r.results[0]["out"]
```
